# Optimizing a Trainium2 kernel written in Bass

```python
import math
import jax, jax.numpy as jnp
from jax import lax
import numpy as np

D_MODEL = 1024
BATCH = 1
SEQ = 128
DEPTH = 1
DEC_BATCH = 1
DEC_SEQ = 2048
PAST_LEN = 128

GRID_W = 64
D_MIX = D_MODEL
D_ATT = D_MIX // 2
D_CONV = D_MIX - D_ATT
HEAD_DIM = 64
V_DIM = 2 * HEAD_DIM
N_ATT_HEADS = D_ATT // V_DIM
CONV_W = 3
ROPE_FREQS = HEAD_DIM // 4
ROPE_BASE = 10000.0
Q_BLOCK = 128
EPS = 1e-6
SPLITS = (D_ATT, D_ATT, D_ATT, D_ATT, D_CONV, D_CONV, D_CONV, D_CONV)
D_IN = sum(SPLITS)

kernel_name = "hymba_diffattn_shortconv_dit_step"

def _rms(x, w):
    xf = x.astype(jnp.float32)
    y = xf * lax.rsqrt(jnp.mean(xf * xf, axis=-1, keepdims=True) + EPS)
    return (y * w.astype(jnp.float32)).astype(x.dtype)

def _modulation(cvec, w_ada, b_ada):
    m = jax.nn.silu(cvec) @ w_ada + b_ada
    return jnp.split(m, 3, axis=-1)

def _lambda_init(layer):
    return 0.8 - 0.6 * math.exp(-0.3 * layer)

def _axial_rope_tables(n):
    rows = n // GRID_W
    t = jnp.arange(rows * GRID_W)
    row = (t // GRID_W).astype(jnp.float32)
    col = (t % GRID_W).astype(jnp.float32)
    inv = 1.0 / (ROPE_BASE ** (jnp.arange(ROPE_FREQS, dtype=jnp.float32) / ROPE_FREQS))
    ang_r = row[:, None] * inv
    ang_c = col[:, None] * inv
    shp = (1, n, 1, 1, ROPE_FREQS)
    return (jnp.cos(ang_r).reshape(shp), jnp.sin(ang_r).reshape(shp),
            jnp.cos(ang_c).reshape(shp), jnp.sin(ang_c).reshape(shp))

def _rope_half(x, cos, sin):
    x1, x2 = jnp.split(x, 2, axis=-1)
    cos = cos.astype(x.dtype)
    sin = sin.astype(x.dtype)
    return jnp.concatenate([x1 * cos - x2 * sin, x2 * cos + x1 * sin], axis=-1)

def _apply_axial_rope(x, tables):
    cos_r, sin_r, cos_c, sin_c = tables
    xr, xc = jnp.split(x, 2, axis=-1)
    return jnp.concatenate([_rope_half(xr, cos_r, sin_r), _rope_half(xc, cos_c, sin_c)], axis=-1)

def _diff_attention(q, k, v, lam):
    b, nq = q.shape[0], q.shape[1]
    nblk = nq // Q_BLOCK
    qb = q.reshape(b, nblk, Q_BLOCK, N_ATT_HEADS, 2, HEAD_DIM).swapaxes(0, 1)
    scale = HEAD_DIM ** -0.5

    def one(qblk):
        s = jnp.einsum('bqhmd,bkhmd->bhmqk', qblk, k).astype(jnp.float32) * scale
        p = jax.nn.softmax(s, axis=-1)
        a = p[:, :, 0] - lam * p[:, :, 1]
        return jnp.einsum('bhqk,bkhe->bqhe', a.astype(v.dtype), v)

    out = lax.map(one, qb)
    return out.swapaxes(0, 1).reshape(b, nq, N_ATT_HEADS, V_DIM)

def _short_conv(u, w, b):
    up = jnp.pad(u, ((0, 0), (1, 1), (0, 0)))
    return up[:, :-2] * w[0] + up[:, 1:-1] * w[1] + up[:, 2:] * w[2] + b

def _project(x, shift, scale, norm_w, w_in, q_norm_w, k_norm_w):
    b, n = x.shape[0], x.shape[1]
    h = _rms(x, norm_w) * (1 + scale) + shift
    z = h @ w_in
    idx = list(np.cumsum(SPLITS)[:-1])
    q, k, v, g_att, cb, cc, ch, g_conv = jnp.split(z, idx, axis=-1)
    q = _rms(q.reshape(b, n, N_ATT_HEADS, 2, HEAD_DIM), q_norm_w)
    k = _rms(k.reshape(b, n, N_ATT_HEADS, 2, HEAD_DIM), k_norm_w)
    v = v.reshape(b, n, N_ATT_HEADS, V_DIM)
    return q, k, v, g_att, cb, cc, ch, g_conv

def _finish(x, att, g_att, cb, cc, ch, g_conv, gate, subln_w, conv_w, conv_b, w_out, lam_init):
    b, n = x.shape[0], x.shape[1]
    att = _rms(att, subln_w) * (1.0 - lam_init)
    att = att.reshape(b, n, D_ATT) * jax.nn.silu(g_att)
    conv = cb * _short_conv(cc * ch, conv_w, conv_b) * jax.nn.silu(g_conv)
    y = jnp.concatenate([att, conv], axis=-1) @ w_out
    return x + gate * y

def setup_inputs(seed: int = 0) -> dict:
    key = jax.random.key(seed)
    ks = jax.random.split(key, 20)
    f = jnp.float32
    nrm = lambda k, s, sc: jax.random.normal(k, s, f) * sc
    return {
        "x_prompt": nrm(ks[0], (BATCH, SEQ, D_MODEL), 1.0),
        "x_sample": nrm(ks[1], (DEC_BATCH, DEC_SEQ, D_MODEL), 1.0),
        "cache_k": nrm(ks[2], (DEC_BATCH, DEPTH, PAST_LEN, N_ATT_HEADS, 2, HEAD_DIM), 1.0),
        "cache_v": nrm(ks[3], (DEC_BATCH, DEPTH, PAST_LEN, N_ATT_HEADS, V_DIM), 1.0),
        "c": nrm(ks[4], (DEC_BATCH, D_MODEL), 1.0),
        "c_ctx": nrm(ks[5], (D_MODEL,), 1.0),
        "norm_w": 1.0 + nrm(ks[6], (DEPTH, D_MODEL), 0.02),
        "w_ada": nrm(ks[7], (DEPTH, D_MODEL, 3 * D_MODEL), 0.5 * D_MODEL ** -0.5),
        "b_ada": nrm(ks[8], (DEPTH, 3 * D_MODEL), 0.02),
        "w_in": nrm(ks[9], (DEPTH, D_MODEL, D_IN), D_MODEL ** -0.5),
        "q_norm_w": 1.0 + nrm(ks[10], (DEPTH, HEAD_DIM), 0.02),
        "k_norm_w": 1.0 + nrm(ks[11], (DEPTH, HEAD_DIM), 0.02),
        "lambda_q1": nrm(ks[12], (DEPTH, HEAD_DIM), 0.1),
        "lambda_k1": nrm(ks[13], (DEPTH, HEAD_DIM), 0.1),
        "lambda_q2": nrm(ks[14], (DEPTH, HEAD_DIM), 0.1),
        "lambda_k2": nrm(ks[15], (DEPTH, HEAD_DIM), 0.1),
        "subln_w": 1.0 + nrm(ks[16], (DEPTH, V_DIM), 0.02),
        "conv_w": nrm(ks[17], (DEPTH, CONV_W, D_CONV), CONV_W ** -0.5),
        "conv_b": nrm(ks[18], (DEPTH, D_CONV), 0.02),
        "w_out": nrm(ks[19], (DEPTH, D_MIX, D_MODEL), D_MIX ** -0.5),
    }

def reference(x_prompt, x_sample, cache_k, cache_v, c, c_ctx, norm_w, w_ada, b_ada, w_in,
              q_norm_w, k_norm_w, lambda_q1, lambda_k1, lambda_q2, lambda_k2, subln_w,
              conv_w, conv_b, w_out):
    rope = _axial_rope_tables(x_sample.shape[1])
    xp = x_prompt
    xs = x_sample
    new_k = []
    new_v = []
    for i in range(DEPTH):
        lam_init = _lambda_init(i)
        lam = (jnp.exp(jnp.sum(lambda_q1[i].astype(jnp.float32) * lambda_k1[i].astype(jnp.float32)))
               - jnp.exp(jnp.sum(lambda_q2[i].astype(jnp.float32) * lambda_k2[i].astype(jnp.float32)))
               + lam_init)
        sh_c, sc_c, ga_c = _modulation(c_ctx, w_ada[i], b_ada[i])
        q, k, v, g_att, cb, cc, ch, g_conv = _project(xp, sh_c, sc_c, norm_w[i], w_in[i],
                                                      q_norm_w[i], k_norm_w[i])
        new_k.append(k)
        new_v.append(v)
        att = _diff_attention(q, k, v, lam)
        xp = _finish(xp, att, g_att, cb, cc, ch, g_conv, ga_c, subln_w[i], conv_w[i], conv_b[i],
                     w_out[i], lam_init)
        sh, sc, ga = _modulation(c, w_ada[i], b_ada[i])
        q, k, v, g_att, cb, cc, ch, g_conv = _project(xs, sh[:, None], sc[:, None], norm_w[i],
                                                      w_in[i], q_norm_w[i], k_norm_w[i])
        q = _apply_axial_rope(q, rope)
        k = _apply_axial_rope(k, rope)
        k_all = jnp.concatenate([k, cache_k[:, i].astype(k.dtype)], axis=1)
        v_all = jnp.concatenate([v, cache_v[:, i].astype(v.dtype)], axis=1)
        att = _diff_attention(q, k_all, v_all, lam)
        xs = _finish(xs, att, g_att, cb, cc, ch, g_conv, ga[:, None], subln_w[i], conv_w[i],
                     conv_b[i], w_out[i], lam_init)
    new_cache_k = jnp.stack(new_k, axis=1)
    new_cache_v = jnp.stack(new_v, axis=1)
    return (xp, xs, new_cache_k, new_cache_v)


_drawn_inputs = setup_inputs


def setup_inputs(seed=0):
    import zlib

    import numpy as np

    out = dict(_drawn_inputs(seed))
    spreads = {}
    factors = {'cache_k': 8.0,
     'cache_v': 8.0,
     'norm_w': 2.843,
     'q_norm_w': 8.0,
     'k_norm_w': 2.739,
     'lambda_q1': 8.0,
     'lambda_k1': 4.597,
     'lambda_q2': 64.0,
     'lambda_k2': 8.0,
     'subln_w': 64.0,
     'conv_b': 26.682}
    for name, (base, spread) in spreads.items():
        noise = np.random.default_rng([zlib.crc32(name.encode()), seed]).standard_normal(out[name].shape)
        drawn = base * np.exp(spread * noise) if base else spread * noise
        out[name] = __import__('jax').numpy.asarray(drawn.astype(out[name].dtype))
    for name, factor in factors.items():
        out[name] = (out[name] * factor).astype(out[name].dtype)
    return out
```

```python
import math
from contextlib import ExitStack

import numpy as np
import concourse.bass as bass
from concourse import mybir

F32 = mybir.dt.float32
F32R = mybir.dt.float32r
ALU = mybir.AluOpType
ACT = mybir.ActivationFunctionType
AX = mybir.AxisListType

P = 128
D = 1024
DJ = D // P
SAMPLE, PROMPT, CACHE = 2048, 128, 128
T = SAMPLE + PROMPT
KEYS = SAMPLE + CACHE
KCOLS = KEYS + PROMPT
H = 4
HD = 64
N = 512
TG = T // N
GROUPS = [(g * N, N) for g in range(TG)] + [(SAMPLE, PROMPT)]
NG = len(GROUPS)
XG = 256
XGROUPS = [(g * XG, XG) for g in range(SAMPLE // XG)] + [(SAMPLE, PROMPT)]
KT = KEYS // P
TILES = T // P
EPS = 1e-6
LAM_INIT = 0.8 - 0.6 * math.exp(-0.3 * 0)
BANKS = 5
QK_UNITS = 2 * NG
CV = 5
CV_UNITS = CV * NG
QT = SAMPLE // P
ITS = H * QT // 4
TGROUPS = [(0, 4), (4, 4), (8, 4), (12, 4), (16, 1)]


def wait(eng, sem, value):
    if isinstance(value, int) and value <= 0:
        return
    eng.wait_ge(sem, value)


def hymba_layer(nc, a):
    spill = {}
    for name, shape in (("k", [H, 2, P, KCOLS]), ("q", [H, 2, P, T]), ("v", [H, P, KT + 1, 2, P]),
                        ("ga", [H, P, T]), ("cv", [H, 2, P, T]), ("att", [H, P, T])):
        spill[name] = nc.dram_tensor(f"spill_{name}", shape, F32, kind="Internal").ap()

    ctx = ExitStack()
    with ctx:
        def sb(name, shape, dt=F32, c=ctx):
            return c.enter_context(nc.sbuf_tensor(name, shape, dt))

        def sem(name):
            return ctx.enter_context(nc.semaphore(name))

        ps = ctx.enter_context(nc.psum_tensor("ps", [P, 8, N], F32))

        cst = sb("cst", [P, 3, P])
        ident, ones, blk = cst[:, 0], cst[:, 1], cst[:, 2]
        small = sb("small", [P, 67])
        norm_w, qk_w, subln = small[:, 0:8], small[:, 8:10], small[:, 10:11]
        taps, b_ada = small[:, 11:27], small[:, 27:51]
        c_in = small[:, 51:67]
        eps = sb("eps", [P, 1])
        sc = sb("sc", [P, DJ, 2])
        mod = sb("mod", [P, 24, 2])
        mult = sb("mult", [P, DJ, 2])
        lamv = sb("lamv", [P, 4, HD])
        lamj = sb("lamj", [P, 2, HD])
        lamt = sb("lamt", [P, 6])
        lamc = sb("lamc", [P, 2])
        sublns = sb("sublns", [P, 1])
        qks = sb("qks", [P, 2])
        tick = sb("tick", [P, 1])
        cw = sb("cw", [P, 4])

        with ExitStack() as actx:
            hT = sb("hT", [P, 2, DJ, T], F32R, actx)
            with ExitStack() as wctx:
                wad = sb("wad", [P, 2, 4, DJ, P], F32, wctx)
            w = sb("w", [P, 5, 2, DJ, P], F32R, actx)
            raw = sb("raw", [P, 2, DJ, P], F32, actx)
            scr = sb("scr", [P, 8000], F32, actx)
        with ExitStack() as bctx:
            kb = sb("kb", [P, 2, 2, KEYS], F32R, bctx)
            vb = sb("vb", [P, KT, 2, P], F32R, bctx)
            qb = sb("qb", [P, 4, 2, 2, P], F32R, bctx)
            e0 = sb("e0", [P, 4, KEYS], F32, bctx)
            e1 = sb("e1", [P, 2, KEYS], F32, bctx)
            at = sb("at", [P, 2, 2, KT, 2 * P], F32R, bctx)
            atto = sb("atto", [P, 2, 2 * P], F32, bctx)
            stt = sb("stt", [P, 2, 8, 6], F32, bctx)
            qp = sb("qp", [P, 2, 2 * H, P], F32R, bctx)
            kp = sb("kp", [P, 2 * H, P], F32R, bctx)
            vp = sb("vp", [P, H, 2, P], F32R, bctx)
            stp = sb("stp", [P, 4, 2 * H], F32, bctx)
        with ExitStack() as cctx:
            wo = sb("wo", [P, 2, DJ, DJ, P], F32R, cctx)
            worw = sb("worw", [P, 2, DJ, P], F32, cctx)
            mix = sb("mix", [P, 2, 2, DJ, N], F32R, cctx)
            atr = sb("atr", [P, H, N], F32, cctx)
            gar = sb("gar", [P, H, N], F32, cctx)
            xr = sb("xr", [P, 2, DJ, N], F32, cctx)
            yo = sb("yo", [P, 4, N], F32, cctx)
            csq = sb("csq", [P, N], F32, cctx)
            cstd = sb("cstd", [P, N], F32, cctx)
            crs = sb("crs", [P, N], F32, cctx)
            cy = sb("cy", [P, N], F32, cctx)

        xs = scr[:, 0:4096].rearrange("p (b j t) -> p b j t", b=2, j=DJ)
        xsq = scr[:, 4096:6144].rearrange("p (j t) -> p j t", j=DJ)
        xstd, xrstd = scr[:, 6144:6400], scr[:, 6400:6656]
        vraw = scr[:, 4352:4864]
        vhi, vlo = scr[:, 6656:7168], scr[:, 7168:7680]
        cosT, sinT = scr[:, 0:T], scr[:, T:2 * T]
        qsq, qrs, qzn, qt1, qt2, qhi, qlo = (scr[:, 2 * T + i * N:2 * T + (i + 1) * N] for i in range(7))
        sig = scr[:, 0:2 * N].rearrange("p (b n) -> p b n", b=2)
        gs, ccs, cc_, chi, clo = (scr[:, i * N:(i + 1) * N] for i in range(2, 7))
        ub = scr[:, 7 * N:7 * N + SAMPLE + 2]
        up = scr[:, 7 * N + SAMPLE + 2:7 * N + SAMPLE + 2 + PROMPT + 2]
        g0 = 7 * N + SAMPLE + PROMPT + 4
        gcb = scr[:, g0:g0 + T]

        def useq(tg):
            c0, n = GROUPS[tg]
            return (up, 0, n) if tg == TG else (ub, c0, n)

        s_const = sem("s_const")
        s_x = [sem(f"s_x{i}") for i in range(2)]
        s_wada = [sem(f"s_wada{i}") for i in range(2)]
        s_raw = [sem(f"s_raw{i}") for i in range(2)]
        s_craw = sem("s_craw")
        s_rope = sem("s_rope")
        stored = sem("stored")
        aux_stored = sem("aux_stored")
        lam_ch = sem("lam_ch")
        lam_e = sem("lam_e")
        sc_ready = sem("sc_ready")
        mod_mm = sem("mod_mm")
        mod_ch = sem("mod_ch")
        sq_ready = sem("sq_ready")
        sum_mm = sem("sum_mm")
        std_ready = sem("std_ready")
        rstd_ready = sem("rstd_ready")
        xn_ready = sem("xn_ready")
        h32_ready = sem("h32_ready")
        hhi_ready = sem("hhi_ready")
        hlo_ready = sem("hlo_ready")
        w_hi = sem("w_hi")
        w_lo = sem("w_lo")
        z_mm = sem("z_mm")
        z_used = sem("z_used")
        hi_ready = sem("hi_ready")
        lo_ready = sem("lo_ready")
        nv_ready = sem("nv_ready")
        sh_ready = sem("sh_ready")
        p_t1 = sem("p_t1")
        p_t2 = sem("p_t2")
        zr_ready = sem("zr_ready")
        sig_ready = sem("sig_ready")
        cvc = sem("cvc")
        tapped = sem("tapped")
        s_p = sem("s_p")
        s_k = sem("s_k")
        s_v = [sem(f"s_v{i}") for i in range(2)]
        s_q = [sem(f"s_q{i}") for i in range(4)]
        pr_mm = sem("pr_mm")
        pr_v = sem("pr_v")
        pr_a = sem("pr_a")
        s_pair = sem("s_pair")
        s_ctx = sem("s_ctx")
        mx_done = sem("mx_done")
        mxc_done = sem("mxc_done")
        gm_done = sem("gm_done")
        exp_done = sem("exp_done")
        expc_done = sem("expc_done")
        d_done = sem("d_done")
        f_done = sem("f_done")
        fz_done = sem("fz_done")
        den_done = sem("den_done")
        rden_done = sem("rden_done")
        rl_done = sem("rl_done")
        coef_done = sem("coef_done")
        e1_done = sem("e1_done")
        a_ready = sem("a_ready")
        t_mm = sem("t_mm")
        t_hi = sem("t_hi")
        t_lo = sem("t_lo")
        pv_mm = sem("pv_mm")
        att_evac = sem("att_evac")
        att_stored = [sem(f"att_stored{i}") for i in range(2)]
        c_raw = [sem(f"c_raw{i}") for i in range(2)]
        c_whi = sem("c_whi")
        c_wlo = sem("c_wlo")
        c_at = sem("c_at")
        c_mix = [sem(f"c_mix{i}") for i in range(2)]
        c_x = [sem(f"c_x{i}") for i in range(2)]
        c_sq = sem("c_sq")
        c_sum = sem("c_sum")
        c_std = sem("c_std")
        c_rs = sem("c_rs")
        c_y1 = sem("c_y1")
        c_y2 = sem("c_y2")
        c_hi = sem("c_hi")
        c_lo = sem("c_lo")
        o_mm = sem("o_mm")
        o_used = sem("o_used")
        o_st = [sem(f"o_st{i}") for i in range(4)]

        block = ctx.enter_context(nc.Block())

        V_UNITS = TILES
        QK0 = V_UNITS
        CV0 = V_UNITS + H * QK_UNITS
        ALL = CV0 + H * CV_UNITS
        XN = len(XGROUPS)
        CHUNKS = 32
        QKC, CVC = 4, 12
        CV_SLOT = [4, 1, 2, 3, 0]
        CV_RAW = [0, 1, 0, 1, 0]

        def f32(ap):
            return ap.bitcast(F32)

        def r32(ap):
            return ap.bitcast(F32R)

        @block.sync
        def _(sp):
            def load_w(c, buf):
                sp.dma_start(raw[:, buf], a["w_in"][c]).then_inc(s_raw[buf], 16)

            sp.dma_start(cst[:], a["cst"]).then_inc(s_const, 16)
            sp.dma_start(small[:], a["small"]).then_inc(s_const, 16)
            sp.dma_start(lamv[:], a["lam"]).then_inc(s_const, 16)
            for g in range(2):
                sp.dma_start(xs[:, g], a["xT"][:, :, g * XG:(g + 1) * XG]).then_inc(s_x[g], 16)
            sp.dma_start(vraw.rearrange("p (h t) -> p h t", h=H),
                         a["cache_k"].rearrange("h p t -> p h t")).then_inc(s_craw, 16)
            load_w(0, 0)
            load_w(1, 1)
            for hf in range(6):
                wait(sp, mod_mm, hf - 1)
                sp.dma_start(wad[:, hf % 2], a["w_ada"][4 * hf:4 * hf + 4].rearrange("n p j c -> p n j c"))\
                    .then_inc(s_wada[hf % 2], 16)
                if hf == 0:
                    sp.wait_ge(hi_ready, 1)
                    sp.wait_ge(lo_ready, 1)
                    for hl, src in ((0, vhi), (1, vlo)):
                        sp.dma_start(spill["k"][:, hl, :, SAMPLE:KEYS].rearrange("h p t -> p h t"),
                                     src.rearrange("p (h t) -> p h t", h=H)).then_inc(stored, 16)
                    sp.dma_start(vraw, a["cache_v"]).then_inc(s_craw, 16)
                if hf == 1:
                    sp.wait_ge(hi_ready, 2)
                    sp.wait_ge(lo_ready, 2)
                    for hl, src in ((0, vhi), (1, vlo)):
                        sp.dma_start(spill["v"][:, :, KT - 1, hl, :].rearrange("h p e -> p h e"),
                                     src.rearrange("p (h e) -> p h e", h=H)).then_inc(stored, 16)

            for c in range(2, 6):
                sp.wait_ge(w_lo, c - 1)
                load_w(c, c % 2)
            for g in range(XN + 1):
                if g + 2 < XN:
                    c0, n = XGROUPS[g + 2]
                    sp.wait_ge(hlo_ready, g + 1)
                    sp.dma_start(xs[:, g % 2, :, 0:n], a["xT"][:, :, c0:c0 + n]).then_inc(s_x[g % 2], 16)
                if g == 3:
                    sp.wait_ge(w_lo, 5)
                    load_w(6, 0)
                for t in range(max(0, 2 * g - 2), min(2 * g, TILES)):
                    sp.wait_ge(hi_ready, 2 + t + 1)
                    sp.wait_ge(z_used, t + 1)
                    for hl, src in ((0, vhi), (1, vlo)):
                        sp.dma_start(spill["v"][:, :, t if t < TILES - 1 else KT, hl, :].rearrange("h p e -> p h e"),
                                     src.rearrange("p (h e) -> p h e", h=H)).then_inc(stored, 16)
            sp.wait_ge(nv_ready, 1)
            sp.dma_start(a["new_v"], vraw).then_inc(aux_stored, 16)
            sp.wait_ge(hlo_ready, XN)
            sp.wait_ge(aux_stored, 16)
            sp.wait_ge(sum_mm, XN)
            sp.dma_start(scr[:, 0:2 * T], a["rope"]).then_inc(s_rope, 16)

            for h in range(H):
                for u in range(QK_UNITS):
                    c0, n = GROUPS[u % NG]
                    if u == 2:
                        sp.wait_ge(w_lo, 6 + 2 * h)
                        load_w(7 + 2 * h, 1)
                    if u == 7:
                        sp.wait_ge(w_lo, 7 + 2 * h)
                        load_w(8 + 2 * h, 0)
                    sp.wait_ge(hi_ready, 2 + V_UNITS + QK_UNITS * h + u + 1)
                    if u == NG - 1:
                        sp.dma_start(a["new_k"][h], qt1[:, 0:n])\
                            .then_inc(aux_stored, 16)
                    sp.wait_ge(lo_ready, 2 + QK_UNITS * h + u + 1)
                    dst = spill["k"] if u < NG else spill["q"]
                    col = c0 if u != NG - 1 else KEYS
                    for hl, src in ((0, qhi), (1, qlo)):
                        sp.dma_start(dst[h, hl, :, col:col + n], src[:, 0:n])\
                            .then_inc(stored, 16)

            for f in range(H):
                c = CVC + CV * f
                for tg in range(NG):
                    c0, n = GROUPS[tg]
                    if tg == 0:
                        sp.wait_ge(w_lo, c + 2)
                        load_w(c + 3, 1)
                        sp.wait_ge(w_lo, c + 3)
                        load_w(c + 4, 0)
                        if f + 1 < H:
                            sp.wait_ge(w_lo, c + 5)
                            load_w(c + 5, 0)
                            load_w(c + 6, 1)
                    sp.wait_ge(z_used, CV0 + CV_UNITS * f + CV * tg + 1)
                    sp.dma_start(spill["ga"][f, :, c0:c0 + n], gs[:, 0:n]).then_inc(aux_stored, 16)
                    for tc in ([] if tg == 0 else [tg - 1] if tg < TG else [TG - 1, TG]):
                        c0, n = GROUPS[tc]
                        sp.wait_ge(cvc, 4 + 6 * (NG * f + tc) + 6)
                        for hl, src in ((0, chi), (1, clo)):
                            sp.dma_start(spill["cv"][f, hl, :, c0:c0 + n], src[:, 0:n]).then_inc(stored, 16)
                if f + 1 < H:
                    sp.wait_ge(w_lo, c + 6)
                    load_w(c + 7, 0)

            sp.wait_ge(z_mm, ALL)
            sp.wait_ge(stored, 32 * (2 + V_UNITS + H * QK_UNITS + H * NG))
            sp.wait_ge(aux_stored, 16 * (1 + H + H * NG))

            def load_q(t, head, col):
                for ver in range(2):
                    for hl in range(2):
                        half = HD * (hl ^ ver)
                        sp.dma_start(f32(qb[half:half + HD, t, ver]),
                                     spill["q"][head, hl, :, col:col + P].rearrange("(m d) t -> d m t", m=2))\
                            .then_inc(s_q[t], 16)

            def load_k(head):
                for hl in range(2):
                    sp.dma_start(f32(kb[HD * hl:HD * hl + HD, head % 2]),
                                 spill["k"][head, hl, :, 0:KEYS].rearrange("(m d) t -> d m t", m=2)).then_inc(s_k, 16)

            def load_v(head, part):
                j0, j1 = (0, 9) if part == 0 else (9, KT)
                sp.dma_start(f32(vb[:, j0:j1]), spill["v"][head, :, j0:j1]).then_inc(s_v[part], 16)

            for head in range(H):
                for hl in range(2):
                    for ver in range(2):
                        half = HD * (hl ^ ver)
                        sp.dma_start(f32(qp[half:half + HD, ver, 2 * head:2 * head + 2]),
                                     spill["q"][head, hl, :, SAMPLE:T].rearrange("(m d) t -> d m t", m=2)).then_inc(s_p, 16)
                    sp.dma_start(f32(kp[HD * hl:HD * hl + HD, 2 * head:2 * head + 2]),
                                 spill["k"][head, hl, :, KEYS:KCOLS].rearrange("(m d) t -> d m t", m=2)).then_inc(s_p, 16)
            sp.dma_start(f32(vp[:]), spill["v"][:, :, KT].rearrange("h p l e -> p h l e")).then_inc(s_p, 16)
            for t in range(4):
                load_q(t, 0, t * P)
            load_k(0)
            load_v(0, 0)
            load_v(0, 1)
            for it in range(ITS):
                head = it // 4
                for t in range(4):
                    sp.wait_ge(s_ctx, 4 * it + t + 1)
                    if it % 4 == 0 and t == 0 and head + 1 < H:
                        load_k(head + 1)
                    if it % 4 == 0 and head > 0 and t >= 2:
                        sp.wait_ge(pv_mm, 4 * it + t - 3)
                        load_v(head, t - 2)
                    if it + 1 < ITS:
                        load_q(t, (it + 1) // 4, ((it + 1) % 4) * 4 * P + t * P)

            sp.wait_ge(pv_mm, 4 * ITS)
            sp.wait_ge(att_evac, 2 * ITS)
            for i in range(2):
                sp.wait_ge(att_stored[i], 16 * ITS)
            sp.wait_ge(pr_a, 3)
            sp.wait_ge(aux_stored, 16 * (1 + H + H * NG + 1))

            def loads(tg):
                c0, n = GROUPS[tg]
                par = tg % 2
                wait(sp, c_lo, 4 * tg)
                sp.dma_start(atr[:, :, 0:n], spill["att"][:, :, c0:c0 + n].rearrange("h p t -> p h t")).then_inc(c_at, 16)
                sp.dma_start(gar[:, :, 0:n], spill["ga"][:, :, c0:c0 + n].rearrange("h p t -> p h t")).then_inc(c_at, 16)
                wait(sp, o_mm, DJ * (tg - 1))
                for hl in range(2):
                    sp.dma_start(f32(mix[:, par, hl, H:DJ, 0:n]),
                                 spill["cv"][:, hl, :, c0:c0 + n].rearrange("f p t -> p f t")).then_inc(c_mix[par], 16)
                wait(sp, o_used, DJ * (tg - 1))
                sp.dma_start(xr[:, par, :, 0:n], a["xT"][:, :, c0:c0 + n]).then_inc(c_x[par], 16)

            def load_wo(n):
                wait(sp, c_wlo, n - 1)
                sp.dma_start(worw[:, n % 2], a["w_out"][n]).then_inc(c_raw[n % 2], 16)

            load_wo(0)
            load_wo(1)
            loads(0)
            for n in range(2, DJ):
                load_wo(n)
            for tg in range(NG):
                if tg + 1 < NG:
                    loads(tg + 1)
                c0, n = GROUPS[tg]
                for o in range(DJ):
                    sp.wait_ge(o_used, DJ * tg + o + 1)
                    sp.dma_start(a["y"][o, :, c0:c0 + n], yo[:, o % 4, 0:n]).then_inc(o_st[o % 4], 16)
            for i in range(4):
                sp.wait_ge(o_st[i], 16 * 2 * NG)

        @block.gpsimd
        def _(pool):
            pool.memset(eps[:], EPS).then_inc(zr_ready, 1)
            pool.memset(lamc[:, 0:1], 1.0).then_inc(p_t1, 1)
            pool.wait_ge(s_rope, 16)
            with pool.Fori(0, H) as h:
                for u in range(QK_UNITS):
                    c0, n = GROUPS[u % NG]
                    k = QK_UNITS * h + u
                    if u == NG:
                        pool.wait_ge(aux_stored, 16 * (h + 2))
                    pool.wait_ge(z_used, QK0 + k + 1)
                    pool.wait_ge(lo_ready, 2 + k)
                    pool.tensor_tensor(qt1[:, 0:n], qzn[:, 0:n], cosT[:, c0:c0 + n], ALU.mult).then_inc(p_t1, 1)
                    pool.wait_ge(sh_ready, k + 1)
                    pool.tensor_tensor(qt2[:, 0:n], qt2[:, 0:n], sinT[:, c0:c0 + n], ALU.mult).then_inc(p_t2, 1)
                    pool.wait_ge(p_t1, 1 + k + 1)
                    pool.wait_ge(p_t2, k + 1)
                    pool.tensor_tensor(qt1[:, 0:n], qt1[:, 0:n], qt2[:, 0:n], ALU.add).then_inc(zr_ready, 1)

            def bc(x):
                return x.rearrange("p (m o) -> p m o", o=1).to_broadcast([P, 2, 3])

            def three(x):
                return x.rearrange("p (m c) -> p m c", m=2)

            def factors(n, b):
                pool.wait_ge(f_done, n + 1)
                pool.tensor_tensor(stt[:, b, 4, :], stt[:, b, 3, :], stt[:, b, 1, :], ALU.mult).then_inc(fz_done, 1)
                pool.wait_ge(rden_done, n + 1)
                pool.tensor_tensor(stt[:, b, 6, 2:4], stt[:, b, 6, 0:2], lamc[:, :], ALU.mult).then_inc(rl_done, 1)
                pool.wait_ge(rl_done, n + 1)
                pool.tensor_tensor(three(stt[:, b, 7, :]), three(stt[:, b, 3, :]), bc(stt[:, b, 6, 2:4]), ALU.mult)\
                    .then_inc(coef_done, 1)

            def diffs(n, b):
                pool.wait_ge(gm_done, n + 1)
                pool.tensor_tensor(three(stt[:, b, 2, :]), bc(stt[:, b, 5, 2:4]), three(stt[:, b, 0, :]), ALU.subtract)\
                    .then_inc(d_done, 1)

            def step(it, t, scores=True, prev=True):
                n = 4 * it + t
                if prev:
                    factors(n - 1, (t - 1) % 2)
                if scores:
                    diffs(n, t % 2)

            for t in range(4):
                step(0, t, prev=t > 0)
            with pool.Fori(1, ITS) as it:
                for t in range(4):
                    step(it, t)
            step(ITS, 0, scores=False)

        @block.tensor
        def _(pe):
            def sums(k, n, lhsT, parts, bank):
                pe.wait_ge(sq_ready, k + 1)
                wait(pe, std_ready, k - 1)
                for j, part in enumerate(parts):
                    mm = pe.matmul(ps[:, bank, 0:n], lhsT, part, start=(j == 0), stop=(j == len(parts) - 1))
                mm.then_inc(sum_mm, 1)

            def passes(out, slot_of, rhs_of):
                todo = [(0, 0), (0, 1), (1, 0)]
                for i, (l, r) in enumerate((l, r) for _ in range(1) for l, r in todo):
                    for j in range(DJ):
                        mm = pe.matmul(out, slot_of(l, j), rhs_of(r, j),
                                       start=(i == 0 and j == 0), stop=(i == 2 and j == DJ - 1))
                mm.then_inc(z_mm, 1)

            pe.wait_ge(s_const, 48)
            sums(0, XG, ones, [xsq[:, j, :] for j in range(DJ)], 5)
            pe.wait_ge(sc_ready, 1)
            for hf in range(6):
                pe.wait_ge(s_wada[hf % 2], 16 * (hf // 2 + 1))
                for i in range(4):
                    for j in range(DJ):
                        mm = pe.matmul(ps[:, 7, 2 * (4 * hf + i):2 * (4 * hf + i) + 2], wad[:, hf % 2, i, j], sc[:, j],
                                       start=(j == 0), stop=(j == DJ - 1))
                mm.then_inc(mod_mm, 1)
            for g in range(XN):
                if g + 1 < XN:
                    n = XGROUPS[g + 1][1]
                    sums(g + 1, n, ones, [xsq[:, j, 0:n] for j in range(DJ)], 5 + (g + 1) % 2)
                pe.wait_ge(hlo_ready, g + 1)
                if g == 0:
                    pe.wait_ge(w_lo, 4)
                for t in range(2 * g, min(2 * g + 2, TILES)):
                    wait(pe, z_used, t - 4)
                    passes(ps[:, t % BANKS, :], lambda l, j: hT[:, l, j, t * P:(t + 1) * P],
                           lambda r, j: w[:, 0:4, r, j, :])

            with pe.Fori(0, H) as h:
                for u in range(QK_UNITS):
                    c0, n = GROUPS[u % NG]
                    k = QK_UNITS * h + u
                    if u % NG == 0:
                        pe.wait_ge(w_lo, QKC + 2 * h + u // NG + 1)
                    pe.wait_ge(z_used, QK0 + k - 4)
                    passes(ps[:, (QK0 + u) % BANKS, 0:n], lambda l, j: w[:, 4 if u < NG else 0, l, j, :],
                           lambda r, j: hT[:, r, j, c0:c0 + n])
                    if u > 0:
                        m = GROUPS[(u - 1) % NG][1]
                        sums(XN + k - 1, m, blk, [qsq[:, 0:m]], 5 + (XN + u - 1) % 2)
                m = GROUPS[NG - 1][1]
                sums(XN + QK_UNITS * h + QK_UNITS - 1, m, blk, [qsq[:, 0:m]], 5 + (XN + QK_UNITS - 1) % 2)

            with pe.Fori(0, H) as f:
                for tg in range(NG):
                    c0, n = GROUPS[tg]
                    for s in range(CV):
                        if tg == 0:
                            pe.wait_ge(w_lo, CVC + CV * f + s + 1)
                        pe.wait_ge(z_used, CV0 + CV_UNITS * f + CV * tg + s - 4)
                        passes(ps[:, (CV0 + s) % BANKS, 0:n], lambda l, j: w[:, CV_SLOT[s], l, j, :],
                               lambda r, j: hT[:, r, j, c0:c0 + n])

            pe.wait_ge(s_p, 16 * (6 * H + 1))
            for m in range(2 * H):
                for ver in range(2):
                    mm = pe.matmul(ps[:, m // 4, (m % 4) * P:(m % 4 + 1) * P], qp[:, ver, m], kp[:, m],
                                   start=(ver == 0), stop=(ver == 1))
            mm.then_inc(pr_mm, 1)
            pe.wait_ge(pr_v, 7)
            for h in range(H):
                mm = pe.transpose(ps[:, 5, h * P:(h + 1) * P], e0[:, 0, h * P:(h + 1) * P], ident)
            mm.then_inc(pr_mm, 1)
            pe.wait_ge(pr_v, 8)
            for h in range(H):
                for i, (l, r) in enumerate(((0, 0), (0, 1), (1, 0))):
                    mm = pe.matmul(ps[:, 7, h * P:(h + 1) * P], vp[:, h, l], at[:, 1, r, h, 0:P],
                                   start=(i == 0), stop=(i == 2))
            mm.then_inc(pr_mm, 1)
            pe.wait_ge(pr_a, 3)

            def transposes(n, t, g):
                j0, cnt = TGROUPS[g]
                k = 5 * n + g
                wait(pe, t_lo, k - 1)
                for i in range(cnt):
                    mm = pe.transpose(ps[:, 5 + (5 * t + g) % 2, i * P:(i + 1) * P],
                                      e0[:, t, (j0 + i) * P:(j0 + i + 1) * P], ident)
                mm.then_inc(t_mm, 1)

            def product(b, half, part):
                js = (range(0, 9), range(9, KT))[half]
                todo = [(j, l, r) for j in js for l, r in ((0, 0), (0, 1), (1, 0))]
                cut = [len(todo) * i // 4 for i in range(5)]
                for i in range(cut[part], cut[part + 1]):
                    j, l, r = todo[i]
                    mm = pe.matmul(ps[:, 7, b * 2 * P:(b + 1) * 2 * P], vb[:, j, l], at[:, b, r, j, :],
                                   start=(half == 0 and i == 0), stop=(half == 1 and i == len(todo) - 1))
                if part == 3:
                    mm.then_inc(pv_mm, 1)

            def step(it, t, scores=True, tr=True, pv=True):
                n = 4 * it + t
                b, half = t // 2, t % 2
                if scores:
                    pe.wait_ge(s_q[t], 64 * (it + 1))
                    if t == 0:
                        pe.wait_ge(s_k, 32 * (it // 4 + 1))
                for p in range(4):
                    if scores:
                        wait(pe, exp_done, 4 * n + p - 1)
                        for ver in range(2):
                            for c in range(2):
                                k0 = ((p % 2) * 2 + c) * N
                                keys = kb[:, 0, p // 2, k0:k0 + N] if isinstance(it, int) else \
                                    kb[:, bass.ds((it // 4) % 2, 1), p // 2, k0:k0 + N].rearrange("p o t -> p (o t)")
                                mm = pe.matmul(ps[:, 2 * (p % 2) + c, :], qb[:, t, ver, p // 2], keys,
                                               start=(ver == 0), stop=(ver == 1))
                        mm.then_inc(s_pair, 1)
                    if pv:
                        if p == 0:
                            pe.wait_ge(s_v[half], 16 * ((it + 3) // 4))
                            if half == 0:
                                pe.wait_ge(t_lo, 5 * (n - 2))
                                wait(pe, att_evac, 2 * (it - 1) + b)
                        product(b, half, p)
                    if tr:
                        if p == 0:
                            pe.wait_ge(a_ready, n - 1)
                        transposes(n - 2, (t - 2) % 4, p)
                if scores:
                    wait(pe, expc_done, n)
                    for m in range(2):
                        for ver in range(2):
                            keys = kb[:, 0, m, SAMPLE:KEYS] if isinstance(it, int) else \
                                kb[:, bass.ds((it // 4) % 2, 1), m, SAMPLE:KEYS].rearrange("p o t -> p (o t)")
                            mm = pe.matmul(ps[:, 4, m * P:(m + 1) * P], qb[:, t, ver, m], keys,
                                           start=(ver == 0), stop=(ver == 1))
                    mm.then_inc(s_ctx, 1)
                if tr:
                    transposes(n - 2, (t - 2) % 4, 4)

            for t in range(4):
                step(0, t, tr=t >= 2, pv=False)
            with pe.Fori(1, ITS) as it:
                for t in range(4):
                    step(it, t)
            for t in range(4):
                step(ITS, t, scores=False, tr=t < 2)

            def csums(k, n):
                pe.wait_ge(c_sq, k + 1)
                wait(pe, c_std, k - 1)
                pe.matmul(ps[:, 6 + k % 2, 0:n], ones, csq[:, 0:n], start=True, stop=True).then_inc(c_sum, 1)

            for h in range(H):
                csums(h, GROUPS[0][1])
            for tg in range(NG):
                c0, n = GROUPS[tg]
                for o in range(DJ):
                    k = DJ * tg + o
                    if tg == 0:
                        pe.wait_ge(c_wlo, o + 1)
                    if o == 0:
                        pe.wait_ge(c_mix[tg % 2], 32 * (tg // 2 + 1))
                    wait(pe, o_used, k - 3)
                    for half, js in ((0, range(H, DJ)), (1, range(H))):
                        if o == 0 and half == 1:
                            pe.wait_ge(c_lo, H * (tg + 1))
                        for i, (l, r) in enumerate(((0, 0), (0, 1), (1, 0))):
                            for j in js:
                                mm = pe.matmul(ps[:, k % 4, 0:n], wo[:, l, o, j], mix[:, tg % 2, r, j, 0:n],
                                               start=(half == 0 and i == 0 and j == H),
                                               stop=(half == 1 and i == 2 and j == H - 1))
                    mm.then_inc(o_mm, 1)
                    if o % 2 and tg + 1 < NG:
                        csums(H * (tg + 1) + o // 2, GROUPS[tg + 1][1])

        @block.scalar
        def _(act):
            act.wait_ge(s_const, 48)
            act.activation(sc[:].rearrange("p j v -> p (j v)"), c_in, ACT.Silu).then_inc(sc_ready, 1)
            act.wait_ge(lam_ch, 2)
            act.activation(lamt[:, 2:4], lamt[:, 0:2], ACT.Exp).then_inc(lam_e, 1)
            act.wait_ge(s_craw, 16)
            act.activation(r32(vhi), vraw, ACT.Copy).then_inc(hi_ready, 1)

            def w_split(c, buf, slot, ordinal):
                act.wait_ge(s_raw[buf], 16 * (ordinal + 1))
                act.activation(w[:, slot, 0], raw[:, buf], ACT.Copy).then_inc(w_hi, 1)

            def v_hi(t):
                act.wait_ge(z_mm, t + 1)
                act.wait_ge(stored, 32 * (2 + t))
                act.activation(r32(vhi), ps[:, t % BANKS, :], ACT.Copy).then_inc(hi_ready, 1)

            def x_square(g):
                n = XGROUPS[g][1]
                act.wait_ge(s_x[g % 2], 16 * (g // 2 + 1))
                wait(act, sum_mm, g)
                if g == 0:
                    act.wait_ge(lo_ready, 2)
                act.activation(xsq[:, :, 0:n], xs[:, g % 2, :, 0:n], ACT.Square).then_inc(sq_ready, 1)

            act.wait_ge(s_craw, 32)
            act.wait_ge(stored, 32)
            act.activation(r32(vhi), vraw, ACT.Copy).then_inc(hi_ready, 1)
            x_square(0)
            for g in range(XN):
                c0, n = XGROUPS[g]
                v = 0 if c0 < SAMPLE else 1
                act.wait_ge(sum_mm, g + 1)
                wait(act, rstd_ready, g)
                if g == 0:
                    act.wait_ge(zr_ready, 1)
                act.activation(xstd[:, 0:n], ps[:, 5 + g % 2, 0:n], ACT.Sqrt, scale=1.0 / D, bias=eps[:])\
                    .then_inc(std_ready, 1)
                if g + 1 < XN:
                    x_square(g + 1)
                if g == 0:
                    act.wait_ge(mod_mm, 6)
                    for c in range(4):
                        w_split(c, c % 2, c, c // 2)
                if g == 1:
                    w_split(4, 0, 4, 2)
                act.wait_ge(xn_ready, g + 1)
                if g == 0:
                    act.wait_ge(mod_ch, 3)
                for j in range(DJ):
                    hm = act.activation(xs[:, g % 2, j, 0:n], xs[:, g % 2, j, 0:n], ACT.Identity,
                                        scale=mult[:, j, v:v + 1], bias=mod[:, j, v:v + 1])
                hm.then_inc(h32_ready, 1)
                for t in range(max(0, 2 * g - 2), 2 * g):
                    v_hi(t)
            v_hi(TILES - 1)

            act.wait_ge(s_rope, 16)
            act.wait_ge(stored, 32 * (2 + V_UNITS))
            with act.Fori(0, H) as h:
                for u in range(QK_UNITS + 2):
                    k = QK_UNITS * h + u
                    if u < QK_UNITS:
                        n = GROUPS[u % NG][1]
                        act.wait_ge(z_mm, QK0 + k + 1)
                        act.wait_ge(sum_mm, XN + k)
                        act.activation(qsq[:, 0:n], ps[:, (QK0 + u) % BANKS, 0:n], ACT.Square).then_inc(sq_ready, 1)
                    if 1 <= u <= QK_UNITS:
                        n = GROUPS[(u - 1) % NG][1]
                        act.wait_ge(sum_mm, XN + k)
                        act.wait_ge(z_used, QK0 + k - 1)
                        act.activation(qrs[:, 0:n], ps[:, 5 + (XN + u - 1) % 2, 0:n], ACT.Sqrt,
                                       scale=1.0 / HD, bias=eps[:]).then_inc(std_ready, 1)
                    if u == 1:
                        act.wait_ge(z_mm, QK0 + QK_UNITS * h)
                        w_split(QKC + 2 * h + 1, 1, 0, 2 + h)
                    if u == 6:
                        act.wait_ge(z_mm, QK0 + QK_UNITS * h + NG)
                        w_split(QKC + 2 * h + 2, 0, 4, 3 + h)
                    if u >= 2:
                        n = GROUPS[(u - 2) % NG][1]
                        act.wait_ge(zr_ready, 1 + k - 1)
                        act.wait_ge(stored, 32 * (2 + V_UNITS) + 32 * (k - 2))
                        act.activation(r32(qhi[:, 0:n]), qt1[:, 0:n], ACT.Copy).then_inc(hi_ready, 1)

            act.wait_ge(lo_ready, 2 + H * QK_UNITS)

            def conv(f, last):
                for s in range(1, CV):
                    act.wait_ge(z_mm, CV0 + CV_UNITS * f - 4 + s)
                    w_split(0, CV_RAW[s], CV_SLOT[s], {1: 6 + 2 * f, 2: 7 + 3 * f, 3: 7 + 2 * f, 4: 8 + 3 * f}[s])
                for tg in range(NG):
                    n = GROUPS[tg][1]
                    for s in range(2):
                        act.wait_ge(z_mm, CV0 + CV_UNITS * f + CV * tg + s + 1)
                        act.wait_ge(z_used, CV0 + CV_UNITS * f + CV * (tg - 1) + s + 1)
                        act.activation(sig[:, s, 0:n], ps[:, (CV0 + s) % BANKS, 0:n], ACT.Sigmoid).then_inc(sig_ready, 1)
                if not last:
                    w_split(0, 0, CV_SLOT[0], 9 + 3 * f)

            with act.Fori(0, H - 1) as f:
                conv(f, False)
            conv(H - 1, True)

            act.wait_ge(pr_v, 2)
            act.activation(e1[:, 0, 0:2 * H * P], e1[:, 0, 0:2 * H * P], ACT.Exp).then_inc(pr_a, 1)
            act.wait_ge(pr_mm, 2)
            act.activation(at[:, 1, 0, 0:H, 0:P], ps[:, 5, :].rearrange("p (h t) -> p h t", h=H), ACT.Copy)\
                .then_inc(pr_a, 1)
            act.wait_ge(pr_mm, 3)
            act.activation(atto[:].rearrange("p b t -> p (b t)"), ps[:, 7, :], ACT.Copy).then_inc(pr_a, 1)
            act.wait_ge(pr_a, 3)
            act.dma_start(spill["att"][:, :, SAMPLE:T].rearrange("h p t -> p h t"),
                          atto[:].rearrange("p b (c t) -> p (b c) t", c=2)).then_inc(aux_stored, 16)
            act.wait_ge(aux_stored, 16 * (1 + H + H * NG + 1))

            def tr_hi(n, t, g):
                j0, cnt = TGROUPS[g]
                k = 5 * n + g
                act.wait_ge(t_mm, k + 1)
                if g == 0 and t % 2 == 0:
                    wait(act, pv_mm, n - 2)
                act.activation(at[:, t // 2, 0, j0:j0 + cnt, (t % 2) * P:(t % 2 + 1) * P],
                               ps[:, 5 + (5 * t + g) % 2, 0:cnt * P].rearrange("p (j q) -> p j q", j=cnt), ACT.Copy)\
                    .then_inc(t_hi, 1)

            def step(it, t, scores=True, prev=True, tr=True, pv=True):
                n = 4 * it + t
                b = t % 2
                for p in range(4):
                    m, c = p // 2, p % 2
                    if scores:
                        act.wait_ge(mx_done, 4 * n + p + 1)
                        if p == 0:
                            wait(act, t_mm, 5 * (n - 3))
                            wait(act, a_ready, n - 1)
                        dst = e0[:, t] if m == 0 else e1[:, b]
                        act.activation(dst[:, c * 1024:(c + 1) * 1024],
                                       ps[:, 2 * c:2 * c + 2, :].rearrange("p c n -> p (c n)"), ACT.Exp,
                                       bias=stt[:, b, 0, 3 * m + c:3 * m + c + 1],
                                       accum_out=stt[:, b, 1, 3 * m + c:3 * m + c + 1]).then_inc(exp_done, 1)
                    if p == 0 and prev:
                        act.wait_ge(d_done, n)
                        act.activation(stt[:, 1 - b, 3, :], stt[:, 1 - b, 2, :], ACT.Exp).then_inc(f_done, 1)
                    if tr:
                        tr_hi(n - 2, (t - 2) % 4, p)
                    if p == 2 and prev:
                        act.wait_ge(coef_done, n)
                        for c, (k0, k1) in enumerate(((0, 1024), (1024, 2048), (2048, KEYS))):
                            em = act.activation(e1[:, 1 - b, k0:k1], e1[:, 1 - b, k0:k1], ACT.Copy,
                                                scale=stt[:, 1 - b, 7, 3 + c:4 + c])
                        em.then_inc(e1_done, 1)
                if scores:
                    act.wait_ge(mxc_done, n + 1)
                    for m in range(2):
                        dst = e0[:, t] if m == 0 else e1[:, b]
                        em = act.activation(dst[:, SAMPLE:KEYS], ps[:, 4, m * P:(m + 1) * P], ACT.Exp,
                                            bias=stt[:, b, 0, 3 * m + 2:3 * m + 3],
                                            accum_out=stt[:, b, 1, 3 * m + 2:3 * m + 3])
                    em.then_inc(expc_done, 1)
                if tr:
                    tr_hi(n - 2, (t - 2) % 4, 4)
                if pv and t % 2:
                    pb = t // 2
                    act.wait_ge(pv_mm, n - 3)
                    wait(act, att_stored[pb], 16 * (it - 1))
                    act.activation(atto[:, pb], ps[:, 7, pb * 2 * P:(pb + 1) * 2 * P], ACT.Copy).then_inc(att_evac, 1)
                    act.wait_ge(att_evac, 2 * (it - 1) + pb + 1)
                    if isinstance(it, int):
                        hh, q0 = (it - 1) // 4, ((it - 1) % 4) * 4 * P + pb * 2 * P
                        dst = spill["att"][hh, :, q0:q0 + 2 * P]
                    else:
                        dst = spill["att"][bass.ds((it - 1) // 4, 1), :,
                                           bass.ds(((it - 1) % 4) * (4 * P) + pb * 2 * P, 2 * P)]\
                            .rearrange("o p t -> (o p) t")
                    act.dma_start(dst, atto[:, pb]).then_inc(att_stored[pb], 16)

            for t in range(4):
                step(0, t, prev=t > 0, tr=t >= 2, pv=False)
            for t in range(4):
                step(1, t)
            with act.Fori(2, ITS) as it:
                for t in range(4):
                    step(it, t)
            for t in range(4):
                step(ITS, t, scores=False, prev=t == 0, tr=t < 2)

            def wo_hi(n):
                act.wait_ge(c_raw[n % 2], 16 * (n // 2 + 1))
                act.activation(wo[:, 0, n], worw[:, n % 2], ACT.Copy).then_inc(c_whi, 1)

            def norm(tg, h):
                n = GROUPS[tg][1]
                k = H * tg + h
                if h == 0:
                    act.wait_ge(c_at, 32 * (tg + 1))
                wait(act, c_sum, k)
                act.activation(csq[:, 0:n], atr[:, h, 0:n], ACT.Square).then_inc(c_sq, 1)
                act.wait_ge(c_sum, k + 1)
                wait(act, c_rs, k)
                act.activation(cstd[:, 0:n], ps[:, 6 + k % 2, 0:n], ACT.Sqrt, scale=1.0 / P, bias=eps[:])\
                    .then_inc(c_std, 1)
                act.wait_ge(c_y2, k + 1)
                wait(act, o_mm, DJ * (tg - 1))
                act.activation(mix[:, tg % 2, 0, h, 0:n], cy[:, 0:n], ACT.Copy).then_inc(c_hi, 1)

            wo_hi(0)
            wo_hi(1)
            for h in range(H):
                norm(0, h)
                wo_hi(2 + h)
            wo_hi(6)
            wo_hi(7)
            for tg in range(1, NG):
                for h in range(H):
                    norm(tg, h)

        @block.vector
        def _(dve):
            dve.wait_ge(s_const, 48)
            for i in range(2):
                dve.tensor_tensor_reduce(lamj[:, i], lamv[:, 2 * i], lamv[:, 2 * i + 1], 1.0, 0.0, ALU.mult, ALU.add,
                                         lamt[:, i:i + 1]).then_inc(lam_ch, 1)
            dve.tensor_scalar(sublns[:], subln, 1.0 - LAM_INIT, None, ALU.mult).then_inc(lam_ch, 1)
            dve.tensor_scalar(qks[:, 0:1], qk_w[:, 0:1], HD ** -0.5, None, ALU.mult).then_inc(lam_ch, 1)
            dve.tensor_copy(qks[:, 1:2], qk_w[:, 1:2]).then_inc(lam_ch, 1)
            dve.wait_ge(lam_e, 1)
            dve.tensor_tensor(lamt[:, 4:5], lamt[:, 3:4], lamt[:, 2:3], ALU.subtract).then_inc(lam_ch, 1)
            dve.wait_ge(lam_ch, 6)
            dve.tensor_scalar(lamc[:, 1:2], lamt[:, 4:5], -LAM_INIT, None, ALU.add).then_inc(lam_ch, 1)

            def cache_lo(i):
                dve.wait_ge(hi_ready, i + 1)
                dve.tensor_tensor(r32(vlo), vraw, vhi, ALU.subtract).then_inc(lo_ready, 1)

            cache_lo(0)
            cache_lo(1)

            def w_split(c, buf, slot):
                dve.wait_ge(w_hi, c + 1)
                dve.tensor_tensor(w[:, slot, 1], raw[:, buf], f32(w[:, slot, 0]), ALU.subtract).then_inc(w_lo, 1)

            def v_lo(t):
                dve.wait_ge(hi_ready, 2 + t + 1)
                dve.tensor_tensor(r32(vlo), ps[:, t % BANKS, :], vhi, ALU.subtract).then_inc(z_used, 1)

            for g in range(XN):
                n = XGROUPS[g][1]
                if g == 0:
                    dve.wait_ge(s_x[0], 16)
                dve.wait_ge(std_ready, g + 1)
                wait(dve, xn_ready, g)
                dve.reciprocal(xrstd[:, 0:n], xstd[:, 0:n]).then_inc(rstd_ready, 1)
                dve.wait_ge(rstd_ready, g + 1)
                x = xs[:, g % 2, :, 0:n]
                dve.tensor_tensor(x, x, xrstd[:, 0:n].rearrange("p (o t) -> p o t", o=1).to_broadcast([P, DJ, n]),
                                  ALU.mult).then_inc(xn_ready, 1)
                if g == 0:
                    dve.wait_ge(mod_mm, 6)
                    dve.tensor_tensor(mod[:], ps[:, 7, 0:48].rearrange("p (n v) -> p n v", v=2),
                                      b_ada.rearrange("p (n o) -> p n o", o=1).to_broadcast([P, 24, 2]), ALU.add)\
                        .then_inc(mod_ch, 1)
                    dve.wait_ge(mod_ch, 1)
                    dve.tensor_scalar(mult[:], mod[:, 8:16], 1.0, None, ALU.add).then_inc(mod_ch, 1)
                    dve.wait_ge(mod_ch, 2)
                    dve.tensor_tensor(mult[:], mult[:], norm_w.rearrange("p (n o) -> p n o", o=1).to_broadcast([P, DJ, 2]),
                                      ALU.mult).then_inc(mod_ch, 1)
                    for c in range(4):
                        w_split(c, c % 2, c)
                if g == 1:
                    w_split(4, 0, 4)
                dve.wait_ge(h32_ready, g + 1)
                c0 = XGROUPS[g][0]
                dve.tensor_copy(hT[:, 0, :, c0:c0 + n], x).then_inc(hhi_ready, 1)
                dve.wait_ge(hhi_ready, g + 1)
                dve.tensor_tensor(hT[:, 1, :, c0:c0 + n], x, f32(hT[:, 0, :, c0:c0 + n]), ALU.subtract)\
                    .then_inc(hlo_ready, 1)
                for t in range(max(0, 2 * g - 2), 2 * g):
                    v_lo(t)
            dve.wait_ge(z_mm, TILES)
            dve.wait_ge(hi_ready, 2 + TILES)
            dve.wait_ge(sum_mm, XN)
            dve.tensor_copy(vraw, ps[:, (TILES - 1) % BANKS, :]).then_inc(nv_ready, 1)
            v_lo(TILES - 1)

            dve.wait_ge(s_rope, 16)
            dve.wait_ge(lam_ch, 7)
            dve.wait_ge(stored, 32 * (2 + V_UNITS))
            with dve.Fori(0, H) as h:
                for u in range(QK_UNITS + 1):
                    k = QK_UNITS * h + u
                    if u < QK_UNITS:
                        n = GROUPS[u % NG][1]
                        comp = 1 - u // NG
                        dve.wait_ge(std_ready, XN + k + 1)
                        dve.reciprocal(qrs[:, 0:n], qrs[:, 0:n]).then_inc(rstd_ready, 1)
                        dve.wait_ge(rstd_ready, XN + k + 1)
                        dve.wait_ge(p_t1, 1 + k)
                        dve.scalar_tensor_tensor(qzn[:, 0:n], ps[:, (QK0 + u) % BANKS, 0:n], qks[:, comp:comp + 1],
                                                 qrs[:, 0:n], ALU.mult, ALU.mult).then_inc(z_used, 1)
                        dve.wait_ge(zr_ready, 1 + k)
                        dve.wait_ge(z_used, QK0 + k + 1)
                        dve.tensor_copy(tick[:], eps[:])
                        dve.stream_shuffle(qt2[:, 0:n], qzn[:, 0:n], [i ^ 16 for i in range(32)]).then_inc(sh_ready, 1)
                    if u == 1:
                        w_split(QKC + 2 * h + 1, 1, 0)
                    if u == 6:
                        w_split(QKC + 2 * h + 2, 0, 4)
                    if u > 0:
                        n = GROUPS[(u - 1) % NG][1]
                        dve.wait_ge(hi_ready, 2 + V_UNITS + k)
                        dve.tensor_tensor(r32(qlo[:, 0:n]), qt1[:, 0:n], qhi[:, 0:n], ALU.subtract).then_inc(lo_ready, 1)

            dve.wait_ge(stored, 32 * (2 + V_UNITS + H * QK_UNITS))
            dve.wait_ge(lo_ready, 2 + H * QK_UNITS)
            for i, z in enumerate((ub[:, 0:1], ub[:, SAMPLE + 1:SAMPLE + 2], up[:, 0:1], up[:, PROMPT + 1:PROMPT + 2])):
                dve.memset(z, 0.0).then_inc(cvc, 1)
            dve.wait_ge(cvc, 4)

            def conv_group(f, tg):
                seq, o, n = useq(tg)
                c0 = GROUPS[tg][0]
                base = 4 + 6 * (NG * f + tg)

                def wcol(i):
                    return cw[:, i:i + 1]

                dve.wait_ge(cvc, base)
                dve.tensor_scalar(cc_[:, 0:n], seq[:, o:o + n], wcol(0), wcol(3), ALU.mult, ALU.add).then_inc(cvc, 1)
                for i in (1, 2):
                    dve.wait_ge(cvc, base + i)
                    dve.scalar_tensor_tensor(cc_[:, 0:n], seq[:, o + i:o + i + n], wcol(i), cc_[:, 0:n],
                                             ALU.mult, ALU.add).then_inc(cvc, 1)
                dve.wait_ge(cvc, base + 3)
                dve.tensor_tensor(cc_[:, 0:n], cc_[:, 0:n], gcb[:, c0:c0 + n], ALU.mult).then_inc(cvc, 1)
                dve.wait_ge(cvc, base + 4)
                dve.wait_ge(stored, 32 * (2 + V_UNITS + H * QK_UNITS) + 32 * (NG * f + tg))
                dve.tensor_copy(r32(chi[:, 0:n]), cc_[:, 0:n]).then_inc(cvc, 1)
                dve.wait_ge(cvc, base + 5)
                dve.tensor_tensor(r32(clo[:, 0:n]), cc_[:, 0:n], chi[:, 0:n], ALU.subtract).then_inc(cvc, 1)

            def conv(f, last):
                dve.wait_ge(cvc, 4 + 6 * NG * f)
                dve.tensor_copy(cw[:, 0:4], taps[:, bass.ds(4 * f, 4)]).then_inc(tapped, 1)
                for s in range(1, CV):
                    w_split(CVC + CV * f + s, CV_RAW[s], CV_SLOT[s])
                for tg in range(NG):
                    c0, n = GROUPS[tg]
                    z0 = CV0 + CV_UNITS * f + CV * tg
                    z = [ps[:, (CV0 + s) % BANKS, 0:n] for s in range(CV)]
                    dve.wait_ge(sig_ready, 2 * (NG * f + tg) + 1)
                    dve.wait_ge(aux_stored, 16 * (1 + H) + 16 * (NG * f + tg))
                    dve.tensor_tensor(gs[:, 0:n], z[0], sig[:, 0, 0:n], ALU.mult).then_inc(z_used, 1)
                    dve.wait_ge(sig_ready, 2 * (NG * f + tg) + 2)
                    g = gcb[:, c0:c0 + n]
                    dve.tensor_tensor(g, z[1], sig[:, 1, 0:n], ALU.mult).then_inc(z_used, 1)
                    dve.wait_ge(z_mm, z0 + 3)
                    dve.wait_ge(z_used, z0 + 2)
                    dve.tensor_tensor(g, z[2], g, ALU.mult).then_inc(z_used, 1)
                    dve.wait_ge(z_mm, z0 + 4)
                    dve.tensor_copy(ccs[:, 0:n], z[3]).then_inc(z_used, 1)
                    dve.wait_ge(z_mm, z0 + 5)
                    dve.wait_ge(z_used, z0 + 4)
                    seq, o, _ = useq(tg)
                    dve.tensor_tensor(seq[:, o + 1:o + 1 + n], z[4], ccs[:, 0:n], ALU.mult).then_inc(z_used, 1)
                    dve.wait_ge(z_used, z0 + 5)
                    if tg == 1:
                        dve.wait_ge(tapped, f + 1)
                    for tc in ([] if tg == 0 else [tg - 1] if tg < TG else [TG - 1, TG]):
                        conv_group(f, tc)
                if not last:
                    w_split(CVC + CV * f + CV, 0, CV_SLOT[0])

            with dve.Fori(0, H - 1) as f:
                conv(f, False)
            conv(H - 1, True)

            def maps(x):
                return x.rearrange("p (m t) -> p m t", m=2 * H)

            def wide(x):
                return x.rearrange("p (m o) -> p m o", o=1).to_broadcast([P, 2 * H, P])

            scores_p = maps(ps[:, 0:2, :].rearrange("p c n -> p (c n)"))
            ep = e1[:, 0, 0:2 * H * P]
            dve.wait_ge(pr_mm, 1)
            dve.tensor_reduce(stp[:, 0], scores_p, AX.X, ALU.max).then_inc(pr_v, 1)
            dve.wait_ge(pr_v, 1)
            dve.tensor_tensor(maps(ep), scores_p, wide(stp[:, 0]), ALU.subtract).then_inc(pr_v, 1)
            dve.wait_ge(pr_a, 1)
            dve.tensor_reduce(stp[:, 1], maps(ep), AX.X, ALU.add).then_inc(pr_v, 1)
            dve.wait_ge(pr_v, 3)
            dve.reciprocal(stp[:, 2], stp[:, 1]).then_inc(pr_v, 1)
            dve.wait_ge(pr_v, 4)
            dve.tensor_tensor(stp[:, 3].rearrange("p (h m) -> p h m", m=2), stp[:, 2].rearrange("p (h m) -> p h m", m=2),
                              lamc[:].rearrange("p (o m) -> p o m", o=1).to_broadcast([P, H, 2]), ALU.mult)\
                .then_inc(pr_v, 1)
            dve.wait_ge(pr_v, 5)
            dve.tensor_tensor(maps(ep), maps(ep), wide(stp[:, 3]), ALU.mult).then_inc(pr_v, 1)
            dve.wait_ge(pr_v, 6)
            eh = ep.rearrange("p (h m t) -> p h m t", h=H, m=2)
            dve.tensor_tensor(e0[:, 0, 0:H * P].rearrange("p (h t) -> p h t", h=H), eh[:, :, 0], eh[:, :, 1], ALU.add)\
                .then_inc(pr_v, 1)
            dve.wait_ge(pr_a, 2)
            dve.tensor_tensor(at[:, 1, 1, 0:H, 0:P], ps[:, 5, :].rearrange("p (h t) -> p h t", h=H),
                              f32(at[:, 1, 0, 0:H, 0:P]), ALU.subtract).then_inc(pr_v, 1)

            def tr_lo(n, t, g):
                j0, cnt = TGROUPS[g]
                k = 5 * n + g
                dve.wait_ge(t_hi, k + 1)
                cols = slice((t % 2) * P, (t % 2 + 1) * P)
                dve.tensor_tensor(at[:, t // 2, 1, j0:j0 + cnt, cols],
                                  ps[:, 5 + (5 * t + g) % 2, 0:cnt * P].rearrange("p (j q) -> p j q", j=cnt),
                                  f32(at[:, t // 2, 0, j0:j0 + cnt, cols]), ALU.subtract).then_inc(t_lo, 1)

            def step(it, t, scores=True, prev=True, tr=True):
                n = 4 * it + t
                b = t % 2
                for p in range(4):
                    m, c = p // 2, p % 2
                    if scores:
                        dve.wait_ge(s_pair, 4 * n + p + 1)
                        if p == 0:
                            wait(dve, coef_done, n - 1)
                            wait(dve, e1_done, n - 1)
                        dve.tensor_reduce(stt[:, b, 0, 3 * m + c:3 * m + c + 1],
                                          ps[:, 2 * c:2 * c + 2, :].rearrange("p c n -> p (c n)"), AX.X, ALU.max,
                                          negate=True).then_inc(mx_done, 1)
                    if tr:
                        tr_lo(n - 2, (t - 2) % 4, p)
                    if p == 1 and prev:
                        o = 1 - b
                        dve.wait_ge(fz_done, n)
                        dve.tensor_reduce(stt[:, o, 5, 0:2], stt[:, o, 4, :].rearrange("p (m c) -> p m c", m=2), AX.X,
                                          ALU.add).then_inc(den_done, 1)
                        dve.wait_ge(den_done, n)
                        dve.reciprocal(stt[:, o, 6, 0:2], stt[:, o, 5, 0:2]).then_inc(rden_done, 1)
                if scores:
                    dve.wait_ge(s_ctx, n + 1)
                    dve.tensor_reduce(stt[:, b, 0, 2:6:3], ps[:, 4, 0:2 * P].rearrange("p (m k) -> p m k", m=2), AX.X,
                                      ALU.max, negate=True).then_inc(mxc_done, 1)
                    dve.wait_ge(mxc_done, n + 1)
                    dve.wait_ge(mx_done, 4 * n + 4)
                    dve.tensor_reduce(stt[:, b, 5, 2:4], stt[:, b, 0, :].rearrange("p (m c) -> p m c", m=2), AX.X,
                                      ALU.min).then_inc(gm_done, 1)
                if tr:
                    tr_lo(n - 2, (t - 2) % 4, 4)
                if prev:
                    o = 1 - b
                    tt = (t - 1) % 4
                    dve.wait_ge(coef_done, n)
                    dve.wait_ge(e1_done, n)
                    for c, (k0, k1) in enumerate(((0, 1024), (1024, 2048), (2048, KEYS))):
                        am = dve.scalar_tensor_tensor(e0[:, tt, k0:k1], e0[:, tt, k0:k1], stt[:, o, 7, c:c + 1],
                                                      e1[:, o, k0:k1], ALU.mult, ALU.add)
                    am.then_inc(a_ready, 1)

            for t in range(4):
                step(0, t, prev=t > 0, tr=t >= 2)
            with dve.Fori(1, ITS) as it:
                for t in range(4):
                    step(it, t)
            for t in range(2):
                step(ITS, t, scores=False, prev=t == 0)

            def wo_lo(n):
                dve.wait_ge(c_whi, n + 1)
                dve.tensor_tensor(wo[:, 1, n], worw[:, n % 2], f32(wo[:, 0, n]), ALU.subtract).then_inc(c_wlo, 1)

            def norm(tg, h):
                n = GROUPS[tg][1]
                k = H * tg + h
                dve.wait_ge(c_std, k + 1)
                dve.reciprocal(crs[:, 0:n], cstd[:, 0:n]).then_inc(c_rs, 1)
                dve.wait_ge(c_rs, k + 1)
                dve.scalar_tensor_tensor(cy[:, 0:n], atr[:, h, 0:n], sublns[:], crs[:, 0:n], ALU.mult, ALU.mult)\
                    .then_inc(c_y1, 1)
                dve.wait_ge(c_y1, k + 1)
                dve.tensor_tensor(cy[:, 0:n], cy[:, 0:n], gar[:, h, 0:n], ALU.mult).then_inc(c_y2, 1)
                dve.wait_ge(c_hi, k + 1)
                dve.tensor_tensor(mix[:, tg % 2, 1, h, 0:n], cy[:, 0:n], f32(mix[:, tg % 2, 0, h, 0:n]), ALU.subtract)\
                    .then_inc(c_lo, 1)

            wo_lo(0)
            wo_lo(1)
            for h in range(H):
                if h == 0:
                    dve.wait_ge(c_at, 32)
                norm(0, h)
                wo_lo(2 + h)
            wo_lo(6)
            wo_lo(7)
            for tg in range(NG):
                c0, n = GROUPS[tg]
                v = 0 if tg < TG else 1
                for o in range(DJ):
                    k = DJ * tg + o
                    dve.wait_ge(o_mm, k + 1)
                    if o == 0:
                        dve.wait_ge(c_x[tg % 2], 16 * (tg // 2 + 1))
                    wait(dve, o_st[o % 4], 16 * (2 * tg + o // 4))
                    dve.scalar_tensor_tensor(yo[:, o % 4, 0:n], ps[:, k % 4, 0:n], mod[:, 16 + o, v:v + 1],
                                             xr[:, tg % 2, o, 0:n], ALU.mult, ALU.add).then_inc(o_used, 1)
                    if o % 2 and tg + 1 < NG:
                        if o == 1:
                            dve.wait_ge(c_at, 32 * (tg + 2))
                        norm(tg + 1, o // 2)


def _rope_tables():
    grid_w, freqs, base = 64, HD // 4, 10000.0
    t = np.arange(SAMPLE)
    inv = (np.float32(1.0) / (np.float32(base) ** (np.arange(freqs, dtype=np.float32) / np.float32(freqs))))
    inv = inv.astype(np.float32)
    ang = np.stack([(t // grid_w).astype(np.float32)[:, None] * inv, (t % grid_w).astype(np.float32)[:, None] * inv])
    cos, sin = np.cos(ang).astype(np.float32), np.sin(ang).astype(np.float32)
    table = np.zeros((P, 2, T), np.float32)
    table[:, 0, SAMPLE:] = 1.0
    for p in range(P):
        d = p % HD
        half, lower, i = d // 32, d % 32 < 16, d % 16
        table[p, 0, :SAMPLE] = cos[half, :, i]
        table[p, 1, :SAMPLE] = -sin[half, :, i] if lower else sin[half, :, i]
    return table.reshape(P, 2 * T)


def _constants():
    blk = np.zeros((P, P), np.float32)
    blk[:HD, :HD] = blk[HD:, HD:] = 1.0
    return np.stack([np.eye(P, dtype=np.float32), np.ones((P, P), np.float32), blk], axis=1)


def kernel(**inputs):
    import concourse.bacc as _bacc
    from concourse.bass_utils import run_bass_kernel_spmd as _run

    x = {k: np.asarray(v) for k, v in inputs.items()}

    def cols(v):
        return np.ascontiguousarray(v.reshape(-1, P).T)

    tokens = np.concatenate([x["x_sample"][0], x["x_prompt"][0]], axis=0)
    xT = tokens.T.reshape(DJ, P, T).transpose(1, 0, 2)
    w_in = x["w_in"][0].reshape(DJ, P, 32, P).transpose(2, 1, 0, 3)
    q0, k0, v0, ga0, cb0, cc0, ch0, gc0 = range(0, 32, 4)
    order = [v0 + i for i in range(4)]
    for i in range(H):
        order += [k0 + i, q0 + i]
    for i in range(H):
        order += [ga0 + i, gc0 + i, cb0 + i, cc0 + i, ch0 + i]
    small = np.concatenate([
        cols(x["norm_w"][0]), np.tile(x["q_norm_w"][0], 2)[:, None], np.tile(x["k_norm_w"][0], 2)[:, None],
        x["subln_w"][0][:, None],
        np.concatenate([np.concatenate([cols(x["conv_w"][0, i])[:, f:f + 1] for i in range(3)]
                                       + [cols(x["conv_b"][0])[:, f:f + 1]], axis=1) for f in range(4)], axis=1),
        cols(x["b_ada"][0]),
        np.stack([cols(x["c"][0]), cols(x["c_ctx"])], axis=2).reshape(P, 2 * DJ)], axis=1)
    arrays = {
        "xT": xT,
        "w_ada": x["w_ada"][0].reshape(DJ, P, 24, P).transpose(2, 1, 0, 3),
        "w_in": w_in[order],
        "w_out": x["w_out"][0].reshape(DJ, P, DJ, P).transpose(2, 1, 0, 3),
        "small": small,
        "lam": np.broadcast_to(np.stack([x["lambda_q1"][0], x["lambda_k1"][0], x["lambda_q2"][0], x["lambda_k2"][0]]),
                               (P, 4, HD)),
        "cache_k": x["cache_k"][0, 0].reshape(CACHE, H, P).transpose(1, 2, 0),
        "cache_v": x["cache_v"][0, 0].reshape(CACHE, H * P),
        "rope": _rope_tables(),
        "cst": _constants(),
    }
    nc = _bacc.Bacc("TRN2", target_bir_lowering=False, num_devices=1, dynamic_dma_scratch_size=1024)
    arrays = {f"in_{k}": np.ascontiguousarray(v) for k, v in arrays.items()}
    aps = {k[3:]: nc.dram_tensor(k, v.shape, mybir.dt.from_np(v.dtype), kind="ExternalInput").ap()
           for k, v in arrays.items()}
    for name, shape in (("y", [DJ, P, T]), ("new_k", [H, P, PROMPT]), ("new_v", [P, H * P])):
        aps[name] = nc.dram_tensor(f"out_{name}", shape, F32, kind="ExternalOutput").ap()
    hymba_layer(nc, aps)
    r = _run(nc, [arrays], core_ids=[0]).results[0]
    y = np.asarray(r["out_y"]).reshape(D, T).T
    new_k = np.asarray(r["out_new_k"]).transpose(2, 0, 1).reshape(1, 1, PROMPT, H, 2, HD)
    new_v = np.asarray(r["out_new_v"]).reshape(1, 1, PROMPT, H, P)
    return (np.ascontiguousarray(y[SAMPLE:])[None], np.ascontiguousarray(y[:SAMPLE])[None],
            np.ascontiguousarray(new_k), np.ascontiguousarray(new_v))
```

```python
import math
from contextlib import ExitStack

import numpy as np
import concourse.bass as bass
from concourse import mybir

F32 = mybir.dt.float32
F32R = mybir.dt.float32r
ALU = mybir.AluOpType
ACT = mybir.ActivationFunctionType
AX = mybir.AxisListType

P = 128
D = 1024
DJ = D // P
SAMPLE, PROMPT, CACHE = 2048, 128, 128
T = SAMPLE + PROMPT
KEYS = SAMPLE + CACHE
KCOLS = KEYS + PROMPT
H = 4
HD = 64
N = 512
TG = T // N
GROUPS = [(g * N, N) for g in range(TG)] + [(SAMPLE, PROMPT)]
NG = len(GROUPS)
XG = 256
XGROUPS = [(g * XG, XG) for g in range(SAMPLE // XG)] + [(SAMPLE, PROMPT)]
KT = KEYS // P
TILES = T // P
EPS = 1e-6
LAM_INIT = 0.8 - 0.6 * math.exp(-0.3 * 0)
BANKS = 5
QK_UNITS = 2 * NG
CV = 5
CV_UNITS = CV * NG
QT = SAMPLE // P
ITS = H * QT // 4
TGROUPS = [(0, 4), (4, 4), (8, 4), (12, 4), (16, 1)]
PIECES = [(0, 1024), (1024, SAMPLE), (SAMPLE, KEYS)]
S_COMB, S_TR, S_PV, S_OUT = 2, 3, 5, 7
NT = H * QT


def wait(eng, sem, value):
    if isinstance(value, int) and value <= 0:
        return
    eng.wait_ge(sem, value)


def hymba_layer(nc, a):
    spill = {}
    for name, shape in (("k", [H, 2, P, KCOLS]), ("q", [H, 2, P, T]), ("v", [H, P, KT + 1, 2, P]),
                        ("ga", [H, P, T]), ("cv", [H, 2, P, T]), ("att", [H, P, T])):
        spill[name] = nc.dram_tensor(f"spill_{name}", shape, F32, kind="Internal").ap()

    ctx = ExitStack()
    with ctx:
        def sb(name, shape, dt=F32, c=ctx):
            return c.enter_context(nc.sbuf_tensor(name, shape, dt))

        def sem(name):
            return ctx.enter_context(nc.semaphore(name))

        ps = ctx.enter_context(nc.psum_tensor("ps", [P, 8, N], F32))

        cst = sb("cst", [P, 3, P])
        ident, ones, blk = cst[:, 0], cst[:, 1], cst[:, 2]
        small = sb("small", [P, 67])
        norm_w, qk_w, subln = small[:, 0:8], small[:, 8:10], small[:, 10:11]
        taps, b_ada = small[:, 11:27], small[:, 27:51]
        c_in = small[:, 51:67]
        eps = sb("eps", [P, 1])
        sc = sb("sc", [P, DJ, 2])
        mod = sb("mod", [P, 24, 2])
        mult = sb("mult", [P, DJ, 2])
        lamv = sb("lamv", [P, 4, HD])
        lamj = sb("lamj", [P, 2, HD])
        lamt = sb("lamt", [P, 6])
        lamc = sb("lamc", [P, 2])
        sublns = sb("sublns", [P, 1])
        qks = sb("qks", [P, 2])
        tick = sb("tick", [P, 1])
        cw = sb("cw", [P, 4])

        with ExitStack() as actx:
            hT = sb("hT", [P, 2, DJ, T], F32R, actx)
            with ExitStack() as wctx:
                wad = sb("wad", [P, 2, 4, DJ, P], F32, wctx)
            w = sb("w", [P, 5, 2, DJ, P], F32R, actx)
            raw = sb("raw", [P, 2, DJ, P], F32, actx)
            scr = sb("scr", [P, 8000], F32, actx)
        with ExitStack() as bctx:
            kb = sb("kb", [P, 2, 2, KEYS], F32R, bctx)
            vb = sb("vb", [P, KT, 2, P], F32R, bctx)
            qb = sb("qb", [P, 4, 2, 2, P], F32R, bctx)
            e0 = sb("e0", [P, 4, KEYS], F32, bctx)
            e1 = sb("e1", [P, 2, KEYS], F32, bctx)
            at = sb("at", [P, 2, 2, KT, 2 * P], F32R, bctx)
            atto = sb("atto", [P, 2, 2 * P], F32, bctx)
            stt = sb("stt", [P, 2, 8, 6], F32, bctx)
            qp = sb("qp", [P, 2, 2 * H, P], F32R, bctx)
            kp = sb("kp", [P, 2 * H, P], F32R, bctx)
            vp = sb("vp", [P, H, 2, P], F32R, bctx)
            stp = sb("stp", [P, 4, 2 * H], F32, bctx)
        with ExitStack() as cctx:
            wo = sb("wo", [P, 2, DJ, DJ, P], F32R, cctx)
            worw = sb("worw", [P, 2, DJ, P], F32, cctx)
            mix = sb("mix", [P, 2, 2, DJ, N], F32R, cctx)
            atr = sb("atr", [P, H, N], F32, cctx)
            gar = sb("gar", [P, H, N], F32, cctx)
            xr = sb("xr", [P, 2, DJ, N], F32, cctx)
            yo = sb("yo", [P, 4, N], F32, cctx)
            csq = sb("csq", [P, N], F32, cctx)
            cstd = sb("cstd", [P, N], F32, cctx)
            crs = sb("crs", [P, N], F32, cctx)
            cy = sb("cy", [P, N], F32, cctx)

        xs = scr[:, 0:4096].rearrange("p (b j t) -> p b j t", b=2, j=DJ)
        xsq = scr[:, 4096:6144].rearrange("p (j t) -> p j t", j=DJ)
        xstd, xrstd = scr[:, 6144:6400], scr[:, 6400:6656]
        vraw = scr[:, 4352:4864]
        vhi, vlo = scr[:, 6656:7168], scr[:, 7168:7680]
        cosT, sinT = scr[:, 0:T], scr[:, T:2 * T]
        qsq, qrs, qzn, qt1, qt2, qhi, qlo = (scr[:, 2 * T + i * N:2 * T + (i + 1) * N] for i in range(7))
        sig = scr[:, 0:2 * N].rearrange("p (b n) -> p b n", b=2)
        gs, ccs, cc_, chi, clo = (scr[:, i * N:(i + 1) * N] for i in range(2, 7))
        ub = scr[:, 7 * N:7 * N + SAMPLE + 2]
        up = scr[:, 7 * N + SAMPLE + 2:7 * N + SAMPLE + 2 + PROMPT + 2]
        g0 = 7 * N + SAMPLE + PROMPT + 4
        gcb = scr[:, g0:g0 + T]

        def useq(tg):
            c0, n = GROUPS[tg]
            return (up, 0, n) if tg == TG else (ub, c0, n)

        s_const = sem("s_const")
        s_x = [sem(f"s_x{i}") for i in range(2)]
        s_wada = [sem(f"s_wada{i}") for i in range(2)]
        s_raw = [sem(f"s_raw{i}") for i in range(2)]
        s_craw = sem("s_craw")
        s_rope = sem("s_rope")
        stored = sem("stored")
        aux_stored = sem("aux_stored")
        lam_ch = sem("lam_ch")
        lam_e = sem("lam_e")
        sc_ready = sem("sc_ready")
        mod_mm = sem("mod_mm")
        mod_ch = sem("mod_ch")
        sq_ready = sem("sq_ready")
        sum_mm = sem("sum_mm")
        std_ready = sem("std_ready")
        rstd_ready = sem("rstd_ready")
        xn_ready = sem("xn_ready")
        h32_ready = sem("h32_ready")
        hhi_ready = sem("hhi_ready")
        hlo_ready = sem("hlo_ready")
        w_hi = sem("w_hi")
        w_lo = sem("w_lo")
        z_mm = sem("z_mm")
        z_used = sem("z_used")
        hi_ready = sem("hi_ready")
        lo_ready = sem("lo_ready")
        nv_ready = sem("nv_ready")
        sh_ready = sem("sh_ready")
        p_t1 = sem("p_t1")
        p_t2 = sem("p_t2")
        zr_ready = sem("zr_ready")
        sig_ready = sem("sig_ready")
        cvc = sem("cvc")
        tapped = sem("tapped")
        s_p = sem("s_p")
        s_k = sem("s_k")
        s_v = [sem(f"s_v{i}") for i in range(2)]
        s_q = [sem(f"s_q{i}") for i in range(4)]
        pr_mm = sem("pr_mm")
        pr_v = sem("pr_v")
        pr_a = sem("pr_a")
        s_pair = sem("s_pair")
        s_ctx = sem("s_ctx")
        mx_done = sem("mx_done")
        mxc_done = sem("mxc_done")
        gm_done = sem("gm_done")
        exp_done = sem("exp_done")
        expc_done = sem("expc_done")
        d_done = sem("d_done")
        f_done = sem("f_done")
        fz_done = sem("fz_done")
        den_done = sem("den_done")
        rden_done = sem("rden_done")
        rl_done = sem("rl_done")
        coef_done = sem("coef_done")
        e1_done = sem("e1_done")
        a_ready = sem("a_ready")
        t_mm = sem("t_mm")
        t_hi = sem("t_hi")
        t_lo = sem("t_lo")
        pv_mm = sem("pv_mm")
        att_evac = sem("att_evac")
        att_stored = [sem(f"att_stored{i}") for i in range(2)]
        c_raw = [sem(f"c_raw{i}") for i in range(2)]
        c_whi = sem("c_whi")
        c_wlo = sem("c_wlo")
        c_at = sem("c_at")
        c_mix = [sem(f"c_mix{i}") for i in range(2)]
        c_x = [sem(f"c_x{i}") for i in range(2)]
        c_sq = sem("c_sq")
        c_sum = sem("c_sum")
        c_std = sem("c_std")
        c_rs = sem("c_rs")
        c_y1 = sem("c_y1")
        c_y2 = sem("c_y2")
        c_hi = sem("c_hi")
        c_lo = sem("c_lo")
        o_mm = sem("o_mm")
        o_used = sem("o_used")
        o_st = [sem(f"o_st{i}") for i in range(4)]

        block = ctx.enter_context(nc.Block())

        V_UNITS = TILES
        QK0 = V_UNITS
        CV0 = V_UNITS + H * QK_UNITS
        ALL = CV0 + H * CV_UNITS
        XN = len(XGROUPS)
        CHUNKS = 32
        QKC, CVC = 4, 12
        CV_SLOT = [4, 1, 2, 3, 0]
        CV_RAW = [0, 1, 0, 1, 0]

        def f32(ap):
            return ap.bitcast(F32)

        def r32(ap):
            return ap.bitcast(F32R)

        def trbank(g):
            cnt = TGROUPS[g][1]
            return ps[:, 5 + g % 2, 0:cnt * P] if g < 4 else ps[:, 4, 2 * P:(2 + cnt) * P]

        @block.sync
        def _(sp):
            def load_w(c, buf):
                sp.dma_start(raw[:, buf], a["w_in"][c]).then_inc(s_raw[buf], 16)

            sp.dma_start(cst[:], a["cst"]).then_inc(s_const, 16)
            sp.dma_start(small[:], a["small"]).then_inc(s_const, 16)
            sp.dma_start(lamv[:], a["lam"]).then_inc(s_const, 16)
            for g in range(2):
                sp.dma_start(xs[:, g], a["xT"][:, :, g * XG:(g + 1) * XG]).then_inc(s_x[g], 16)
            sp.dma_start(vraw.rearrange("p (h t) -> p h t", h=H),
                         a["cache_k"].rearrange("h p t -> p h t")).then_inc(s_craw, 16)
            load_w(0, 0)
            load_w(1, 1)
            for hf in range(6):
                wait(sp, mod_mm, hf - 1)
                sp.dma_start(wad[:, hf % 2], a["w_ada"][4 * hf:4 * hf + 4].rearrange("n p j c -> p n j c"))\
                    .then_inc(s_wada[hf % 2], 16)
                if hf == 0:
                    sp.wait_ge(hi_ready, 1)
                    sp.wait_ge(lo_ready, 1)
                    for hl, src in ((0, vhi), (1, vlo)):
                        sp.dma_start(spill["k"][:, hl, :, SAMPLE:KEYS].rearrange("h p t -> p h t"),
                                     src.rearrange("p (h t) -> p h t", h=H)).then_inc(stored, 16)
                    sp.dma_start(vraw, a["cache_v"]).then_inc(s_craw, 16)
                if hf == 1:
                    sp.wait_ge(hi_ready, 2)
                    sp.wait_ge(lo_ready, 2)
                    for hl, src in ((0, vhi), (1, vlo)):
                        sp.dma_start(spill["v"][:, :, KT - 1, hl, :].rearrange("h p e -> p h e"),
                                     src.rearrange("p (h e) -> p h e", h=H)).then_inc(stored, 16)

            for c in range(2, 6):
                sp.wait_ge(w_lo, c - 1)
                load_w(c, c % 2)
            for g in range(XN + 1):
                if g + 2 < XN:
                    c0, n = XGROUPS[g + 2]
                    sp.wait_ge(hlo_ready, g + 1)
                    sp.dma_start(xs[:, g % 2, :, 0:n], a["xT"][:, :, c0:c0 + n]).then_inc(s_x[g % 2], 16)
                if g == 3:
                    sp.wait_ge(w_lo, 5)
                    load_w(6, 0)
                for t in range(max(0, 2 * g - 2), min(2 * g, TILES)):
                    sp.wait_ge(hi_ready, 2 + t + 1)
                    sp.wait_ge(z_used, t + 1)
                    for hl, src in ((0, vhi), (1, vlo)):
                        sp.dma_start(spill["v"][:, :, t if t < TILES - 1 else KT, hl, :].rearrange("h p e -> p h e"),
                                     src.rearrange("p (h e) -> p h e", h=H)).then_inc(stored, 16)
            sp.wait_ge(nv_ready, 1)
            sp.dma_start(a["new_v"], vraw).then_inc(aux_stored, 16)
            sp.wait_ge(hlo_ready, XN)
            sp.wait_ge(aux_stored, 16)
            sp.wait_ge(sum_mm, XN)
            sp.dma_start(scr[:, 0:2 * T], a["rope"]).then_inc(s_rope, 16)

            for h in range(H):
                for u in range(QK_UNITS):
                    c0, n = GROUPS[u % NG]
                    if u == 2:
                        sp.wait_ge(w_lo, 6 + 2 * h)
                        load_w(7 + 2 * h, 1)
                    if u == 7:
                        sp.wait_ge(w_lo, 7 + 2 * h)
                        load_w(8 + 2 * h, 0)
                    sp.wait_ge(hi_ready, 2 + V_UNITS + QK_UNITS * h + u + 1)
                    if u == NG - 1:
                        sp.dma_start(a["new_k"][h], qt1[:, 0:n])\
                            .then_inc(aux_stored, 16)
                    sp.wait_ge(lo_ready, 2 + QK_UNITS * h + u + 1)
                    dst = spill["k"] if u < NG else spill["q"]
                    col = c0 if u != NG - 1 else KEYS
                    for hl, src in ((0, qhi), (1, qlo)):
                        sp.dma_start(dst[h, hl, :, col:col + n], src[:, 0:n])\
                            .then_inc(stored, 16)

            for f in range(H):
                c = CVC + CV * f
                for tg in range(NG):
                    c0, n = GROUPS[tg]
                    if tg == 0:
                        sp.wait_ge(w_lo, c + 2)
                        load_w(c + 3, 1)
                        sp.wait_ge(w_lo, c + 3)
                        load_w(c + 4, 0)
                        if f + 1 < H:
                            sp.wait_ge(w_lo, c + 5)
                            load_w(c + 5, 0)
                            load_w(c + 6, 1)
                    sp.wait_ge(z_used, CV0 + CV_UNITS * f + CV * tg + 1)
                    sp.dma_start(spill["ga"][f, :, c0:c0 + n], gs[:, 0:n]).then_inc(aux_stored, 16)
                    for tc in ([] if tg == 0 else [tg - 1] if tg < TG else [TG - 1, TG]):
                        c0, n = GROUPS[tc]
                        sp.wait_ge(cvc, 4 + 6 * (NG * f + tc) + 6)
                        for hl, src in ((0, chi), (1, clo)):
                            sp.dma_start(spill["cv"][f, hl, :, c0:c0 + n], src[:, 0:n]).then_inc(stored, 16)
                if f + 1 < H:
                    sp.wait_ge(w_lo, c + 6)
                    load_w(c + 7, 0)

            sp.wait_ge(z_mm, ALL)
            sp.wait_ge(stored, 32 * (2 + V_UNITS + H * QK_UNITS + H * NG))
            sp.wait_ge(aux_stored, 16 * (1 + H + H * NG))

            def load_q(t, head, col):
                for ver in range(2):
                    for hl in range(2):
                        half = HD * (hl ^ ver)
                        sp.dma_start(f32(qb[half:half + HD, t, ver]),
                                     spill["q"][head, hl, :, col:col + P].rearrange("(m d) t -> d m t", m=2))\
                            .then_inc(s_q[t], 16)

            def load_k(head):
                for hl in range(2):
                    sp.dma_start(f32(kb[HD * hl:HD * hl + HD, head % 2]),
                                 spill["k"][head, hl, :, 0:KEYS].rearrange("(m d) t -> d m t", m=2)).then_inc(s_k, 16)

            def load_v(head, part):
                j0, j1 = (0, 9) if part == 0 else (9, KT)
                sp.dma_start(f32(vb[:, j0:j1]), spill["v"][head, :, j0:j1]).then_inc(s_v[part], 16)

            for head in range(H):
                for hl in range(2):
                    for ver in range(2):
                        half = HD * (hl ^ ver)
                        sp.dma_start(f32(qp[half:half + HD, ver, 2 * head:2 * head + 2]),
                                     spill["q"][head, hl, :, SAMPLE:T].rearrange("(m d) t -> d m t", m=2)).then_inc(s_p, 16)
                    sp.dma_start(f32(kp[HD * hl:HD * hl + HD, 2 * head:2 * head + 2]),
                                 spill["k"][head, hl, :, KEYS:KCOLS].rearrange("(m d) t -> d m t", m=2)).then_inc(s_p, 16)
            sp.dma_start(f32(vp[:]), spill["v"][:, :, KT].rearrange("h p l e -> p h l e")).then_inc(s_p, 16)
            for t in range(4):
                load_q(t, 0, t * P)
            load_k(0)
            load_v(0, 0)
            load_v(0, 1)
            for it in range(ITS):
                head = it // 4
                for t in range(4):
                    sp.wait_ge(s_pair, 4 * (4 * it + t + 1))
                    if it % 4 == 0 and t == 0 and head + 1 < H:
                        load_k(head + 1)
                    if it % 4 == 0 and head > 0 and t == 3:
                        sp.wait_ge(pv_mm, 4 * it - 1)
                        load_v(head, 0)
                    if it % 4 == 1 and head > 0 and t == 0:
                        sp.wait_ge(pv_mm, 4 * (it - 1))
                        load_v(head, 1)
                    if it + 1 < ITS:
                        load_q(t, (it + 1) // 4, ((it + 1) % 4) * 4 * P + t * P)

            sp.wait_ge(pv_mm, NT)
            sp.wait_ge(att_evac, NT // 2)
            for i in range(2):
                sp.wait_ge(att_stored[i], 16 * ITS)
            sp.wait_ge(pr_a, 3)
            sp.wait_ge(aux_stored, 16 * (1 + H + H * NG + 1))

            def loads(tg):
                c0, n = GROUPS[tg]
                par = tg % 2
                wait(sp, c_lo, 4 * tg)
                sp.dma_start(atr[:, :, 0:n], spill["att"][:, :, c0:c0 + n].rearrange("h p t -> p h t")).then_inc(c_at, 16)
                sp.dma_start(gar[:, :, 0:n], spill["ga"][:, :, c0:c0 + n].rearrange("h p t -> p h t")).then_inc(c_at, 16)
                wait(sp, o_mm, DJ * (tg - 1))
                for hl in range(2):
                    sp.dma_start(f32(mix[:, par, hl, H:DJ, 0:n]),
                                 spill["cv"][:, hl, :, c0:c0 + n].rearrange("f p t -> p f t")).then_inc(c_mix[par], 16)
                wait(sp, o_used, DJ * (tg - 1))
                sp.dma_start(xr[:, par, :, 0:n], a["xT"][:, :, c0:c0 + n]).then_inc(c_x[par], 16)

            def load_wo(n):
                wait(sp, c_wlo, n - 1)
                sp.dma_start(worw[:, n % 2], a["w_out"][n]).then_inc(c_raw[n % 2], 16)

            load_wo(0)
            load_wo(1)
            loads(0)
            for n in range(2, DJ):
                load_wo(n)
            for tg in range(NG):
                if tg + 1 < NG:
                    loads(tg + 1)
                c0, n = GROUPS[tg]
                for o in range(DJ):
                    sp.wait_ge(o_used, DJ * tg + o + 1)
                    sp.dma_start(a["y"][o, :, c0:c0 + n], yo[:, o % 4, 0:n]).then_inc(o_st[o % 4], 16)
            for i in range(4):
                sp.wait_ge(o_st[i], 16 * 2 * NG)

        @block.gpsimd
        def _(pool):
            pool.memset(eps[:], EPS).then_inc(zr_ready, 1)
            pool.memset(lamc[:, 0:1], 1.0).then_inc(p_t1, 1)
            pool.wait_ge(s_rope, 16)
            with pool.Fori(0, H) as h:
                for u in range(QK_UNITS):
                    c0, n = GROUPS[u % NG]
                    k = QK_UNITS * h + u
                    if u == NG:
                        pool.wait_ge(aux_stored, 16 * (h + 2))
                    pool.wait_ge(z_used, QK0 + k + 1)
                    pool.wait_ge(lo_ready, 2 + k)
                    pool.tensor_tensor(qt1[:, 0:n], qzn[:, 0:n], cosT[:, c0:c0 + n], ALU.mult).then_inc(p_t1, 1)
                    pool.wait_ge(sh_ready, k + 1)
                    pool.tensor_tensor(qt2[:, 0:n], qt2[:, 0:n], sinT[:, c0:c0 + n], ALU.mult).then_inc(p_t2, 1)
                    pool.wait_ge(p_t1, 1 + k + 1)
                    pool.wait_ge(p_t2, k + 1)
                    pool.tensor_tensor(qt1[:, 0:n], qt1[:, 0:n], qt2[:, 0:n], ALU.add).then_inc(zr_ready, 1)

            def bc(x):
                return x.rearrange("p (m o) -> p m o", o=1).to_broadcast([P, 2, 3])

            def three(x):
                return x.rearrange("p (m c) -> p m c", m=2)

            def factors(n, b):
                pool.wait_ge(f_done, n + 1)
                pool.tensor_tensor(stt[:, b, 4, :], stt[:, b, 3, :], stt[:, b, 1, :], ALU.mult).then_inc(fz_done, 1)
                pool.wait_ge(rden_done, n + 1)
                pool.tensor_tensor(stt[:, b, 6, 2:4], stt[:, b, 6, 0:2], lamc[:, :], ALU.mult).then_inc(rl_done, 1)
                pool.wait_ge(rl_done, n + 1)
                pool.tensor_tensor(three(stt[:, b, 7, :]), three(stt[:, b, 3, :]), bc(stt[:, b, 6, 2:4]), ALU.mult)\
                    .then_inc(coef_done, 1)
                pool.wait_ge(coef_done, n + 1)
                for c, (k0, k1) in enumerate(PIECES):
                    pool.tensor_tensor(e1[:, b, k0:k1], e1[:, b, k0:k1],
                                       stt[:, b, 7, 3 + c:4 + c].to_broadcast([P, k1 - k0]), ALU.mult)\
                        .then_inc(e1_done, 1)

            def diffs(n, b):
                pool.wait_ge(gm_done, n + 1)
                pool.tensor_tensor(three(stt[:, b, 2, :]), bc(stt[:, b, 5, 2:4]), three(stt[:, b, 0, :]), ALU.subtract)\
                    .then_inc(d_done, 1)

            for t in range(4):
                diffs(t, t % 2)
                factors(t, t % 2)
            with pool.Fori(1, ITS) as it:
                for t in range(4):
                    diffs(4 * it + t, t % 2)
                    factors(4 * it + t, t % 2)

        @block.tensor
        def _(pe):
            def sums(k, n, lhsT, parts, bank):
                pe.wait_ge(sq_ready, k + 1)
                wait(pe, std_ready, k - 1)
                for j, part in enumerate(parts):
                    mm = pe.matmul(ps[:, bank, 0:n], lhsT, part, start=(j == 0), stop=(j == len(parts) - 1))
                mm.then_inc(sum_mm, 1)

            def passes(out, slot_of, rhs_of):
                todo = [(0, 0), (0, 1), (1, 0)]
                for i, (l, r) in enumerate((l, r) for _ in range(1) for l, r in todo):
                    for j in range(DJ):
                        mm = pe.matmul(out, slot_of(l, j), rhs_of(r, j),
                                       start=(i == 0 and j == 0), stop=(i == 2 and j == DJ - 1))
                mm.then_inc(z_mm, 1)

            pe.wait_ge(s_const, 48)
            sums(0, XG, ones, [xsq[:, j, :] for j in range(DJ)], 5)
            pe.wait_ge(sc_ready, 1)
            for hf in range(6):
                pe.wait_ge(s_wada[hf % 2], 16 * (hf // 2 + 1))
                for i in range(4):
                    for j in range(DJ):
                        mm = pe.matmul(ps[:, 7, 2 * (4 * hf + i):2 * (4 * hf + i) + 2], wad[:, hf % 2, i, j], sc[:, j],
                                       start=(j == 0), stop=(j == DJ - 1))
                mm.then_inc(mod_mm, 1)
            for g in range(XN):
                if g + 1 < XN:
                    n = XGROUPS[g + 1][1]
                    sums(g + 1, n, ones, [xsq[:, j, 0:n] for j in range(DJ)], 5 + (g + 1) % 2)
                pe.wait_ge(hlo_ready, g + 1)
                if g == 0:
                    pe.wait_ge(w_lo, 4)
                for t in range(2 * g, min(2 * g + 2, TILES)):
                    wait(pe, z_used, t - 4)
                    passes(ps[:, t % BANKS, :], lambda l, j: hT[:, l, j, t * P:(t + 1) * P],
                           lambda r, j: w[:, 0:4, r, j, :])

            with pe.Fori(0, H) as h:
                for u in range(QK_UNITS):
                    c0, n = GROUPS[u % NG]
                    k = QK_UNITS * h + u
                    if u % NG == 0:
                        pe.wait_ge(w_lo, QKC + 2 * h + u // NG + 1)
                    pe.wait_ge(z_used, QK0 + k - 4)
                    passes(ps[:, (QK0 + u) % BANKS, 0:n], lambda l, j: w[:, 4 if u < NG else 0, l, j, :],
                           lambda r, j: hT[:, r, j, c0:c0 + n])
                    if u > 0:
                        m = GROUPS[(u - 1) % NG][1]
                        sums(XN + k - 1, m, blk, [qsq[:, 0:m]], 5 + (XN + u - 1) % 2)
                m = GROUPS[NG - 1][1]
                sums(XN + QK_UNITS * h + QK_UNITS - 1, m, blk, [qsq[:, 0:m]], 5 + (XN + QK_UNITS - 1) % 2)

            with pe.Fori(0, H) as f:
                for tg in range(NG):
                    c0, n = GROUPS[tg]
                    for s in range(CV):
                        if tg == 0:
                            pe.wait_ge(w_lo, CVC + CV * f + s + 1)
                        pe.wait_ge(z_used, CV0 + CV_UNITS * f + CV * tg + s - 4)
                        passes(ps[:, (CV0 + s) % BANKS, 0:n], lambda l, j: w[:, CV_SLOT[s], l, j, :],
                               lambda r, j: hT[:, r, j, c0:c0 + n])

            pe.wait_ge(s_p, 16 * (6 * H + 1))
            for m in range(2 * H):
                for ver in range(2):
                    mm = pe.matmul(ps[:, m // 4, (m % 4) * P:(m % 4 + 1) * P], qp[:, ver, m], kp[:, m],
                                   start=(ver == 0), stop=(ver == 1))
            mm.then_inc(pr_mm, 1)
            pe.wait_ge(pr_v, 7)
            for h in range(H):
                mm = pe.transpose(ps[:, 5, h * P:(h + 1) * P], e0[:, 0, h * P:(h + 1) * P], ident)
            mm.then_inc(pr_mm, 1)
            pe.wait_ge(pr_v, 8)
            for h in range(H):
                for i, (l, r) in enumerate(((0, 0), (0, 1), (1, 0))):
                    mm = pe.matmul(ps[:, 7, h * P:(h + 1) * P], vp[:, h, l], at[:, 1, r, h, 0:P],
                                   start=(i == 0), stop=(i == 2))
            mm.then_inc(pr_mm, 1)
            pe.wait_ge(pr_a, 3)

            def transposes(n, t, g):
                j0, cnt = TGROUPS[g]
                if g == 0:
                    pe.wait_ge(a_ready, 3 * (n + 1))
                wait(pe, t_lo, 5 * n + g - 1 if g in (2, 3) else 5 * n if g == 4 else 5 * (n - 1) + g + 3)
                for i in range(cnt):
                    mm = pe.transpose(trbank(g)[:, i * P:(i + 1) * P], e0[:, t, (j0 + i) * P:(j0 + i + 1) * P], ident)
                mm.then_inc(t_mm, 1)

            def product(b, half, part):
                js = (range(0, 9), range(9, KT))[half]
                todo = [(j, l, r) for j in js for l, r in ((0, 0), (0, 1), (1, 0))]
                cut = [0] + [len(todo) * i // 3 for i in range(4)] if half == 0 else [len(todo) * i // 4 for i in range(5)]
                for i in range(cut[part], cut[part + 1]):
                    j, l, r = todo[i]
                    mm = pe.matmul(ps[:, 7, b * 2 * P:(b + 1) * 2 * P], vb[:, j, l], at[:, b, r, j, :],
                                   start=(half == 0 and i == 0), stop=(half == 1 and i == len(todo) - 1))
                if part == 3:
                    mm.then_inc(pv_mm, 1)

            def scores(it, t, out, m, k0, k1):
                for ver in range(2):
                    for c0 in range(k0, k1, N):
                        c1 = min(c0 + N, k1)
                        keys = kb[:, 0, m, c0:c1] if isinstance(it, int) else \
                            kb[:, bass.ds((it // 4) % 2, 1), m, c0:c1].rearrange("p o t -> p (o t)")
                        mm = pe.matmul(out[:, c0 - k0:c1 - k0], qb[:, t, ver, m], keys, start=(ver == 0), stop=(ver == 1))
                return mm

            def step(it, t, sc=True, tr=True, pv=True):
                n = 4 * it + t
                for p in range(4):
                    if sc:
                        if p == 0:
                            pe.wait_ge(s_q[t], 64 * (it + 1))
                            if t == 0:
                                pe.wait_ge(s_k, 32 * (it // 4 + 1))
                        wait(pe, exp_done, 4 * n + p - 1)
                        pair = ps[:, 2 * (p % 2):2 * (p % 2) + 2, :].rearrange("p c n -> p (c n)")
                        scores(it, t, pair, p // 2, *PIECES[p % 2]).then_inc(s_pair, 1)
                    if pv:
                        half = 1 - t % 2
                        b = 0 if t in (1, 2) else 1
                        if p == 1 - half:
                            pe.wait_ge(s_v[half], 16 * ((it + (2 if t == 0 else 3)) // 4))
                            if half == 0:
                                pe.wait_ge(t_lo, 5 * (n - 4) + 3)
                                wait(pe, att_evac, 2 * it - (2 if t == 1 else 1))
                            else:
                                pe.wait_ge(t_lo, 5 * (n - 4))
                        product(b, half, p)
                    if tr:
                        transposes(n - S_TR, (t - S_TR) % 4, p)
                    if sc and p == 1:
                        wait(pe, expc_done, n)
                        wait(pe, t_lo, 5 * (n - S_TR))
                        scores(it, t, ps[:, 4, 0:P], 0, SAMPLE, KEYS)
                        scores(it, t, ps[:, 4, P:2 * P], 1, SAMPLE, KEYS).then_inc(s_ctx, 1)
                    if tr and p == 3:
                        if sc:
                            pe.wait_ge(expc_done, n + 1)
                        transposes(n - S_TR, (t - S_TR) % 4, 4)

            for it in range(2):
                for t in range(4):
                    n = 4 * it + t
                    step(it, t, tr=n >= S_TR, pv=n >= S_PV)
            with pe.Fori(2, ITS) as it:
                for t in range(4):
                    step(it, t)
            for n in range(NT, NT + S_PV):
                step(n // 4, n % 4, sc=False, tr=n < NT + S_TR)

            def csums(k, n):
                pe.wait_ge(c_sq, k + 1)
                wait(pe, c_std, k - 1)
                pe.matmul(ps[:, 6 + k % 2, 0:n], ones, csq[:, 0:n], start=True, stop=True).then_inc(c_sum, 1)

            for h in range(H):
                csums(h, GROUPS[0][1])
            for tg in range(NG):
                c0, n = GROUPS[tg]
                for o in range(DJ):
                    k = DJ * tg + o
                    if tg == 0:
                        pe.wait_ge(c_wlo, o + 1)
                    if o == 0:
                        pe.wait_ge(c_mix[tg % 2], 32 * (tg // 2 + 1))
                    wait(pe, o_used, k - 3)
                    for half, js in ((0, range(H, DJ)), (1, range(H))):
                        if o == 0 and half == 1:
                            pe.wait_ge(c_lo, H * (tg + 1))
                        for i, (l, r) in enumerate(((0, 0), (0, 1), (1, 0))):
                            for j in js:
                                mm = pe.matmul(ps[:, k % 4, 0:n], wo[:, l, o, j], mix[:, tg % 2, r, j, 0:n],
                                               start=(half == 0 and i == 0 and j == H),
                                               stop=(half == 1 and i == 2 and j == H - 1))
                    mm.then_inc(o_mm, 1)
                    if o % 2 and tg + 1 < NG:
                        csums(H * (tg + 1) + o // 2, GROUPS[tg + 1][1])

        @block.scalar
        def _(act):
            act.wait_ge(s_const, 48)
            act.activation(sc[:].rearrange("p j v -> p (j v)"), c_in, ACT.Silu).then_inc(sc_ready, 1)
            act.wait_ge(lam_ch, 2)
            act.activation(lamt[:, 2:4], lamt[:, 0:2], ACT.Exp).then_inc(lam_e, 1)
            act.wait_ge(s_craw, 16)
            act.activation(r32(vhi), vraw, ACT.Copy).then_inc(hi_ready, 1)

            def w_split(c, buf, slot, ordinal):
                act.wait_ge(s_raw[buf], 16 * (ordinal + 1))
                act.activation(w[:, slot, 0], raw[:, buf], ACT.Copy).then_inc(w_hi, 1)

            def v_hi(t):
                act.wait_ge(z_mm, t + 1)
                act.wait_ge(stored, 32 * (2 + t))
                act.activation(r32(vhi), ps[:, t % BANKS, :], ACT.Copy).then_inc(hi_ready, 1)

            def x_square(g):
                n = XGROUPS[g][1]
                act.wait_ge(s_x[g % 2], 16 * (g // 2 + 1))
                wait(act, sum_mm, g)
                if g == 0:
                    act.wait_ge(lo_ready, 2)
                act.activation(xsq[:, :, 0:n], xs[:, g % 2, :, 0:n], ACT.Square).then_inc(sq_ready, 1)

            act.wait_ge(s_craw, 32)
            act.wait_ge(stored, 32)
            act.activation(r32(vhi), vraw, ACT.Copy).then_inc(hi_ready, 1)
            x_square(0)
            for g in range(XN):
                c0, n = XGROUPS[g]
                v = 0 if c0 < SAMPLE else 1
                act.wait_ge(sum_mm, g + 1)
                wait(act, rstd_ready, g)
                if g == 0:
                    act.wait_ge(zr_ready, 1)
                act.activation(xstd[:, 0:n], ps[:, 5 + g % 2, 0:n], ACT.Sqrt, scale=1.0 / D, bias=eps[:])\
                    .then_inc(std_ready, 1)
                if g + 1 < XN:
                    x_square(g + 1)
                if g == 0:
                    act.wait_ge(mod_mm, 6)
                    for c in range(4):
                        w_split(c, c % 2, c, c // 2)
                if g == 1:
                    w_split(4, 0, 4, 2)
                act.wait_ge(xn_ready, g + 1)
                if g == 0:
                    act.wait_ge(mod_ch, 3)
                for j in range(DJ):
                    hm = act.activation(xs[:, g % 2, j, 0:n], xs[:, g % 2, j, 0:n], ACT.Identity,
                                        scale=mult[:, j, v:v + 1], bias=mod[:, j, v:v + 1])
                hm.then_inc(h32_ready, 1)
                for t in range(max(0, 2 * g - 2), 2 * g):
                    v_hi(t)
            v_hi(TILES - 1)

            act.wait_ge(s_rope, 16)
            act.wait_ge(stored, 32 * (2 + V_UNITS))
            with act.Fori(0, H) as h:
                for u in range(QK_UNITS + 2):
                    k = QK_UNITS * h + u
                    if u < QK_UNITS:
                        n = GROUPS[u % NG][1]
                        act.wait_ge(z_mm, QK0 + k + 1)
                        act.wait_ge(sum_mm, XN + k)
                        act.activation(qsq[:, 0:n], ps[:, (QK0 + u) % BANKS, 0:n], ACT.Square).then_inc(sq_ready, 1)
                    if 1 <= u <= QK_UNITS:
                        n = GROUPS[(u - 1) % NG][1]
                        act.wait_ge(sum_mm, XN + k)
                        act.wait_ge(z_used, QK0 + k - 1)
                        act.activation(qrs[:, 0:n], ps[:, 5 + (XN + u - 1) % 2, 0:n], ACT.Sqrt,
                                       scale=1.0 / HD, bias=eps[:]).then_inc(std_ready, 1)
                    if u == 1:
                        act.wait_ge(z_mm, QK0 + QK_UNITS * h)
                        w_split(QKC + 2 * h + 1, 1, 0, 2 + h)
                    if u == 6:
                        act.wait_ge(z_mm, QK0 + QK_UNITS * h + NG)
                        w_split(QKC + 2 * h + 2, 0, 4, 3 + h)
                    if u >= 2:
                        n = GROUPS[(u - 2) % NG][1]
                        act.wait_ge(zr_ready, 1 + k - 1)
                        act.wait_ge(stored, 32 * (2 + V_UNITS) + 32 * (k - 2))
                        act.activation(r32(qhi[:, 0:n]), qt1[:, 0:n], ACT.Copy).then_inc(hi_ready, 1)

            act.wait_ge(lo_ready, 2 + H * QK_UNITS)

            def conv(f, last):
                for s in range(1, CV):
                    act.wait_ge(z_mm, CV0 + CV_UNITS * f - 4 + s)
                    w_split(0, CV_RAW[s], CV_SLOT[s], {1: 6 + 2 * f, 2: 7 + 3 * f, 3: 7 + 2 * f, 4: 8 + 3 * f}[s])
                for tg in range(NG):
                    n = GROUPS[tg][1]
                    for s in range(2):
                        act.wait_ge(z_mm, CV0 + CV_UNITS * f + CV * tg + s + 1)
                        act.wait_ge(z_used, CV0 + CV_UNITS * f + CV * (tg - 1) + s + 1)
                        act.activation(sig[:, s, 0:n], ps[:, (CV0 + s) % BANKS, 0:n], ACT.Sigmoid).then_inc(sig_ready, 1)
                if not last:
                    w_split(0, 0, CV_SLOT[0], 9 + 3 * f)

            with act.Fori(0, H - 1) as f:
                conv(f, False)
            conv(H - 1, True)

            act.wait_ge(pr_v, 2)
            act.activation(e1[:, 0, 0:2 * H * P], e1[:, 0, 0:2 * H * P], ACT.Exp).then_inc(pr_a, 1)
            act.wait_ge(pr_mm, 2)
            act.activation(at[:, 1, 0, 0:H, 0:P], ps[:, 5, :].rearrange("p (h t) -> p h t", h=H), ACT.Copy)\
                .then_inc(pr_a, 1)
            act.wait_ge(pr_mm, 3)
            act.activation(atto[:].rearrange("p b t -> p (b t)"), ps[:, 7, :], ACT.Copy).then_inc(pr_a, 1)
            act.wait_ge(pr_a, 3)
            act.dma_start(spill["att"][:, :, SAMPLE:T].rearrange("h p t -> p h t"),
                          atto[:].rearrange("p b (c t) -> p (b c) t", c=2)).then_inc(aux_stored, 16)
            act.wait_ge(aux_stored, 16 * (1 + H + H * NG + 1))

            def tr_hi(n, t, g):
                j0, cnt = TGROUPS[g]
                act.wait_ge(t_mm, 5 * n + g + 1)
                if g == 0 and t % 2 == 0:
                    wait(act, pv_mm, n - 2)
                act.activation(at[:, t // 2, 0, j0:j0 + cnt, (t % 2) * P:(t % 2 + 1) * P],
                               trbank(g).rearrange("p (j q) -> p j q", j=cnt), ACT.Copy).then_inc(t_hi, 1)

            def step(it, t, sc=True, tr=True, out=True):
                n = 4 * it + t
                b = t % 2
                for p in range(4):
                    m, c = p // 2, p % 2
                    if sc and p == 3:
                        act.wait_ge(mxc_done, n + 1)
                        wait(act, a_ready, 3 * (n - 1))
                        for mc in range(2):
                            dst = e0[:, t] if mc == 0 else e1[:, b]
                            em = act.activation(dst[:, SAMPLE:KEYS], ps[:, 4, mc * P:(mc + 1) * P], ACT.Exp,
                                                bias=stt[:, b, 0, 3 * mc + 2:3 * mc + 3],
                                                accum_out=stt[:, b, 1, 3 * mc + 2:3 * mc + 3])
                        em.then_inc(expc_done, 1)
                    if sc:
                        act.wait_ge(mx_done, 4 * n + p + 1)
                        if p == 0:
                            wait(act, t_mm, 5 * (n - 3))
                        if p == 2:
                            wait(act, a_ready, 3 * (n - 1) - 2)
                        dst = e0[:, t] if m == 0 else e1[:, b]
                        act.activation(dst[:, c * 1024:(c + 1) * 1024],
                                       ps[:, 2 * c:2 * c + 2, :].rearrange("p c n -> p (c n)"), ACT.Exp,
                                       bias=stt[:, b, 0, 3 * m + c:3 * m + c + 1],
                                       accum_out=stt[:, b, 1, 3 * m + c:3 * m + c + 1]).then_inc(exp_done, 1)
                    if out and p == 0:
                        pb = 1 if t == 1 else 0
                        pair = 2 * it - (3 if t == 1 else 2)
                        act.wait_ge(pv_mm, n - S_PV)
                        wait(act, att_stored[pb], 16 * (it - (2 if t == 1 else 1)))
                        act.activation(atto[:, pb], ps[:, 7, pb * 2 * P:(pb + 1) * 2 * P], ACT.Copy).then_inc(att_evac, 1)
                        act.wait_ge(att_evac, pair + 1)
                        u = it - (2 if t == 1 else 1)
                        q0 = (u % 4) * (4 * P) + pb * 2 * P
                        if isinstance(it, int):
                            dst = spill["att"][u // 4, :, q0:q0 + 2 * P]
                        else:
                            dst = spill["att"][bass.ds(u // 4, 1), :, bass.ds(q0, 2 * P)].rearrange("o p t -> (o p) t")
                        act.dma_start(dst, atto[:, pb]).then_inc(att_stored[pb], 16)
                    if tr:
                        tr_hi(n - S_TR, (t - S_TR) % 4, p)
                        if p == 3:
                            tr_hi(n - S_TR, (t - S_TR) % 4, 4)
                if sc:
                    act.wait_ge(d_done, n + 1)
                    act.activation(stt[:, b, 3, :], stt[:, b, 2, :], ACT.Exp).then_inc(f_done, 1)

            for it in range(3):
                for t in range(4):
                    n = 4 * it + t
                    step(it, t, tr=n >= S_TR, out=n >= S_OUT and t % 2 == 1)
            with act.Fori(3, ITS) as it:
                for t in range(4):
                    step(it, t, out=t % 2 == 1)
            for n in range(NT, NT + S_OUT - 1):
                step(n // 4, n % 4, sc=False, tr=n < NT + S_TR, out=n % 2 == 1)

            def wo_hi(n):
                act.wait_ge(c_raw[n % 2], 16 * (n // 2 + 1))
                act.activation(wo[:, 0, n], worw[:, n % 2], ACT.Copy).then_inc(c_whi, 1)

            def norm(tg, h):
                n = GROUPS[tg][1]
                k = H * tg + h
                if h == 0:
                    act.wait_ge(c_at, 32 * (tg + 1))
                wait(act, c_sum, k)
                act.activation(csq[:, 0:n], atr[:, h, 0:n], ACT.Square).then_inc(c_sq, 1)
                act.wait_ge(c_sum, k + 1)
                wait(act, c_rs, k)
                act.activation(cstd[:, 0:n], ps[:, 6 + k % 2, 0:n], ACT.Sqrt, scale=1.0 / P, bias=eps[:])\
                    .then_inc(c_std, 1)
                act.wait_ge(c_y2, k + 1)
                wait(act, o_mm, DJ * (tg - 1))
                act.activation(mix[:, tg % 2, 0, h, 0:n], cy[:, 0:n], ACT.Copy).then_inc(c_hi, 1)

            wo_hi(0)
            wo_hi(1)
            for h in range(H):
                norm(0, h)
                wo_hi(2 + h)
            wo_hi(6)
            wo_hi(7)
            for tg in range(1, NG):
                for h in range(H):
                    norm(tg, h)

        @block.vector
        def _(dve):
            dve.wait_ge(s_const, 48)
            for i in range(2):
                dve.tensor_tensor_reduce(lamj[:, i], lamv[:, 2 * i], lamv[:, 2 * i + 1], 1.0, 0.0, ALU.mult, ALU.add,
                                         lamt[:, i:i + 1]).then_inc(lam_ch, 1)
            dve.tensor_scalar(sublns[:], subln, 1.0 - LAM_INIT, None, ALU.mult).then_inc(lam_ch, 1)
            dve.tensor_scalar(qks[:, 0:1], qk_w[:, 0:1], HD ** -0.5, None, ALU.mult).then_inc(lam_ch, 1)
            dve.tensor_copy(qks[:, 1:2], qk_w[:, 1:2]).then_inc(lam_ch, 1)
            dve.wait_ge(lam_e, 1)
            dve.tensor_tensor(lamt[:, 4:5], lamt[:, 3:4], lamt[:, 2:3], ALU.subtract).then_inc(lam_ch, 1)
            dve.wait_ge(lam_ch, 6)
            dve.tensor_scalar(lamc[:, 1:2], lamt[:, 4:5], -LAM_INIT, None, ALU.add).then_inc(lam_ch, 1)

            def cache_lo(i):
                dve.wait_ge(hi_ready, i + 1)
                dve.tensor_tensor(r32(vlo), vraw, vhi, ALU.subtract).then_inc(lo_ready, 1)

            cache_lo(0)
            cache_lo(1)

            def w_split(c, buf, slot):
                dve.wait_ge(w_hi, c + 1)
                dve.tensor_tensor(w[:, slot, 1], raw[:, buf], f32(w[:, slot, 0]), ALU.subtract).then_inc(w_lo, 1)

            def v_lo(t):
                dve.wait_ge(hi_ready, 2 + t + 1)
                dve.tensor_tensor(r32(vlo), ps[:, t % BANKS, :], vhi, ALU.subtract).then_inc(z_used, 1)

            for g in range(XN):
                n = XGROUPS[g][1]
                if g == 0:
                    dve.wait_ge(s_x[0], 16)
                dve.wait_ge(std_ready, g + 1)
                wait(dve, xn_ready, g)
                dve.reciprocal(xrstd[:, 0:n], xstd[:, 0:n]).then_inc(rstd_ready, 1)
                dve.wait_ge(rstd_ready, g + 1)
                x = xs[:, g % 2, :, 0:n]
                dve.tensor_tensor(x, x, xrstd[:, 0:n].rearrange("p (o t) -> p o t", o=1).to_broadcast([P, DJ, n]),
                                  ALU.mult).then_inc(xn_ready, 1)
                if g == 0:
                    dve.wait_ge(mod_mm, 6)
                    dve.tensor_tensor(mod[:], ps[:, 7, 0:48].rearrange("p (n v) -> p n v", v=2),
                                      b_ada.rearrange("p (n o) -> p n o", o=1).to_broadcast([P, 24, 2]), ALU.add)\
                        .then_inc(mod_ch, 1)
                    dve.wait_ge(mod_ch, 1)
                    dve.tensor_scalar(mult[:], mod[:, 8:16], 1.0, None, ALU.add).then_inc(mod_ch, 1)
                    dve.wait_ge(mod_ch, 2)
                    dve.tensor_tensor(mult[:], mult[:], norm_w.rearrange("p (n o) -> p n o", o=1).to_broadcast([P, DJ, 2]),
                                      ALU.mult).then_inc(mod_ch, 1)
                    for c in range(4):
                        w_split(c, c % 2, c)
                if g == 1:
                    w_split(4, 0, 4)
                dve.wait_ge(h32_ready, g + 1)
                c0 = XGROUPS[g][0]
                dve.tensor_copy(hT[:, 0, :, c0:c0 + n], x).then_inc(hhi_ready, 1)
                dve.wait_ge(hhi_ready, g + 1)
                dve.tensor_tensor(hT[:, 1, :, c0:c0 + n], x, f32(hT[:, 0, :, c0:c0 + n]), ALU.subtract)\
                    .then_inc(hlo_ready, 1)
                for t in range(max(0, 2 * g - 2), 2 * g):
                    v_lo(t)
            dve.wait_ge(z_mm, TILES)
            dve.wait_ge(hi_ready, 2 + TILES)
            dve.wait_ge(sum_mm, XN)
            dve.tensor_copy(vraw, ps[:, (TILES - 1) % BANKS, :]).then_inc(nv_ready, 1)
            v_lo(TILES - 1)

            dve.wait_ge(s_rope, 16)
            dve.wait_ge(lam_ch, 7)
            dve.wait_ge(stored, 32 * (2 + V_UNITS))
            with dve.Fori(0, H) as h:
                for u in range(QK_UNITS + 1):
                    k = QK_UNITS * h + u
                    if u < QK_UNITS:
                        n = GROUPS[u % NG][1]
                        comp = 1 - u // NG
                        dve.wait_ge(std_ready, XN + k + 1)
                        dve.reciprocal(qrs[:, 0:n], qrs[:, 0:n]).then_inc(rstd_ready, 1)
                        dve.wait_ge(rstd_ready, XN + k + 1)
                        dve.wait_ge(p_t1, 1 + k)
                        dve.scalar_tensor_tensor(qzn[:, 0:n], ps[:, (QK0 + u) % BANKS, 0:n], qks[:, comp:comp + 1],
                                                 qrs[:, 0:n], ALU.mult, ALU.mult).then_inc(z_used, 1)
                        dve.wait_ge(zr_ready, 1 + k)
                        dve.wait_ge(z_used, QK0 + k + 1)
                        dve.tensor_copy(tick[:], eps[:])
                        dve.stream_shuffle(qt2[:, 0:n], qzn[:, 0:n], [i ^ 16 for i in range(32)]).then_inc(sh_ready, 1)
                    if u == 1:
                        w_split(QKC + 2 * h + 1, 1, 0)
                    if u == 6:
                        w_split(QKC + 2 * h + 2, 0, 4)
                    if u > 0:
                        n = GROUPS[(u - 1) % NG][1]
                        dve.wait_ge(hi_ready, 2 + V_UNITS + k)
                        dve.tensor_tensor(r32(qlo[:, 0:n]), qt1[:, 0:n], qhi[:, 0:n], ALU.subtract).then_inc(lo_ready, 1)

            dve.wait_ge(stored, 32 * (2 + V_UNITS + H * QK_UNITS))
            dve.wait_ge(lo_ready, 2 + H * QK_UNITS)
            for i, z in enumerate((ub[:, 0:1], ub[:, SAMPLE + 1:SAMPLE + 2], up[:, 0:1], up[:, PROMPT + 1:PROMPT + 2])):
                dve.memset(z, 0.0).then_inc(cvc, 1)
            dve.wait_ge(cvc, 4)

            def conv_group(f, tg):
                seq, o, n = useq(tg)
                c0 = GROUPS[tg][0]
                base = 4 + 6 * (NG * f + tg)

                def wcol(i):
                    return cw[:, i:i + 1]

                dve.wait_ge(cvc, base)
                dve.tensor_scalar(cc_[:, 0:n], seq[:, o:o + n], wcol(0), wcol(3), ALU.mult, ALU.add).then_inc(cvc, 1)
                for i in (1, 2):
                    dve.wait_ge(cvc, base + i)
                    dve.scalar_tensor_tensor(cc_[:, 0:n], seq[:, o + i:o + i + n], wcol(i), cc_[:, 0:n],
                                             ALU.mult, ALU.add).then_inc(cvc, 1)
                dve.wait_ge(cvc, base + 3)
                dve.tensor_tensor(cc_[:, 0:n], cc_[:, 0:n], gcb[:, c0:c0 + n], ALU.mult).then_inc(cvc, 1)
                dve.wait_ge(cvc, base + 4)
                dve.wait_ge(stored, 32 * (2 + V_UNITS + H * QK_UNITS) + 32 * (NG * f + tg))
                dve.tensor_copy(r32(chi[:, 0:n]), cc_[:, 0:n]).then_inc(cvc, 1)
                dve.wait_ge(cvc, base + 5)
                dve.tensor_tensor(r32(clo[:, 0:n]), cc_[:, 0:n], chi[:, 0:n], ALU.subtract).then_inc(cvc, 1)

            def conv(f, last):
                dve.wait_ge(cvc, 4 + 6 * NG * f)
                dve.tensor_copy(cw[:, 0:4], taps[:, bass.ds(4 * f, 4)]).then_inc(tapped, 1)
                for s in range(1, CV):
                    w_split(CVC + CV * f + s, CV_RAW[s], CV_SLOT[s])
                for tg in range(NG):
                    c0, n = GROUPS[tg]
                    z0 = CV0 + CV_UNITS * f + CV * tg
                    z = [ps[:, (CV0 + s) % BANKS, 0:n] for s in range(CV)]
                    dve.wait_ge(sig_ready, 2 * (NG * f + tg) + 1)
                    dve.wait_ge(aux_stored, 16 * (1 + H) + 16 * (NG * f + tg))
                    dve.tensor_tensor(gs[:, 0:n], z[0], sig[:, 0, 0:n], ALU.mult).then_inc(z_used, 1)
                    dve.wait_ge(sig_ready, 2 * (NG * f + tg) + 2)
                    g = gcb[:, c0:c0 + n]
                    dve.tensor_tensor(g, z[1], sig[:, 1, 0:n], ALU.mult).then_inc(z_used, 1)
                    dve.wait_ge(z_mm, z0 + 3)
                    dve.wait_ge(z_used, z0 + 2)
                    dve.tensor_tensor(g, z[2], g, ALU.mult).then_inc(z_used, 1)
                    dve.wait_ge(z_mm, z0 + 4)
                    dve.tensor_copy(ccs[:, 0:n], z[3]).then_inc(z_used, 1)
                    dve.wait_ge(z_mm, z0 + 5)
                    dve.wait_ge(z_used, z0 + 4)
                    seq, o, _ = useq(tg)
                    dve.tensor_tensor(seq[:, o + 1:o + 1 + n], z[4], ccs[:, 0:n], ALU.mult).then_inc(z_used, 1)
                    dve.wait_ge(z_used, z0 + 5)
                    if tg == 1:
                        dve.wait_ge(tapped, f + 1)
                    for tc in ([] if tg == 0 else [tg - 1] if tg < TG else [TG - 1, TG]):
                        conv_group(f, tc)
                if not last:
                    w_split(CVC + CV * f + CV, 0, CV_SLOT[0])

            with dve.Fori(0, H - 1) as f:
                conv(f, False)
            conv(H - 1, True)

            def maps(x):
                return x.rearrange("p (m t) -> p m t", m=2 * H)

            def wide(x):
                return x.rearrange("p (m o) -> p m o", o=1).to_broadcast([P, 2 * H, P])

            scores_p = maps(ps[:, 0:2, :].rearrange("p c n -> p (c n)"))
            ep = e1[:, 0, 0:2 * H * P]
            dve.wait_ge(pr_mm, 1)
            dve.tensor_reduce(stp[:, 0], scores_p, AX.X, ALU.max).then_inc(pr_v, 1)
            dve.wait_ge(pr_v, 1)
            dve.tensor_tensor(maps(ep), scores_p, wide(stp[:, 0]), ALU.subtract).then_inc(pr_v, 1)
            dve.wait_ge(pr_a, 1)
            dve.tensor_reduce(stp[:, 1], maps(ep), AX.X, ALU.add).then_inc(pr_v, 1)
            dve.wait_ge(pr_v, 3)
            dve.reciprocal(stp[:, 2], stp[:, 1]).then_inc(pr_v, 1)
            dve.wait_ge(pr_v, 4)
            dve.tensor_tensor(stp[:, 3].rearrange("p (h m) -> p h m", m=2), stp[:, 2].rearrange("p (h m) -> p h m", m=2),
                              lamc[:].rearrange("p (o m) -> p o m", o=1).to_broadcast([P, H, 2]), ALU.mult)\
                .then_inc(pr_v, 1)
            dve.wait_ge(pr_v, 5)
            dve.tensor_tensor(maps(ep), maps(ep), wide(stp[:, 3]), ALU.mult).then_inc(pr_v, 1)
            dve.wait_ge(pr_v, 6)
            eh = ep.rearrange("p (h m t) -> p h m t", h=H, m=2)
            dve.tensor_tensor(e0[:, 0, 0:H * P].rearrange("p (h t) -> p h t", h=H), eh[:, :, 0], eh[:, :, 1], ALU.add)\
                .then_inc(pr_v, 1)
            dve.wait_ge(pr_a, 2)
            dve.tensor_tensor(at[:, 1, 1, 0:H, 0:P], ps[:, 5, :].rearrange("p (h t) -> p h t", h=H),
                              f32(at[:, 1, 0, 0:H, 0:P]), ALU.subtract).then_inc(pr_v, 1)

            def tr_lo(n, t, g):
                j0, cnt = TGROUPS[g]
                dve.wait_ge(t_hi, 5 * n + g + 1)
                cols = slice((t % 2) * P, (t % 2 + 1) * P)
                dve.tensor_tensor(at[:, t // 2, 1, j0:j0 + cnt, cols], trbank(g).rearrange("p (j q) -> p j q", j=cnt),
                                  f32(at[:, t // 2, 0, j0:j0 + cnt, cols]), ALU.subtract).then_inc(t_lo, 1)

            def combine(n, t, c):
                k0, k1 = PIECES[c]
                dve.wait_ge(e1_done, 3 * n + c + 1)
                dve.scalar_tensor_tensor(e0[:, t, k0:k1], e0[:, t, k0:k1], stt[:, t % 2, 7, c:c + 1],
                                         e1[:, t % 2, k0:k1], ALU.mult, ALU.add).then_inc(a_ready, 1)

            def step(it, t, sc=True, den=True, comb=True, tr=True, tr_last=True):
                n = 4 * it + t
                b = t % 2
                for p in range(4):
                    m, c = p // 2, p % 2
                    if sc:
                        dve.wait_ge(s_pair, 4 * n + p + 1)
                        if p == 0:
                            wait(dve, coef_done, n - 1)
                        dve.tensor_reduce(stt[:, b, 0, 3 * m + c:3 * m + c + 1],
                                          ps[:, 2 * c:2 * c + 2, :].rearrange("p c n -> p (c n)"), AX.X, ALU.max,
                                          negate=True).then_inc(mx_done, 1)
                    if p == 0 and tr_last:
                        tr_lo(n - 1 - S_TR, (t - 1 - S_TR) % 4, 3)
                        tr_lo(n - 1 - S_TR, (t - 1 - S_TR) % 4, 4)
                    if p == 0 and den:
                        dve.wait_ge(fz_done, n)
                        dve.tensor_reduce(stt[:, 1 - b, 5, 0:2], stt[:, 1 - b, 4, :].rearrange("p (m c) -> p m c", m=2),
                                          AX.X, ALU.add).then_inc(den_done, 1)
                        dve.wait_ge(den_done, n)
                        dve.reciprocal(stt[:, 1 - b, 6, 0:2], stt[:, 1 - b, 5, 0:2]).then_inc(rden_done, 1)
                    if p == 3 and sc:
                        dve.wait_ge(mxc_done, n + 1)
                        dve.wait_ge(mx_done, 4 * n + 4)
                        dve.tensor_reduce(stt[:, b, 5, 2:4], stt[:, b, 0, :].rearrange("p (m c) -> p m c", m=2), AX.X,
                                          ALU.min).then_inc(gm_done, 1)
                    if p > 0 and tr:
                        tr_lo(n - S_TR, (t - S_TR) % 4, p - 1)
                    if p < 3 and comb:
                        combine(n - S_COMB, (t - S_COMB) % 4, p)
                    if sc and p == 2:
                        dve.wait_ge(s_ctx, n + 1)
                        dve.tensor_reduce(stt[:, b, 0, 2:6:3], ps[:, 4, 0:2 * P].rearrange("p (m k) -> p m k", m=2), AX.X,
                                          ALU.max, negate=True).then_inc(mxc_done, 1)

            for t in range(4):
                step(0, t, den=t >= 1, comb=t >= S_COMB, tr=t >= S_TR, tr_last=t > S_TR)
            with dve.Fori(1, ITS) as it:
                for t in range(4):
                    step(it, t)
            for n in range(NT, NT + S_TR + 1):
                step(n // 4, n % 4, sc=False, den=n == NT, comb=n < NT + S_COMB, tr=n < NT + S_TR)

            def wo_lo(n):
                dve.wait_ge(c_whi, n + 1)
                dve.tensor_tensor(wo[:, 1, n], worw[:, n % 2], f32(wo[:, 0, n]), ALU.subtract).then_inc(c_wlo, 1)

            def norm(tg, h):
                n = GROUPS[tg][1]
                k = H * tg + h
                dve.wait_ge(c_std, k + 1)
                dve.reciprocal(crs[:, 0:n], cstd[:, 0:n]).then_inc(c_rs, 1)
                dve.wait_ge(c_rs, k + 1)
                dve.scalar_tensor_tensor(cy[:, 0:n], atr[:, h, 0:n], sublns[:], crs[:, 0:n], ALU.mult, ALU.mult)\
                    .then_inc(c_y1, 1)
                dve.wait_ge(c_y1, k + 1)
                dve.tensor_tensor(cy[:, 0:n], cy[:, 0:n], gar[:, h, 0:n], ALU.mult).then_inc(c_y2, 1)
                dve.wait_ge(c_hi, k + 1)
                dve.tensor_tensor(mix[:, tg % 2, 1, h, 0:n], cy[:, 0:n], f32(mix[:, tg % 2, 0, h, 0:n]), ALU.subtract)\
                    .then_inc(c_lo, 1)

            wo_lo(0)
            wo_lo(1)
            for h in range(H):
                if h == 0:
                    dve.wait_ge(c_at, 32)
                norm(0, h)
                wo_lo(2 + h)
            wo_lo(6)
            wo_lo(7)
            for tg in range(NG):
                c0, n = GROUPS[tg]
                v = 0 if tg < TG else 1
                for o in range(DJ):
                    k = DJ * tg + o
                    dve.wait_ge(o_mm, k + 1)
                    if o == 0:
                        dve.wait_ge(c_x[tg % 2], 16 * (tg // 2 + 1))
                    wait(dve, o_st[o % 4], 16 * (2 * tg + o // 4))
                    dve.scalar_tensor_tensor(yo[:, o % 4, 0:n], ps[:, k % 4, 0:n], mod[:, 16 + o, v:v + 1],
                                             xr[:, tg % 2, o, 0:n], ALU.mult, ALU.add).then_inc(o_used, 1)
                    if o % 2 and tg + 1 < NG:
                        if o == 1:
                            dve.wait_ge(c_at, 32 * (tg + 2))
                        norm(tg + 1, o // 2)


def _rope_tables():
    grid_w, freqs, base = 64, HD // 4, 10000.0
    t = np.arange(SAMPLE)
    inv = (np.float32(1.0) / (np.float32(base) ** (np.arange(freqs, dtype=np.float32) / np.float32(freqs))))
    inv = inv.astype(np.float32)
    ang = np.stack([(t // grid_w).astype(np.float32)[:, None] * inv, (t % grid_w).astype(np.float32)[:, None] * inv])
    cos, sin = np.cos(ang).astype(np.float32), np.sin(ang).astype(np.float32)
    table = np.zeros((P, 2, T), np.float32)
    table[:, 0, SAMPLE:] = 1.0
    for p in range(P):
        d = p % HD
        half, lower, i = d // 32, d % 32 < 16, d % 16
        table[p, 0, :SAMPLE] = cos[half, :, i]
        table[p, 1, :SAMPLE] = -sin[half, :, i] if lower else sin[half, :, i]
    return table.reshape(P, 2 * T)


def _constants():
    blk = np.zeros((P, P), np.float32)
    blk[:HD, :HD] = blk[HD:, HD:] = 1.0
    return np.stack([np.eye(P, dtype=np.float32), np.ones((P, P), np.float32), blk], axis=1)


def kernel(**inputs):
    import concourse.bacc as _bacc
    from concourse.bass_utils import run_bass_kernel_spmd as _run

    x = {k: np.asarray(v) for k, v in inputs.items()}

    def cols(v):
        return np.ascontiguousarray(v.reshape(-1, P).T)

    tokens = np.concatenate([x["x_sample"][0], x["x_prompt"][0]], axis=0)
    xT = tokens.T.reshape(DJ, P, T).transpose(1, 0, 2)
    w_in = x["w_in"][0].reshape(DJ, P, 32, P).transpose(2, 1, 0, 3)
    q0, k0, v0, ga0, cb0, cc0, ch0, gc0 = range(0, 32, 4)
    order = [v0 + i for i in range(4)]
    for i in range(H):
        order += [k0 + i, q0 + i]
    for i in range(H):
        order += [ga0 + i, gc0 + i, cb0 + i, cc0 + i, ch0 + i]
    small = np.concatenate([
        cols(x["norm_w"][0]), np.tile(x["q_norm_w"][0], 2)[:, None], np.tile(x["k_norm_w"][0], 2)[:, None],
        x["subln_w"][0][:, None],
        np.concatenate([np.concatenate([cols(x["conv_w"][0, i])[:, f:f + 1] for i in range(3)]
                                       + [cols(x["conv_b"][0])[:, f:f + 1]], axis=1) for f in range(4)], axis=1),
        cols(x["b_ada"][0]),
        np.stack([cols(x["c"][0]), cols(x["c_ctx"])], axis=2).reshape(P, 2 * DJ)], axis=1)
    arrays = {
        "xT": xT,
        "w_ada": x["w_ada"][0].reshape(DJ, P, 24, P).transpose(2, 1, 0, 3),
        "w_in": w_in[order],
        "w_out": x["w_out"][0].reshape(DJ, P, DJ, P).transpose(2, 1, 0, 3),
        "small": small,
        "lam": np.broadcast_to(np.stack([x["lambda_q1"][0], x["lambda_k1"][0], x["lambda_q2"][0], x["lambda_k2"][0]]),
                               (P, 4, HD)),
        "cache_k": x["cache_k"][0, 0].reshape(CACHE, H, P).transpose(1, 2, 0),
        "cache_v": x["cache_v"][0, 0].reshape(CACHE, H * P),
        "rope": _rope_tables(),
        "cst": _constants(),
    }
    nc = _bacc.Bacc("TRN2", target_bir_lowering=False, num_devices=1, dynamic_dma_scratch_size=1024)
    arrays = {f"in_{k}": np.ascontiguousarray(v) for k, v in arrays.items()}
    aps = {k[3:]: nc.dram_tensor(k, v.shape, mybir.dt.from_np(v.dtype), kind="ExternalInput").ap()
           for k, v in arrays.items()}
    for name, shape in (("y", [DJ, P, T]), ("new_k", [H, P, PROMPT]), ("new_v", [P, H * P])):
        aps[name] = nc.dram_tensor(f"out_{name}", shape, F32, kind="ExternalOutput").ap()
    hymba_layer(nc, aps)
    r = _run(nc, [arrays], core_ids=[0]).results[0]
    y = np.asarray(r["out_y"]).reshape(D, T).T
    new_k = np.asarray(r["out_new_k"]).transpose(2, 0, 1).reshape(1, 1, PROMPT, H, 2, HD)
    new_v = np.asarray(r["out_new_v"]).reshape(1, 1, PROMPT, H, P)
    return (np.ascontiguousarray(y[SAMPLE:])[None], np.ascontiguousarray(y[:SAMPLE])[None],
            np.ascontiguousarray(new_k), np.ascontiguousarray(new_v))
```

```python
import math
from contextlib import ExitStack

import numpy as np
import concourse.bass as bass
from concourse import mybir

F32 = mybir.dt.float32
F32R = mybir.dt.float32r
ALU = mybir.AluOpType
ACT = mybir.ActivationFunctionType
AX = mybir.AxisListType

P = 128
D = 1024
DJ = D // P
SAMPLE, PROMPT, CACHE = 2048, 128, 128
T = SAMPLE + PROMPT
KEYS = SAMPLE + CACHE
KCOLS = KEYS + PROMPT
H = 4
HD = 64
N = 512
NG = -(-T // N)
GW = -(-T // (NG * 64)) * 64
GROUPS = [(g * GW, min(GW, T - g * GW)) for g in range(NG)]
TG = NG - 1
SPLIT = SAMPLE - GROUPS[TG][0]
XG = 256
XGROUPS = [(g * XG, XG) for g in range(SAMPLE // XG)] + [(SAMPLE, PROMPT)]
KT = KEYS // P
TILES = T // P
EPS = 1e-6
LAM_INIT = 0.8 - 0.6 * math.exp(-0.3 * 0)
BANKS = 5
QK_UNITS = 2 * NG
CV = 5
CV_UNITS = CV * NG
QT = SAMPLE // P
NORM_AT = {2: 0, 4: 1, 5: 2, 6: 3}
ITS = H * QT // 4
TGROUPS = [(0, 4), (4, 4), (8, 4), (12, 4), (16, 1)]
PIECES = [(0, 1024), (1024, SAMPLE), (SAMPLE, KEYS)]
S_COMB, S_TR, S_PV, S_OUT = 2, 3, 5, 7
NT = H * QT


def wait(eng, sem, value):
    if isinstance(value, int) and value <= 0:
        return
    eng.wait_ge(sem, value)


def hymba_layer(nc, a):
    spill = {}
    for name, shape in (("k", [H, 2, P, KCOLS]), ("q", [H, 2, P, T]), ("v", [H, P, KT + 1, 2, P]),
                        ("ga", [H, P, T]), ("cv", [H, 2, P, T]), ("att", [H, P, T])):
        spill[name] = nc.dram_tensor(f"spill_{name}", shape, F32, kind="Internal").ap()

    ctx = ExitStack()
    with ctx:
        def sb(name, shape, dt=F32, c=ctx):
            return c.enter_context(nc.sbuf_tensor(name, shape, dt))

        def sem(name):
            return ctx.enter_context(nc.semaphore(name))

        ps = ctx.enter_context(nc.psum_tensor("ps", [P, 8, N], F32))

        cst = sb("cst", [P, 3, P])
        ident, ones, blk = cst[:, 0], cst[:, 1], cst[:, 2]
        small = sb("small", [P, 67])
        norm_w, qk_w, subln = small[:, 0:8], small[:, 8:10], small[:, 10:11]
        taps, b_ada = small[:, 11:27], small[:, 27:51]
        c_in = small[:, 51:67]
        eps = sb("eps", [P, 1])
        sc = sb("sc", [P, DJ, 2])
        mod = sb("mod", [P, 24, 2])
        mult = sb("mult", [P, DJ, 2])
        lamv = sb("lamv", [P, 4, HD])
        lamj = sb("lamj", [P, 2, HD])
        lamt = sb("lamt", [P, 6])
        lamc = sb("lamc", [P, 2])
        sublns = sb("sublns", [P, 1])
        qks = sb("qks", [P, 2])
        tick = sb("tick", [P, 1])
        cw = sb("cw", [P, 4])

        with ExitStack() as actx:
            with ExitStack() as mctx:
                sb("pad", [P, 2 * DJ * T - 24 * P - 2 * DJ * P], F32, mctx)
                raw2 = sb("raw2", [P, 2, DJ, P], F32, mctx)
                modr = sb("modr", [P, 24 * P], F32, mctx)
            hT = sb("hT", [P, 2, DJ, T], F32R, actx)
            with ExitStack() as wctx:
                wad = sb("wad", [P, 2, 4, DJ, P], F32, wctx)
            with ExitStack() as qctx:
                sb("pad2", [P, 2, 2, DJ, P], F32, qctx)
                qx = sb("qx", [P, 8, N], F32, qctx)
            w = sb("w", [P, 5, 2, DJ, P], F32R, actx)
            raw = sb("raw", [P, 2, DJ, P], F32, actx)
            scr = sb("scr", [P, 8000], F32, actx)
        with ExitStack() as bctx:
            kb = sb("kb", [P, 2, 2, KEYS], F32R, bctx)
            qb = sb("qb", [P, 4, 2, 2, P], F32R, bctx)
            e1 = sb("e1", [P, 2, KEYS], F32, bctx)
            e0 = sb("e0", [P, 4, KEYS], F32, bctx)
            stt = sb("stt", [P, 2, 8, 6], F32, bctx)
            vb = sb("vb", [P, KT, 2, P], F32R, bctx)
            at = sb("at", [P, 2, 2, KT, 2 * P], F32R, bctx)
            atto = sb("atto", [P, 2, 2 * P], F32, bctx)
            stp = sb("stp", [P, 4, 2 * H], F32, bctx)
            qp = sb("qp", [P, 2, 2 * H, P], F32R, bctx)
            kp = sb("kp", [P, 2 * H, P], F32R, bctx)
            vp = sb("vp", [P, H, 2, P], F32R, bctx)
            ep = sb("ep", [P, 2 * H * P], F32, bctx)
            ap_ = sb("ap", [P, H * P], F32, bctx)
            atp = sb("atp", [P, 2, H, P], F32R, bctx)
            pro = sb("pro", [P, H * P], F32, bctx)
        with ExitStack() as cctx:
            worw = sb("worw", [P, 2, DJ, P], F32, cctx)
            atr = sb("atr", [P, H, N], F32, cctx)
            sb("pad0", [P, 2 * KEYS - 2 * DJ * P - H * N], F32, cctx)
            wo = sb("wo", [P, DJ, 2, DJ, P], F32R, cctx)
            gar = sb("gar", [P, H, N], F32, cctx)
            yo = sb("yo", [P, 4, N], F32, cctx)
            csq = sb("csq", [P, 2, N], F32, cctx)
            crs = sb("crs", [P, 2, N], F32, cctx)
            cy = sb("cy", [P, 2, N], F32, cctx)
            sb("pad1", [P, 352], F32, cctx)
            mix = sb("mix", [P, 2, 2, DJ, N], F32R, cctx)
            xr = sb("xr", [P, 2, DJ, N], F32, cctx)

        xs = scr[:, 0:4096].rearrange("p (b j t) -> p b j t", b=2, j=DJ)
        xsq = scr[:, 4096:6144].rearrange("p (j t) -> p j t", j=DJ)
        xstd, xrstd = scr[:, 6144:6400], scr[:, 6400:6656]
        vraw = scr[:, 4352:4864]
        vhi, vlo = scr[:, 6656:7168], scr[:, 7168:7680]
        cosT, sinT = scr[:, 0:T], scr[:, T:2 * T]
        qsq, qhi, qlo = ([scr[:, 2 * T + (2 * i + b) * N:2 * T + (2 * i + b + 1) * N] for b in range(2)] for i in range(3))
        qrs, qzn, qt1, qt2 = ([qx[:, 2 * i + b] for b in range(2)] for i in range(4))
        sig = scr[:, 0:2 * N].rearrange("p (b n) -> p b n", b=2)
        gs, ccs, cc_, chi, clo = (scr[:, i * N:(i + 1) * N] for i in range(2, 7))
        ub = scr[:, 7 * N:7 * N + SAMPLE + 2]
        up = scr[:, 7 * N + SAMPLE + 2:7 * N + SAMPLE + 2 + PROMPT + 2]
        g0 = 7 * N + SAMPLE + PROMPT + 4
        gcb = scr[:, g0:g0 + T]

        def useq(tg):
            c0, n = GROUPS[tg]
            return [(ub, c0, slice(0, n))] if tg < TG else [(ub, c0, slice(0, SPLIT)), (up, 0, slice(SPLIT, n))]

        s_const = sem("s_const")
        s_x = [sem(f"s_x{i}") for i in range(2)]
        s_wada = [sem(f"s_wada{i}") for i in range(2)]
        s_raw = [sem(f"s_raw{i}") for i in range(2)]
        mod_cp = sem("mod_cp")
        mod_tr = sem("mod_tr")
        s_raw2 = [sem(f"s_raw2{i}") for i in range(2)]
        s_craw = sem("s_craw")
        s_rope = sem("s_rope")
        stored = sem("stored")
        q_stored = [sem(f"q_stored{i}") for i in range(2)]
        aux_stored = sem("aux_stored")
        lam_ch = sem("lam_ch")
        lam_e = sem("lam_e")
        sc_ready = sem("sc_ready")
        mod_mm = sem("mod_mm")
        mod_ch = sem("mod_ch")
        sq_ready = sem("sq_ready")
        sum_mm = sem("sum_mm")
        std_ready = sem("std_ready")
        rstd_ready = sem("rstd_ready")
        xn_ready = sem("xn_ready")
        h32_ready = sem("h32_ready")
        hhi_ready = sem("hhi_ready")
        hlo_ready = sem("hlo_ready")
        w_hi = sem("w_hi")
        w_lo = sem("w_lo")
        z_mm = sem("z_mm")
        z_used = sem("z_used")
        hi_ready = sem("hi_ready")
        lo_ready = sem("lo_ready")
        q_hi = sem("q_hi")
        q_lo = sem("q_lo")
        nv_ready = sem("nv_ready")
        sh_ready = sem("sh_ready")
        p_t1 = sem("p_t1")
        p_t2 = sem("p_t2")
        zr_ready = sem("zr_ready")
        sig_ready = sem("sig_ready")
        cvc = sem("cvc")
        tapped = sem("tapped")
        s_p = sem("s_p")
        s_k = sem("s_k")
        s_v = [sem(f"s_v{i}") for i in range(2)]
        s_q = [sem(f"s_q{i}") for i in range(4)]
        pr_mm = sem("pr_mm")
        pr_v = sem("pr_v")
        pr_a = sem("pr_a")
        s_pair = sem("s_pair")
        s_ctx = sem("s_ctx")
        mx_done = sem("mx_done")
        mxc_done = sem("mxc_done")
        gm_done = sem("gm_done")
        exp_done = sem("exp_done")
        expc_done = sem("expc_done")
        d_done = sem("d_done")
        f_done = sem("f_done")
        fz_done = sem("fz_done")
        den_done = sem("den_done")
        rden_done = sem("rden_done")
        rl_done = sem("rl_done")
        coef_done = sem("coef_done")
        e1_done = sem("e1_done")
        e0_done = sem("e0_done")
        a_ready = sem("a_ready")
        a1_ready = sem("a1_ready")
        t_mm = sem("t_mm")
        t_hi = sem("t_hi")
        t_lo = sem("t_lo")
        pv_mm = sem("pv_mm")
        att_evac = sem("att_evac")
        att_stored = [sem(f"att_stored{i}") for i in range(2)]
        c_raw = [sem(f"c_raw{i}") for i in range(2)]
        c_whi = sem("c_whi")
        c_wlo = sem("c_wlo")
        c_at = sem("c_at")
        c_mix = [sem(f"c_mix{i}") for i in range(2)]
        c_x = [sem(f"c_x{i}") for i in range(2)]
        c_sq = sem("c_sq")
        c_sum = sem("c_sum")
        c_std = sem("c_std")
        c_rs = sem("c_rs")
        c_y1 = sem("c_y1")
        c_y2 = sem("c_y2")
        c_hi = sem("c_hi")
        c_lo = sem("c_lo")
        o_mm = sem("o_mm")
        o_used = sem("o_used")
        o_st = [sem(f"o_st{i}") for i in range(4)]

        block = ctx.enter_context(nc.Block())

        V_UNITS = TILES
        QK0 = V_UNITS
        CV0 = V_UNITS + H * QK_UNITS
        ALL = CV0 + H * CV_UNITS
        XN = len(XGROUPS)
        CHUNKS = 32
        QKC, CVC = 4, 12
        CV_SLOT = [4, 1, 2, 3, 0]
        CV_RAW = [0, 1, 0, 1, 0]

        def f32(ap):
            return ap.bitcast(F32)

        def r32(ap):
            return ap.bitcast(F32R)

        def v_tiles(g):
            return range(max(0, 2 * g - 3), 2 * g - 1) if g < XN else range(2 * g - 3, TILES)

        def trbank(g):
            cnt = TGROUPS[g][1]
            return ps[:, 5 + g % 2, 0:cnt * P] if g < 4 else ps[:, 4, 2 * P:(2 + cnt) * P]

        @block.sync
        def _(sp):
            def load_w(c, buf):
                sp.dma_start(raw[:, buf], a["w_in"][c]).then_inc(s_raw[buf], 16)

            sp.dma_start(cst[:], a["cst"]).then_inc(s_const, 16)
            sp.dma_start(small[:], a["small"]).then_inc(s_const, 16)
            sp.dma_start(lamv[:], a["lam"]).then_inc(s_const, 16)
            def load_ada(hf):
                wait(sp, mod_mm, hf - 1)
                sp.dma_start(wad[:, hf % 2], a["w_ada"][4 * hf:4 * hf + 4].rearrange("n p j c -> p n j c"))\
                    .then_inc(s_wada[hf % 2], 16)

            load_ada(0)
            sp.dma_start(vraw.rearrange("p (h t) -> p h t", h=H),
                         a["cache_k"].rearrange("h p t -> p h t")).then_inc(s_craw, 16)
            load_ada(1)
            sp.dma_start(xs[:, 0], a["xT"][:, :, 0:XG]).then_inc(s_x[0], 16)
            sp.wait_ge(hi_ready, 1)
            sp.wait_ge(lo_ready, 1)
            for hl, src in ((0, vhi), (1, vlo)):
                sp.dma_start(spill["k"][:, hl, :, T:KCOLS].rearrange("h p t -> p h t"),
                             src.rearrange("p (h t) -> p h t", h=H)).then_inc(stored, 16)
            sp.dma_start(vraw, a["cache_v"]).then_inc(s_craw, 16)
            load_ada(2)
            sp.wait_ge(hi_ready, 2)
            sp.wait_ge(lo_ready, 2)
            for hl, src in ((0, vhi), (1, vlo)):
                sp.dma_start(spill["v"][:, :, KT - 1, hl, :].rearrange("h p e -> p h e"),
                             src.rearrange("p (h e) -> p h e", h=H)).then_inc(stored, 16)
            load_ada(3)
            sp.dma_start(xs[:, 1], a["xT"][:, :, XG:2 * XG]).then_inc(s_x[1], 16)
            load_w(0, 0)
            load_w(1, 1)
            load_ada(4)
            for i in range(2):
                sp.dma_start(raw2[:, i], a["w_in"][2 + i]).then_inc(s_raw2[i], 16)
            load_ada(5)

            for c in range(4, 6):
                sp.wait_ge(w_lo, c - 3)
                load_w(c, c % 2)
            for g in range(1, XN + 1):
                if g + 1 < XN:
                    c0, n = XGROUPS[g + 1]
                    sp.wait_ge(hlo_ready, g)
                    sp.dma_start(xs[:, (g + 1) % 2, :, 0:n], a["xT"][:, :, c0:c0 + n]).then_inc(s_x[(g + 1) % 2], 16)
                if g == 4:
                    sp.wait_ge(w_lo, 5)
                    load_w(6, 0)
                if g == XN:
                    sp.wait_ge(hlo_ready, XN)
                    sp.wait_ge(sum_mm, XN)
                    sp.dma_start(scr[:, 0:2 * T], a["rope"]).then_inc(s_rope, 16)
                for t in v_tiles(g):
                    sp.wait_ge(hi_ready, 2 + t + 1)
                    sp.wait_ge(z_used, t + 1)
                    for hl, src in ((0, vhi), (1, vlo)):
                        sp.dma_start(spill["v"][:, :, t if t < TILES - 1 else KT, hl, :].rearrange("h p e -> p h e"),
                                     src.rearrange("p (h e) -> p h e", h=H)).then_inc(stored, 16)
            sp.wait_ge(nv_ready, 1)
            sp.dma_start(a["new_v"], vraw).then_inc(aux_stored, 16)

            for h in range(H):
                for u in range(QK_UNITS):
                    c0, n = GROUPS[u % NG]
                    if u == 2:
                        sp.wait_ge(w_lo, 6 + 2 * h)
                        load_w(7 + 2 * h, 1)
                    if u == 7:
                        sp.wait_ge(w_lo, 7 + 2 * h)
                        load_w(8 + 2 * h, 0)
                    sp.wait_ge(q_hi, QK_UNITS * h + u + 1)
                    if u == NG - 1:
                        sp.dma_start(a["new_k"][h], qt1[u % 2][:, SPLIT:n]).then_inc(aux_stored, 16)
                    sp.wait_ge(q_lo, QK_UNITS * h + u + 1)
                    dst = spill["k"] if u < NG else spill["q"]
                    for hl, src in ((0, qhi), (1, qlo)):
                        sp.dma_start(dst[h, hl, :, c0:c0 + n], src[u % 2][:, 0:n]).then_inc(q_stored[u % 2], 16)

            def load_q(t, head, col):
                for ver in range(2):
                    for hl in range(2):
                        half = HD * (hl ^ ver)
                        sp.dma_start(f32(qb[half:half + HD, t, ver]),
                                     spill["q"][head, hl, :, col:col + P].rearrange("(m d) t -> d m t", m=2))\
                            .then_inc(s_q[t], 16)

            def load_k(head):
                for hl in range(2):
                    for k0, k1, c0 in ((0, SAMPLE, 0), (SAMPLE, KEYS, T)):
                        sp.dma_start(f32(kb[HD * hl:HD * hl + HD, head % 2, :, k0:k1]),
                                     spill["k"][head, hl, :, c0:c0 + k1 - k0].rearrange("(m d) t -> d m t", m=2))\
                            .then_inc(s_k, 16)

            def load_v(head, part):
                j0, j1 = (0, 9) if part == 0 else (9, KT)
                sp.dma_start(f32(vb[:, j0:j1]), spill["v"][head, :, j0:j1]).then_inc(s_v[part], 16)

            def load_prompt():
                for head in range(H):
                    for hl in range(2):
                        for ver in range(2):
                            half = HD * (hl ^ ver)
                            sp.dma_start(f32(qp[half:half + HD, ver, 2 * head:2 * head + 2]),
                                         spill["q"][head, hl, :, SAMPLE:T].rearrange("(m d) t -> d m t", m=2))\
                                .then_inc(s_p, 16)
                        sp.dma_start(f32(kp[HD * hl:HD * hl + HD, 2 * head:2 * head + 2]),
                                     spill["k"][head, hl, :, SAMPLE:T].rearrange("(m d) t -> d m t", m=2))\
                            .then_inc(s_p, 16)
                sp.dma_start(f32(vp[:]), spill["v"][:, :, KT].rearrange("h p l e -> p h l e")).then_inc(s_p, 16)

            def store_conv(f, tc):
                c0, n = GROUPS[tc]
                sp.wait_ge(cvc, 4 + 6 * (NG * f + tc) + 6)
                for hl, src in ((0, chi), (1, clo)):
                    sp.dma_start(spill["cv"][f, hl, :, c0:c0 + n], src[:, 0:n]).then_inc(stored, 16)

            for f in range(H):
                c = CVC + CV * f
                for tg in range(NG):
                    c0, n = GROUPS[tg]
                    if tg == 0:
                        sp.wait_ge(w_lo, c + 2)
                        load_w(c + 3, 1)
                        sp.wait_ge(w_lo, c + 3)
                        load_w(c + 4, 0)
                        if f + 1 < H:
                            sp.wait_ge(w_lo, c + 5)
                            load_w(c + 5, 0)
                            load_w(c + 6, 1)
                    sp.wait_ge(z_used, CV0 + CV_UNITS * f + CV * tg + 1)
                    sp.dma_start(spill["ga"][f, :, c0:c0 + n], gs[:, 0:n]).then_inc(aux_stored, 16)
                    if tg == TG and f + 1 < H:
                        sp.wait_ge(w_lo, c + 6)
                        load_w(c + 7, 0)
                    for tc in ([] if tg == 0 else [tg - 1] if tg < TG else [TG - 1, TG] if f < H - 1 else []):
                        store_conv(f, tc)

            sp.wait_ge(z_mm, ALL)
            sp.wait_ge(stored, 32 * (2 + V_UNITS))
            for i in range(2):
                sp.wait_ge(q_stored[i], 32 * H * QK_UNITS // 2)
            load_q(0, 0, 0)
            load_k(0)
            store_conv(H - 1, TG - 1)
            load_q(1, 0, P)
            load_q(2, 0, 2 * P)
            store_conv(H - 1, TG)
            load_q(3, 0, 3 * P)
            load_v(0, 0)
            load_v(0, 1)
            sp.wait_ge(stored, 32 * (2 + V_UNITS + H * NG))
            sp.wait_ge(aux_stored, 16 * (1 + H + H * NG))
            load_prompt()

            def load_wo(n):
                wait(sp, c_wlo, n - 1)
                sp.dma_start(worw[:, n % 2], a["w_out"][n]).then_inc(c_raw[n % 2], 16)

            for it in range(ITS):
                head = it // 4
                for t in range(4):
                    sp.wait_ge(s_pair, 4 * (4 * it + t + 1))
                    if it == 4 * (H - 1) and t == 0:
                        load_wo(0)
                        load_wo(1)
                    if it % 4 == 0 and t == 0 and head + 1 < H:
                        load_k(head + 1)
                    if it % 4 == 0 and head > 0 and t == 3:
                        sp.wait_ge(pv_mm, 4 * it - 1)
                        load_v(head, 0)
                    if it % 4 == 1 and head > 0 and t == 0:
                        sp.wait_ge(pv_mm, 4 * (it - 1))
                        load_v(head, 1)
                    if it + 1 < ITS:
                        load_q(t, (it + 1) // 4, ((it + 1) % 4) * 4 * P + t * P)

            def load_att(tg):
                c0, n = GROUPS[tg]
                wait(sp, c_lo, 4 * tg)
                for i in range(2):
                    sp.wait_ge(att_stored[i], 16 * (ITS - 4 + 1 if tg == 0 else ITS))
                if tg == TG:
                    sp.wait_ge(aux_stored, 16 * (1 + H + H * NG + 1))
                sp.dma_start(atr[:, :, 0:n], spill["att"][:, :, c0:c0 + n].rearrange("h p t -> p h t")).then_inc(c_at, 16)

            def load_gates(tg):
                c0, n = GROUPS[tg]
                sp.dma_start(gar[:, :, 0:n], spill["ga"][:, :, c0:c0 + n].rearrange("h p t -> p h t")).then_inc(c_at, 16)

            def load_mix(tg):
                c0, n = GROUPS[tg]
                par = tg % 2
                wait(sp, o_mm, DJ * (tg - 1))
                for hl in range(2):
                    sp.dma_start(f32(mix[:, par, hl, H:DJ, 0:n]),
                                 spill["cv"][:, hl, :, c0:c0 + n].rearrange("f p t -> p f t")).then_inc(c_mix[par], 16)

            def load_x(tg):
                c0, n = GROUPS[tg]
                par = tg % 2
                wait(sp, o_used, DJ * (tg - 1))
                sp.dma_start(xr[:, par, :, 0:n], a["xT"][:, :, c0:c0 + n]).then_inc(c_x[par], 16)

            load_att(0)
            for n in range(2, 6):
                load_wo(n)
            sp.wait_ge(t_mm, 5 * NT)
            load_gates(0)
            sp.wait_ge(pv_mm, NT - 2)
            load_mix(0)
            load_wo(6)
            load_wo(7)
            sp.wait_ge(pv_mm, NT)
            sp.wait_ge(aux_stored, 16 * (1 + H + H * NG + 1))
            for i in range(2):
                sp.wait_ge(att_stored[i], 16 * ITS)
            load_x(0)
            for tg in range(NG):
                if tg + 1 < NG:
                    load_att(tg + 1)
                    load_gates(tg + 1)
                    load_mix(tg + 1)
                    load_x(tg + 1)
                c0, n = GROUPS[tg]
                for o in range(DJ):
                    sp.wait_ge(o_used, DJ * tg + o + 1)
                    sp.dma_start(a["y"][o, :, c0:c0 + n], yo[:, o % 4, 0:n]).then_inc(o_st[o % 4], 16)
            for i in range(4):
                sp.wait_ge(o_st[i], 16 * 2 * NG)

        @block.gpsimd
        def _(pool):
            pool.memset(eps[:], EPS).then_inc(zr_ready, 1)
            pool.memset(lamc[:, 0:1], 1.0).then_inc(p_t1, 1)
            pool.wait_ge(s_rope, 16)

            def qk_unit(h, u, unit=True, lo=True):
                k = QK_UNITS * h + u
                b = u % 2
                if unit:
                    n = GROUPS[u % NG][1]
                    t1, t2 = qt1[b][:, 0:n], qt2[b][:, 0:n]
                    cols = slice(GROUPS[u % NG][0], GROUPS[u % NG][0] + n)
                    if u == NG + 1:
                        pool.wait_ge(aux_stored, 16 * (h + 2))
                    pool.wait_ge(z_used, QK0 + k + 1)
                    wait(pool, q_hi, k - 1)
                    wait(pool, q_lo, k - 1)
                    pool.tensor_tensor(t1, qzn[b][:, 0:n], cosT[:, cols], ALU.mult).then_inc(p_t1, 1)
                    pool.wait_ge(sh_ready, k + 1)
                    pool.tensor_tensor(t2, t2, sinT[:, cols], ALU.mult).then_inc(p_t2, 1)
                    pool.wait_ge(p_t1, 1 + k + 1)
                    pool.wait_ge(p_t2, k + 1)
                    pool.tensor_tensor(t1, t1, t2, ALU.add).then_inc(zr_ready, 1)
                if lo:
                    n = GROUPS[(u - 1) % NG][1]
                    pool.wait_ge(q_hi, k)
                    if u > 2 or not isinstance(h, int) or h > 0:
                        pool.wait_ge(q_stored[1 - b], 32 * (5 * h + (u - 3) // 2 + 1))
                    pool.tensor_tensor(r32(qlo[1 - b][:, 0:n]), qt1[1 - b][:, 0:n], qhi[1 - b][:, 0:n], ALU.subtract)\
                        .then_inc(q_lo, 1)

            for u in range(QK_UNITS):
                qk_unit(0, u, lo=u > 0)
            with pool.Fori(1, H) as h:
                for u in range(QK_UNITS):
                    qk_unit(h, u)
            qk_unit(H, 0, unit=False)

            def bc(x):
                return x.rearrange("p (m o) -> p m o", o=1).to_broadcast([P, 2, 3])

            def three(x):
                return x.rearrange("p (m c) -> p m c", m=2)

            def factors(n, t):
                b = t % 2
                pool.wait_ge(rden_done, n + 1)
                pool.tensor_tensor(stt[:, b, 6, 2:4], stt[:, b, 6, 0:2], lamc[:, :], ALU.mult).then_inc(rl_done, 1)
                pool.wait_ge(rl_done, n + 1)
                pool.tensor_tensor(three(stt[:, b, 7, :]), three(stt[:, b, 3, :]), bc(stt[:, b, 6, 2:4]), ALU.mult)\
                    .then_inc(coef_done, 1)
                pool.wait_ge(coef_done, n + 1)
                for c in (0, 2, 1):
                    k0, k1 = PIECES[c]
                    pool.tensor_tensor(e1[:, b, k0:k1], e1[:, b, k0:k1],
                                       stt[:, b, 7, 3 + c:4 + c].to_broadcast([P, k1 - k0]), ALU.mult)\
                        .then_inc(e1_done, 1)
                pool.tensor_tensor(e0[:, t, k0:k1], e0[:, t, k0:k1], stt[:, b, 7, 1:2].to_broadcast([P, k1 - k0]), ALU.mult)\
                    .then_inc(e0_done, 1)
                pool.wait_ge(e1_done, 3 * (n + 1))
                pool.wait_ge(e0_done, n + 1)
                pool.tensor_tensor(e0[:, t, k0:k1], e0[:, t, k0:k1], e1[:, b, k0:k1], ALU.add).then_inc(a1_ready, 1)

            for t in range(4):
                factors(t, t)
            with pool.Fori(1, ITS) as it:
                for t in range(4):
                    factors(4 * it + t, t)

        @block.tensor
        def _(pe):
            def sums(k, n, lhsT, parts, bank):
                pe.wait_ge(sq_ready, k + 1)
                wait(pe, std_ready, k - 1)
                for j, part in enumerate(parts):
                    mm = pe.matmul(ps[:, bank, 0:n], lhsT, part, start=(j == 0), stop=(j == len(parts) - 1))
                mm.then_inc(sum_mm, 1)

            def passes(out, slot_of, rhs_of):
                todo = [(0, 0), (0, 1), (1, 0)]
                for i, (l, r) in enumerate(todo):
                    for j in range(DJ):
                        mm = pe.matmul(out, slot_of(l, j), rhs_of(r, j),
                                       start=(i == 0 and j == 0), stop=(i == 2 and j == DJ - 1))
                mm.then_inc(z_mm, 1)

            pe.wait_ge(s_const, 48)
            def mod_turn(hf):
                pe.wait_ge(mod_cp, hf + 1)
                for i in range(4 * hf, 4 * hf + 4):
                    mm = pe.transpose(ps[:, 7, 2 * i:2 * i + 2], modr[0:2, i * P:(i + 1) * P], ident[0:2, 0:2])
                mm.then_inc(mod_tr, 1)

            pe.wait_ge(sc_ready, 1)
            for hf in range(6):
                pe.wait_ge(s_wada[hf % 2], 16 * (hf // 2 + 1))
                wait(pe, mod_cp, hf - 4)
                for j in range(DJ):
                    mm = pe.matmul(ps[0:2, hf % BANKS, :], sc[:, j], wad[:, hf % 2, :, j, :],
                                   start=(j == 0), stop=(j == DJ - 1))
                mm.then_inc(mod_mm, 1)
                if hf > 0:
                    mod_turn(hf - 1)
                if hf == 3:
                    sums(0, XG, ones, [xsq[:, j, :] for j in range(DJ)], 5)
            mod_turn(5)
            sums(1, XG, ones, [xsq[:, j, :] for j in range(DJ)], 6)
            for g in range(XN):
                pe.wait_ge(hlo_ready, g + 1)
                if g == 0:
                    pe.wait_ge(w_lo, 4)
                for t in range(2 * g, min(2 * g + 2, TILES)):
                    wait(pe, z_used, t - 4)
                    passes(ps[:, t % BANKS, :], lambda l, j: hT[:, l, j, t * P:(t + 1) * P],
                           lambda r, j: w[:, 0:4, r, j, :])
                    if t == 2 * g and g + 2 < XN:
                        n = XGROUPS[g + 2][1]
                        sums(g + 2, n, ones, [xsq[:, j, 0:n] for j in range(DJ)], 5 + g % 2)

            def qk_sums(k, u):
                n = GROUPS[u % NG][1]
                sums(XN + k, n, blk, [qsq[u % 2][:, 0:n]], 5 + (XN + u) % 2)

            def qk_unit(h, u, last=True):
                c0, n = GROUPS[u % NG]
                k = QK_UNITS * h + u
                if u % NG == 0:
                    pe.wait_ge(w_lo, QKC + 2 * h + u // NG + 1)
                pe.wait_ge(z_used, QK0 + k - 4)
                passes(ps[:, (QK0 + u) % BANKS, 0:n], lambda l, j: w[:, 4 if u < NG else 0, l, j, :],
                       lambda r, j: hT[:, r, j, c0:c0 + n])
                if last:
                    qk_sums(k - 1, (u - 1) % QK_UNITS)

            for u in range(QK_UNITS):
                qk_unit(0, u, last=u > 0)
            with pe.Fori(1, H) as h:
                for u in range(QK_UNITS):
                    qk_unit(h, u)
            qk_sums(H * QK_UNITS - 1, QK_UNITS - 1)

            with pe.Fori(0, H) as f:
                for tg in range(NG):
                    c0, n = GROUPS[tg]
                    for s in range(CV):
                        if tg == 0:
                            pe.wait_ge(w_lo, CVC + CV * f + s + 1)
                        pe.wait_ge(z_used, CV0 + CV_UNITS * f + CV * tg + s - 4)
                        passes(ps[:, (CV0 + s) % BANKS, 0:n], lambda l, j: w[:, CV_SLOT[s], l, j, :],
                               lambda r, j: hT[:, r, j, c0:c0 + n])

            def prompt_scores():
                pe.wait_ge(s_p, 16 * (6 * H + 1))
                pe.wait_ge(exp_done, 4 * NT)
                for m in range(2 * H):
                    for ver in range(2):
                        mm = pe.matmul(ps[:, m // 4, (m % 4) * P:(m % 4 + 1) * P], qp[:, ver, m], kp[:, m],
                                       start=(ver == 0), stop=(ver == 1))
                mm.then_inc(pr_mm, 1)

            def prompt_transposes():
                pe.wait_ge(pr_v, 7)
                for h in range(H):
                    mm = pe.transpose(ps[:, 2, h * P:(h + 1) * P], ap_[:, h * P:(h + 1) * P], ident)
                mm.then_inc(pr_mm, 1)

            def prompt_product():
                pe.wait_ge(pr_v, 8)
                for h in range(H):
                    for i, (l, r) in enumerate(((0, 0), (0, 1), (1, 0))):
                        mm = pe.matmul(ps[:, 3, h * P:(h + 1) * P], vp[:, h, l], atp[:, r, h],
                                       start=(i == 0), stop=(i == 2))
                mm.then_inc(pr_mm, 1)

            def transposes(n, t, g):
                j0, cnt = TGROUPS[g]
                if g == 0:
                    pe.wait_ge(a_ready, 2 * (n + 1))
                    pe.wait_ge(a1_ready, n + 1)
                wait(pe, t_lo, 5 * n + g - 1 if g in (2, 3) else 5 * n if g == 4 else 5 * (n - 1) + g + 3)
                for i in range(cnt):
                    mm = pe.transpose(trbank(g)[:, i * P:(i + 1) * P], e0[:, t, (j0 + i) * P:(j0 + i + 1) * P], ident)
                mm.then_inc(t_mm, 1)

            def product(b, half, part):
                js = (range(0, 9), range(9, KT))[half]
                todo = [(j, l, r) for j in js for l, r in ((0, 0), (0, 1), (1, 0))]
                cut = [0] + [len(todo) * i // 5 for i in (0, 1, 3, 5)] if half == 0 else [len(todo) * i // 4 for i in range(5)]
                for i in range(cut[part], cut[part + 1]):
                    j, l, r = todo[i]
                    mm = pe.matmul(ps[:, 7, b * 2 * P:(b + 1) * 2 * P], vb[:, j, l], at[:, b, r, j, :],
                                   start=(half == 0 and i == 0), stop=(half == 1 and i == len(todo) - 1))
                if part == 3:
                    mm.then_inc(pv_mm, 1)

            def scores(it, t, out, m, k0, k1):
                for ver in range(2):
                    for c0 in range(k0, k1, N):
                        c1 = min(c0 + N, k1)
                        keys = kb[:, 0, m, c0:c1] if isinstance(it, int) else \
                            kb[:, bass.ds((it // 4) % 2, 1), m, c0:c1].rearrange("p o t -> p (o t)")
                        mm = pe.matmul(out[:, c0 - k0:c1 - k0], qb[:, t, ver, m], keys, start=(ver == 0), stop=(ver == 1))
                return mm

            def step(it, t, sc=True, tr=True, tr_last=True, pv=True):
                n = 4 * it + t
                for p in range(4):
                    if sc:
                        if p == 0:
                            pe.wait_ge(s_q[t], 64 * (it + 1))
                            if t == 0:
                                pe.wait_ge(s_k, 64 * (it // 4 + 1))
                        wait(pe, exp_done, 4 * n + p - 1)
                        pair = ps[:, 2 * (p % 2):2 * (p % 2) + 2, :].rearrange("p c n -> p (c n)")
                        scores(it, t, pair, p // 2, *PIECES[p % 2]).then_inc(s_pair, 1)
                    if p == 0 and tr_last:
                        if sc or n == NT:
                            pe.wait_ge(expc_done, n)
                        transposes(n - 1 - S_TR, (t - 1 - S_TR) % 4, 4)
                    if pv:
                        half = 1 - t % 2
                        b = 0 if t in (1, 2) else 1
                        if p == 1 - half:
                            pe.wait_ge(s_v[half], 16 * ((it + (2 if t == 0 else 3)) // 4))
                            if half == 0:
                                pe.wait_ge(t_lo, 5 * (n - 4) + 3)
                                wait(pe, att_evac, 2 * it - (2 if t == 1 else 1))
                            else:
                                pe.wait_ge(t_lo, 5 * (n - 4))
                        product(b, half, p)
                    if tr:
                        transposes(n - S_TR, (t - S_TR) % 4, p)
                    if sc and p == 1:
                        wait(pe, expc_done, n)
                        wait(pe, t_lo, 5 * (n - S_TR))
                        scores(it, t, ps[:, 4, 0:P], 0, SAMPLE, KEYS)
                        scores(it, t, ps[:, 4, P:2 * P], 1, SAMPLE, KEYS).then_inc(s_ctx, 1)

            pe.wait_ge(z_used, ALL)
            for it in range(2):
                for t in range(4):
                    n = 4 * it + t
                    step(it, t, tr=n >= S_TR, tr_last=n > S_TR, pv=n >= S_PV)
            with pe.Fori(2, ITS) as it:
                for t in range(4):
                    step(it, t)
            prompt_scores()
            for n in range(NT, NT + S_PV):
                step(n // 4, n % 4, sc=False, tr=n < NT + S_TR, tr_last=n <= NT + S_TR)
                if n == NT + 2:
                    prompt_transposes()
                if n == NT + 4:
                    prompt_product()

            def csums(k, n):
                pe.wait_ge(c_sq, k + 1)
                wait(pe, c_std, k - 1)
                pe.matmul(ps[:, 6 + k % 2, 0:n], ones, csq[:, k % 2, 0:n], start=True, stop=True).then_inc(c_sum, 1)

            def out_half(tg, o, half):
                n = GROUPS[tg][1]
                k = DJ * tg + o
                if half == 0:
                    if tg == 0:
                        pe.wait_ge(c_wlo, o + 1)
                    if o == 0:
                        pe.wait_ge(c_mix[tg % 2], 32 * (tg // 2 + 1))
                    wait(pe, o_used, k - 3)
                elif o == 0:
                    pe.wait_ge(c_lo, H * (tg + 1))
                js = range(H) if half else range(H, DJ)
                for i, (l, r) in enumerate(((0, 0), (0, 1), (1, 0))):
                    for j in js:
                        mm = pe.matmul(ps[:, k % 4, 0:n], wo[:, o, l, j], mix[:, tg % 2, r, j, 0:n],
                                       start=(half == 0 and i == 0 and j == H),
                                       stop=(half == 1 and i == 2 and j == H - 1))
                if half:
                    mm.then_inc(o_mm, 1)

            for h in range(H):
                csums(h, GROUPS[0][1])
                out_half(0, h, 0)
            for tg in range(NG):
                for o in range(DJ):
                    if tg > 0 or o >= H:
                        out_half(tg, o, 0)
                    out_half(tg, o, 1)
                    if o in NORM_AT and tg + 1 < NG:
                        csums(H * (tg + 1) + NORM_AT[o], GROUPS[tg + 1][1])

        @block.scalar
        def _(act):
            act.wait_ge(s_const, 48)
            act.activation(sc[:].rearrange("p j v -> p (j v)"), c_in, ACT.Silu).then_inc(sc_ready, 1)
            act.wait_ge(lam_ch, 2)
            act.activation(lamt[:, 2:4], lamt[:, 0:2], ACT.Exp).then_inc(lam_e, 1)
            act.wait_ge(s_craw, 16)
            act.activation(r32(vhi), vraw, ACT.Copy).then_inc(hi_ready, 1)

            def w_split(c, buf, slot, ordinal):
                act.wait_ge(s_raw[buf], 16 * ordinal)
                act.activation(w[:, slot, 0], raw[:, buf], ACT.Copy).then_inc(w_hi, 1)

            def v_hi(t):
                act.wait_ge(z_mm, t + 1)
                act.wait_ge(stored, 32 * (2 + t))
                act.activation(r32(vhi), ps[:, t % BANKS, :], ACT.Copy).then_inc(hi_ready, 1)

            def x_square(g):
                n = XGROUPS[g][1]
                act.wait_ge(s_x[g % 2], 16 * (g // 2 + 1))
                wait(act, sum_mm, g)
                if g == 0:
                    act.wait_ge(lo_ready, 2)
                act.activation(xsq[:, :, 0:n], xs[:, g % 2, :, 0:n], ACT.Square).then_inc(sq_ready, 1)

            def mod_copy(hf):
                act.wait_ge(mod_mm, hf + 1)
                act.activation(modr[0:2, hf * N:(hf + 1) * N], ps[0:2, hf % BANKS, :], ACT.Copy).then_inc(mod_cp, 1)

            act.wait_ge(s_craw, 32)
            act.wait_ge(stored, 32)
            act.activation(r32(vhi), vraw, ACT.Copy).then_inc(hi_ready, 1)
            mod_copy(0)
            x_square(0)
            for hf in range(1, 4):
                mod_copy(hf)
            def x_root(g):
                n = XGROUPS[g][1]
                act.wait_ge(sum_mm, g + 1)
                wait(act, rstd_ready, g)
                act.activation(xstd[:, 0:n], ps[:, 5 + g % 2, 0:n], ACT.Sqrt, scale=1.0 / D, bias=eps[:])\
                    .then_inc(std_ready, 1)

            act.wait_ge(zr_ready, 1)
            x_root(0)
            x_square(1)
            mod_copy(4)
            mod_copy(5)
            for c in range(4):
                if c < 2:
                    w_split(c, c, c, 1)
                else:
                    act.wait_ge(s_raw2[c - 2], 16)
                    act.activation(w[:, c, 0], raw2[:, c - 2], ACT.Copy).then_inc(w_hi, 1)
            for g in range(XN):
                c0, n = XGROUPS[g]
                v = 0 if c0 < SAMPLE else 1
                tiles = list(v_tiles(g))
                for t in tiles[:-1]:
                    v_hi(t)
                act.wait_ge(xn_ready, g + 1)
                if g == 0:
                    act.wait_ge(mod_ch, 3)
                for j in range(DJ):
                    hm = act.activation(xs[:, g % 2, j, 0:n], xs[:, g % 2, j, 0:n], ACT.Identity,
                                        scale=mult[:, j, v:v + 1], bias=mod[:, j, v:v + 1])
                hm.then_inc(h32_ready, 1)
                if 0 < g < XN - 1:
                    x_square(g + 1)
                for t in tiles[-1:]:
                    v_hi(t)
                if g + 1 < XN:
                    x_root(g + 1)
                if g == 1:
                    w_split(4, 0, 4, 2)
            for t in v_tiles(XN):
                v_hi(t)

            act.wait_ge(stored, 32 * (2 + V_UNITS))
            act.wait_ge(aux_stored, 16)

            def qk_unit(h, u, sq=True, root=True, hi=True):
                k = QK_UNITS * h + u
                b = u % 2
                if sq:
                    n = GROUPS[u % NG][1]
                    act.wait_ge(z_mm, QK0 + k + 1)
                    act.wait_ge(sum_mm, XN + k - 1)
                    act.activation(qsq[b][:, 0:n], ps[:, (QK0 + u) % BANKS, 0:n], ACT.Square).then_inc(sq_ready, 1)
                if root:
                    n = GROUPS[(u - 1) % NG][1]
                    act.wait_ge(sum_mm, XN + k)
                    act.wait_ge(z_used, QK0 + k - 2)
                    act.activation(qrs[1 - b][:, 0:n], ps[:, 5 + (XN + u - 1) % 2, 0:n], ACT.Sqrt,
                                   scale=1.0 / HD, bias=eps[:]).then_inc(std_ready, 1)
                if u == 1 and sq:
                    act.wait_ge(z_mm, QK0 + QK_UNITS * h)
                    w_split(QKC + 2 * h + 1, 1, 0, 2 + h)
                if u == 6:
                    act.wait_ge(z_mm, QK0 + QK_UNITS * h + NG)
                    w_split(QKC + 2 * h + 2, 0, 4, 3 + h)
                if hi:
                    n = GROUPS[(u - 2) % NG][1]
                    act.wait_ge(zr_ready, 1 + k - 1)
                    if u > 3 or not isinstance(h, int) or h > 0:
                        act.wait_ge(q_stored[b], 32 * (5 * h + (u - 4) // 2 + 1))
                    act.activation(r32(qhi[b][:, 0:n]), qt1[b][:, 0:n], ACT.Copy).then_inc(q_hi, 1)

            for u in range(QK_UNITS):
                qk_unit(0, u, root=u > 0, hi=u > 1)
            with act.Fori(1, H) as h:
                for u in range(QK_UNITS):
                    qk_unit(h, u)
            w_split(CVC + 1, 1, CV_SLOT[1], 6)
            qk_unit(H, 0, sq=False)
            qk_unit(H, 1, sq=False, root=False)

            act.wait_ge(q_lo, H * QK_UNITS)

            def conv(f, last):
                for s in range(2, CV):
                    act.wait_ge(z_mm, CV0 + CV_UNITS * f - 4 + s)
                    w_split(0, CV_RAW[s], CV_SLOT[s], {2: 7 + 3 * f, 3: 7 + 2 * f, 4: 8 + 3 * f}[s])
                for tg in range(NG):
                    n = GROUPS[tg][1]
                    for s in range(2):
                        act.wait_ge(z_mm, CV0 + CV_UNITS * f + CV * tg + s + 1)
                        act.wait_ge(z_used, CV0 + CV_UNITS * f + CV * (tg - 1) + s + 1)
                        act.activation(sig[:, s, 0:n], ps[:, (CV0 + s) % BANKS, 0:n], ACT.Sigmoid).then_inc(sig_ready, 1)
                if not last:
                    w_split(0, 0, CV_SLOT[0], 9 + 3 * f)
                    act.wait_ge(z_mm, CV0 + CV_UNITS * f + CV_UNITS - 3)
                    w_split(0, 1, CV_SLOT[1], 8 + 2 * f)

            conv(0, False)
            with act.Fori(1, H - 1) as f:
                conv(f, False)
            conv(H - 1, True)

            def prompt_exp():
                act.wait_ge(pr_v, 2)
                act.activation(ep[:], ep[:], ACT.Exp).then_inc(pr_a, 1)

            def prompt_hi():
                act.wait_ge(pr_mm, 2)
                act.activation(atp[:, 0].rearrange("p h t -> p (h t)"), ps[:, 2, :], ACT.Copy).then_inc(pr_a, 1)

            def prompt_out():
                act.wait_ge(pr_mm, 3)
                act.activation(pro[:], ps[:, 3, :], ACT.Copy).then_inc(pr_a, 1)
                act.wait_ge(pr_a, 3)
                act.dma_start(spill["att"][:, :, SAMPLE:T].rearrange("h p t -> p h t"),
                              pro[:].rearrange("p (h t) -> p h t", h=H)).then_inc(aux_stored, 16)

            def wo_hi(n):
                act.wait_ge(c_raw[n % 2], 16 * (n // 2 + 1))
                act.activation(wo[:, n, 0], worw[:, n % 2], ACT.Copy).then_inc(c_whi, 1)

            def tr_hi(n, t, g):
                j0, cnt = TGROUPS[g]
                act.wait_ge(t_mm, 5 * n + g + 1)
                if g == 0 and t % 2 == 0:
                    wait(act, pv_mm, n - 2)
                act.activation(at[:, t // 2, 0, j0:j0 + cnt, (t % 2) * P:(t % 2 + 1) * P],
                               trbank(g).rearrange("p (j q) -> p j q", j=cnt), ACT.Copy).then_inc(t_hi, 1)

            def step(it, t, sc=True, tr=True, tr_last=True, out=True):
                n = 4 * it + t
                b = t % 2
                for p in range(4):
                    m, c = p // 2, p % 2
                    if sc and p == 3:
                        act.wait_ge(mxc_done, n + 1)
                        wait(act, a_ready, 2 * (n - 1))
                        for mc in range(2):
                            dst = e0[:, t] if mc == 0 else e1[:, b]
                            em = act.activation(dst[:, SAMPLE:KEYS], ps[:, 4, mc * P:(mc + 1) * P], ACT.Exp,
                                                bias=stt[:, b, 0, 3 * mc + 2:3 * mc + 3],
                                                accum_out=stt[:, b, 1, 3 * mc + 2:3 * mc + 3])
                        em.then_inc(expc_done, 1)
                    if sc:
                        act.wait_ge(mx_done, 4 * n + p + 1)
                        if p == 0:
                            wait(act, t_mm, 5 * (n - 3))
                        if p == 2:
                            wait(act, a_ready, 2 * (n - 1) - 1)
                        if p == 3:
                            wait(act, a1_ready, n - 1)
                        dst = e0[:, t] if m == 0 else e1[:, b]
                        act.activation(dst[:, c * 1024:(c + 1) * 1024],
                                       ps[:, 2 * c:2 * c + 2, :].rearrange("p c n -> p (c n)"), ACT.Exp,
                                       bias=stt[:, b, 0, 3 * m + c:3 * m + c + 1],
                                       accum_out=stt[:, b, 1, 3 * m + c:3 * m + c + 1]).then_inc(exp_done, 1)
                    if p == 0 and tr_last:
                        tr_hi(n - 1 - S_TR, (t - 1 - S_TR) % 4, 4)
                    if out and p == 0:
                        pb = 1 if t == 1 else 0
                        pair = 2 * it - (3 if t == 1 else 2)
                        act.wait_ge(pv_mm, n - S_PV)
                        wait(act, att_stored[pb], 16 * (it - (2 if t == 1 else 1)))
                        act.activation(atto[:, pb], ps[:, 7, pb * 2 * P:(pb + 1) * 2 * P], ACT.Copy).then_inc(att_evac, 1)
                        act.wait_ge(att_evac, pair + 1)
                        u = it - (2 if t == 1 else 1)
                        q0 = (u % 4) * (4 * P) + pb * 2 * P
                        if isinstance(it, int):
                            dst = spill["att"][u // 4, :, q0:q0 + 2 * P]
                        else:
                            dst = spill["att"][bass.ds(u // 4, 1), :, bass.ds(q0, 2 * P)].rearrange("o p t -> (o p) t")
                        act.dma_start(dst, atto[:, pb]).then_inc(att_stored[pb], 16)
                    if tr:
                        tr_hi(n - S_TR, (t - S_TR) % 4, p)
                if sc:
                    act.wait_ge(d_done, n + 1)
                    act.activation(stt[:, b, 3, :], stt[:, b, 2, :], ACT.Exp).then_inc(f_done, 1)

            for it in range(3):
                for t in range(4):
                    n = 4 * it + t
                    step(it, t, tr=n >= S_TR, tr_last=n > S_TR, out=n >= S_OUT and t % 2 == 1)
            with act.Fori(3, ITS) as it:
                for t in range(4):
                    step(it, t, out=t % 2 == 1)
            for n in range(NT, NT + S_OUT - 1):
                step(n // 4, n % 4, sc=False, tr=n < NT + S_TR, tr_last=n <= NT + S_TR,
                     out=n % 2 == 1)
                if n == NT:
                    wo_hi(0)
                    wo_hi(1)
                    prompt_exp()
                if n == NT + 2:
                    act.wait_ge(a_ready, 2 * NT)
                    act.wait_ge(a1_ready, NT)
                    wo_hi(2)
                    wo_hi(3)
                if n == NT + 3:
                    prompt_hi()
                    act.wait_ge(t_mm, 5 * (NT - 1))
                    for o in range(4, DJ):
                        wo_hi(o)
            prompt_out()


            def square(tg, h):
                n = GROUPS[tg][1]
                k = H * tg + h
                if h == 0:
                    act.wait_ge(c_at, 32 * (tg + 1))
                wait(act, c_sum, k - 1)
                act.activation(csq[:, k % 2, 0:n], atr[:, h, 0:n], ACT.Square).then_inc(c_sq, 1)

            def root(tg, h):
                n = GROUPS[tg][1]
                k = H * tg + h
                act.wait_ge(c_sum, k + 1)
                wait(act, c_y1, k - 1)
                act.activation(crs[:, k % 2, 0:n], ps[:, 6 + k % 2, 0:n], ACT.Sqrt, scale=1.0 / P, bias=eps[:])\
                    .then_inc(c_std, 1)

            def mix_hi(tg, h):
                n = GROUPS[tg][1]
                k = H * tg + h
                act.wait_ge(c_y2, k + 1)
                wait(act, o_mm, DJ * (tg - 1))
                act.activation(mix[:, tg % 2, 0, h, 0:n], cy[:, k % 2, 0:n], ACT.Copy).then_inc(c_hi, 1)

            for tg in range(NG):
                for h in range(H + 2):
                    if h < H:
                        square(tg, h)
                    if 1 <= h <= H:
                        root(tg, h - 1)
                    if h >= 2:
                        mix_hi(tg, h - 2)

        @block.vector
        def _(dve):
            dve.wait_ge(s_const, 48)
            for i in range(2):
                dve.tensor_tensor_reduce(lamj[:, i], lamv[:, 2 * i], lamv[:, 2 * i + 1], 1.0, 0.0, ALU.mult, ALU.add,
                                         lamt[:, i:i + 1]).then_inc(lam_ch, 1)
            dve.tensor_scalar(sublns[:], subln, 1.0 - LAM_INIT, None, ALU.mult).then_inc(lam_ch, 1)
            dve.tensor_scalar(qks[:, 0:1], qk_w[:, 0:1], HD ** -0.5, None, ALU.mult).then_inc(lam_ch, 1)
            dve.tensor_copy(qks[:, 1:2], qk_w[:, 1:2]).then_inc(lam_ch, 1)
            dve.wait_ge(lam_e, 1)
            dve.tensor_tensor(lamt[:, 4:5], lamt[:, 3:4], lamt[:, 2:3], ALU.subtract).then_inc(lam_ch, 1)
            dve.wait_ge(lam_ch, 6)
            dve.tensor_scalar(lamc[:, 1:2], lamt[:, 4:5], -LAM_INIT, None, ALU.add).then_inc(lam_ch, 1)

            def cache_lo(i):
                dve.wait_ge(hi_ready, i + 1)
                dve.tensor_tensor(r32(vlo), vraw, vhi, ALU.subtract).then_inc(lo_ready, 1)

            cache_lo(0)
            cache_lo(1)

            def w_split(c, buf, slot, src=raw):
                dve.wait_ge(w_hi, c + 1)
                dve.tensor_tensor(w[:, slot, 1], src[:, buf], f32(w[:, slot, 0]), ALU.subtract).then_inc(w_lo, 1)

            def v_lo(t):
                dve.wait_ge(hi_ready, 2 + t + 1)
                dve.tensor_tensor(r32(vlo), ps[:, t % BANKS, :], vhi, ALU.subtract).then_inc(z_used, 1)

            def x_recip(g):
                n = XGROUPS[g][1]
                dve.wait_ge(std_ready, g + 1)
                wait(dve, xn_ready, g)
                dve.reciprocal(xrstd[:, 0:n], xstd[:, 0:n]).then_inc(rstd_ready, 1)

            dve.wait_ge(s_x[0], 16)
            x_recip(0)
            for g in range(XN):
                n = XGROUPS[g][1]
                tiles = list(v_tiles(g))
                dve.wait_ge(rstd_ready, g + 1)
                x = xs[:, g % 2, :, 0:n]
                dve.tensor_tensor(x, x, xrstd[:, 0:n].rearrange("p (o t) -> p o t", o=1).to_broadcast([P, DJ, n]),
                                  ALU.mult).then_inc(xn_ready, 1)
                for t in tiles[:-1]:
                    v_lo(t)
                if g == 0:
                    dve.wait_ge(mod_tr, 6)
                    dve.tensor_tensor(mod[:], ps[:, 7, 0:48].rearrange("p (n v) -> p n v", v=2),
                                      b_ada.rearrange("p (n o) -> p n o", o=1).to_broadcast([P, 24, 2]), ALU.add)\
                        .then_inc(mod_ch, 1)
                    dve.wait_ge(mod_ch, 1)
                    dve.tensor_scalar(mult[:], mod[:, 8:16], 1.0, None, ALU.add).then_inc(mod_ch, 1)
                    dve.wait_ge(mod_ch, 2)
                    dve.tensor_tensor(mult[:], mult[:], norm_w.rearrange("p (n o) -> p n o", o=1).to_broadcast([P, DJ, 2]),
                                      ALU.mult).then_inc(mod_ch, 1)
                    for c in range(4):
                        w_split(c, c % 2, c, raw if c < 2 else raw2)
                dve.wait_ge(h32_ready, g + 1)
                c0 = XGROUPS[g][0]
                dve.tensor_copy(hT[:, 0, :, c0:c0 + n], x).then_inc(hhi_ready, 1)
                dve.wait_ge(hhi_ready, g + 1)
                dve.tensor_tensor(hT[:, 1, :, c0:c0 + n], x, f32(hT[:, 0, :, c0:c0 + n]), ALU.subtract)\
                    .then_inc(hlo_ready, 1)
                for t in tiles[-1:]:
                    v_lo(t)
                if g + 1 < XN:
                    x_recip(g + 1)
                if g == 1:
                    w_split(4, 0, 4)
            v_lo(TILES - 2)
            dve.wait_ge(z_mm, TILES)
            dve.wait_ge(hi_ready, 2 + TILES)
            dve.wait_ge(sum_mm, XN)
            dve.tensor_copy(vraw, ps[:, (TILES - 1) % BANKS, :]).then_inc(nv_ready, 1)
            v_lo(TILES - 1)

            dve.wait_ge(lam_ch, 7)

            def qk_unit(h, u):
                n = GROUPS[u % NG][1]
                comp = 1 - u // NG
                k = QK_UNITS * h + u
                b = u % 2
                rs, zn = qrs[b][:, 0:n], qzn[b][:, 0:n]
                dve.wait_ge(std_ready, XN + k + 1)
                dve.reciprocal(rs, rs).then_inc(rstd_ready, 1)
                dve.wait_ge(rstd_ready, XN + k + 1)
                wait(dve, p_t1, k)
                wait(dve, sh_ready, k - 1)
                dve.scalar_tensor_tensor(zn, ps[:, (QK0 + u) % BANKS, 0:n], qks[:, comp:comp + 1], rs,
                                         ALU.mult, ALU.mult).then_inc(z_used, 1)
                wait(dve, zr_ready, k)
                dve.wait_ge(z_used, QK0 + k + 1)
                dve.tensor_copy(tick[:], eps[:])
                dve.stream_shuffle(qt2[b][:, 0:n], zn, [i ^ 16 for i in range(32)]).then_inc(sh_ready, 1)
                if u == 1:
                    w_split(QKC + 2 * h + 1, 1, 0)
                if u == 6:
                    w_split(QKC + 2 * h + 2, 0, 4)

            for u in range(QK_UNITS):
                qk_unit(0, u)
            with dve.Fori(1, H) as h:
                for u in range(QK_UNITS):
                    qk_unit(h, u)
            w_split(CVC + 1, 1, CV_SLOT[1])

            dve.wait_ge(q_lo, H * QK_UNITS)
            for i in range(2):
                dve.wait_ge(q_stored[i], 32 * H * QK_UNITS // 2)
            for i, z in enumerate((ub[:, 0:1], ub[:, SAMPLE + 1:SAMPLE + 2], up[:, 0:1], up[:, PROMPT + 1:PROMPT + 2])):
                dve.memset(z, 0.0).then_inc(cvc, 1)
            dve.wait_ge(cvc, 4)

            def conv_group(f, tg):
                c0, n = GROUPS[tg]
                base = 4 + 6 * (NG * f + tg)

                def wcol(i):
                    return cw[:, i:i + 1]

                dve.wait_ge(cvc, base)
                for i in range(3):
                    if i:
                        dve.wait_ge(cvc, base + i)
                    for seq, o, cols in useq(tg):
                        u = seq[:, o + i:o + i + cols.stop - cols.start]
                        if i == 0:
                            tap = dve.tensor_scalar(cc_[:, cols], u, wcol(0), wcol(3), ALU.mult, ALU.add)
                        else:
                            tap = dve.scalar_tensor_tensor(cc_[:, cols], u, wcol(i), cc_[:, cols], ALU.mult, ALU.add)
                    tap.then_inc(cvc, 1)
                dve.wait_ge(cvc, base + 3)
                dve.tensor_tensor(cc_[:, 0:n], cc_[:, 0:n], gcb[:, c0:c0 + n], ALU.mult).then_inc(cvc, 1)
                dve.wait_ge(cvc, base + 4)
                dve.wait_ge(stored, 32 * (2 + V_UNITS) + 32 * (NG * f + tg))
                dve.tensor_copy(r32(chi[:, 0:n]), cc_[:, 0:n]).then_inc(cvc, 1)
                dve.wait_ge(cvc, base + 5)
                dve.tensor_tensor(r32(clo[:, 0:n]), cc_[:, 0:n], chi[:, 0:n], ALU.subtract).then_inc(cvc, 1)

            def conv(f, last):
                dve.wait_ge(cvc, 4 + 6 * NG * f)
                dve.tensor_copy(cw[:, 0:4], taps[:, bass.ds(4 * f, 4)]).then_inc(tapped, 1)
                for s in range(2, CV):
                    w_split(CVC + CV * f + s, CV_RAW[s], CV_SLOT[s])
                for tg in range(NG):
                    c0, n = GROUPS[tg]
                    z0 = CV0 + CV_UNITS * f + CV * tg
                    z = [ps[:, (CV0 + s) % BANKS, 0:n] for s in range(CV)]
                    dve.wait_ge(sig_ready, 2 * (NG * f + tg) + 1)
                    dve.wait_ge(aux_stored, 16 * (1 + H) + 16 * (NG * f + tg))
                    dve.tensor_tensor(gs[:, 0:n], z[0], sig[:, 0, 0:n], ALU.mult).then_inc(z_used, 1)
                    dve.wait_ge(sig_ready, 2 * (NG * f + tg) + 2)
                    g = gcb[:, c0:c0 + n]
                    dve.tensor_tensor(g, z[1], sig[:, 1, 0:n], ALU.mult).then_inc(z_used, 1)
                    dve.wait_ge(z_mm, z0 + 3)
                    dve.wait_ge(z_used, z0 + 2)
                    dve.tensor_tensor(g, z[2], g, ALU.mult).then_inc(z_used, 1)
                    if tg == TG and not last:
                        w_split(CVC + CV * f + CV, 0, CV_SLOT[0])
                    dve.wait_ge(z_mm, z0 + 4)
                    dve.tensor_copy(ccs[:, 0:n], z[3]).then_inc(z_used, 1)
                    dve.wait_ge(z_mm, z0 + 5)
                    dve.wait_ge(z_used, z0 + 4)
                    for seq, o, cols in useq(tg):
                        um = dve.tensor_tensor(seq[:, o + 1:o + 1 + cols.stop - cols.start], z[4][:, cols], ccs[:, cols],
                                               ALU.mult)
                    um.then_inc(z_used, 1)
                    if tg == TG and not last:
                        w_split(CVC + CV * f + CV + 1, 1, CV_SLOT[1])
                    dve.wait_ge(z_used, z0 + 5)
                    if tg == 1:
                        dve.wait_ge(tapped, f + 1)
                    for tc in ([] if tg == 0 else [tg - 1] if tg < TG else [TG - 1, TG]):
                        conv_group(f, tc)

            conv(0, False)
            with dve.Fori(1, H - 1) as f:
                conv(f, False)
            conv(H - 1, True)

            def maps(x):
                return x.rearrange("p (m t) -> p m t", m=2 * H)

            def wide(x):
                return x.rearrange("p (m o) -> p m o", o=1).to_broadcast([P, 2 * H, P])

            def prompt_maps():
                scores_p = maps(ps[:, 0:2, :].rearrange("p c n -> p (c n)"))
                dve.wait_ge(pr_mm, 1)
                dve.tensor_reduce(stp[:, 0], scores_p, AX.X, ALU.max).then_inc(pr_v, 1)
                dve.wait_ge(pr_v, 1)
                dve.tensor_tensor(maps(ep[:]), scores_p, wide(stp[:, 0]), ALU.subtract).then_inc(pr_v, 1)
                dve.wait_ge(pr_a, 1)
                dve.tensor_reduce(stp[:, 1], maps(ep[:]), AX.X, ALU.add).then_inc(pr_v, 1)
                dve.wait_ge(pr_v, 3)
                dve.reciprocal(stp[:, 2], stp[:, 1]).then_inc(pr_v, 1)
                dve.wait_ge(pr_v, 4)
                dve.tensor_tensor(stp[:, 3].rearrange("p (h m) -> p h m", m=2),
                                  stp[:, 2].rearrange("p (h m) -> p h m", m=2),
                                  lamc[:].rearrange("p (o m) -> p o m", o=1).to_broadcast([P, H, 2]), ALU.mult)\
                    .then_inc(pr_v, 1)
                dve.wait_ge(pr_v, 5)
                dve.tensor_tensor(maps(ep[:]), maps(ep[:]), wide(stp[:, 3]), ALU.mult).then_inc(pr_v, 1)
                dve.wait_ge(pr_v, 6)
                eh = ep[:].rearrange("p (h m t) -> p h m t", h=H, m=2)
                dve.tensor_tensor(ap_[:].rearrange("p (h t) -> p h t", h=H), eh[:, :, 0], eh[:, :, 1], ALU.add)\
                    .then_inc(pr_v, 1)

            def prompt_lo():
                dve.wait_ge(pr_a, 2)
                dve.tensor_tensor(atp[:, 1].rearrange("p h t -> p (h t)"), ps[:, 2, :],
                                  f32(atp[:, 0]).rearrange("p h t -> p (h t)"), ALU.subtract).then_inc(pr_v, 1)

            def wo_lo(n):
                dve.wait_ge(c_whi, n + 1)
                dve.tensor_tensor(wo[:, n, 1], worw[:, n % 2], f32(wo[:, n, 0]), ALU.subtract).then_inc(c_wlo, 1)

            def tr_lo(n, t, g):
                j0, cnt = TGROUPS[g]
                dve.wait_ge(t_hi, 5 * n + g + 1)
                cols = slice((t % 2) * P, (t % 2 + 1) * P)
                dve.tensor_tensor(at[:, t // 2, 1, j0:j0 + cnt, cols], trbank(g).rearrange("p (j q) -> p j q", j=cnt),
                                  f32(at[:, t // 2, 0, j0:j0 + cnt, cols]), ALU.subtract).then_inc(t_lo, 1)

            def combine(n, t, c):
                k0, k1 = PIECES[c]
                dve.wait_ge(e1_done, 3 * n + (1 if c == 0 else 2))
                dve.scalar_tensor_tensor(e0[:, t, k0:k1], e0[:, t, k0:k1], stt[:, t % 2, 7, c:c + 1],
                                         e1[:, t % 2, k0:k1], ALU.mult, ALU.add).then_inc(a_ready, 1)

            def bc(x):
                return x.rearrange("p (m o) -> p m o", o=1).to_broadcast([P, 2, 3])

            def three(x):
                return x.rearrange("p (m c) -> p m c", m=2)

            def step(it, t, sc=True, den=True, comb=True, tr=True, tr_last=True):
                n = 4 * it + t
                b = t % 2
                for p in range(4):
                    m, c = p // 2, p % 2
                    if sc:
                        dve.wait_ge(s_pair, 4 * n + p + 1)
                        if p == 0:
                            wait(dve, coef_done, n - 1)
                        dve.tensor_reduce(stt[:, b, 0, 3 * m + c:3 * m + c + 1],
                                          ps[:, 2 * c:2 * c + 2, :].rearrange("p c n -> p (c n)"), AX.X, ALU.max,
                                          negate=True).then_inc(mx_done, 1)
                    if p == 0 and comb:
                        combine(n - S_COMB, (t - S_COMB) % 4, 0)
                    if p == 0 and den:
                        dve.wait_ge(f_done, n)
                        dve.tensor_tensor(stt[:, 1 - b, 4, :], stt[:, 1 - b, 3, :], stt[:, 1 - b, 1, :], ALU.mult)\
                            .then_inc(fz_done, 1)
                    if p == 0 and tr_last:
                        tr_lo(n - 1 - S_TR, (t - 1 - S_TR) % 4, 3)
                    if p == 0 and den:
                        dve.wait_ge(fz_done, n)
                        dve.tensor_reduce(stt[:, 1 - b, 5, 0:2], three(stt[:, 1 - b, 4, :]), AX.X, ALU.add)\
                            .then_inc(den_done, 1)
                    if p == 0 and tr_last:
                        tr_lo(n - 1 - S_TR, (t - 1 - S_TR) % 4, 4)
                    if p == 0 and den:
                        dve.wait_ge(den_done, n)
                        dve.reciprocal(stt[:, 1 - b, 6, 0:2], stt[:, 1 - b, 5, 0:2]).then_inc(rden_done, 1)
                    if p > 0 and tr:
                        tr_lo(n - S_TR, (t - S_TR) % 4, p - 1)
                    if p == 3 and sc:
                        dve.wait_ge(mxc_done, n + 1)
                        dve.wait_ge(mx_done, 4 * n + 4)
                        dve.tensor_reduce(stt[:, b, 5, 2:4], stt[:, b, 0, :].rearrange("p (m c) -> p m c", m=2), AX.X,
                                          ALU.min).then_inc(gm_done, 1)
                        dve.wait_ge(gm_done, n + 1)
                        dve.tensor_tensor(three(stt[:, b, 2, :]), bc(stt[:, b, 5, 2:4]), three(stt[:, b, 0, :]),
                                          ALU.subtract).then_inc(d_done, 1)
                    if p == 2 and comb:
                        combine(n - S_COMB, (t - S_COMB) % 4, 2)
                    if sc and p == 2:
                        dve.wait_ge(s_ctx, n + 1)
                        dve.tensor_reduce(stt[:, b, 0, 2:6:3], ps[:, 4, 0:2 * P].rearrange("p (m k) -> p m k", m=2), AX.X,
                                          ALU.max, negate=True).then_inc(mxc_done, 1)

            for t in range(4):
                step(0, t, den=t >= 1, comb=t >= S_COMB, tr=t >= S_TR, tr_last=t > S_TR)
            with dve.Fori(1, ITS) as it:
                for t in range(4):
                    step(it, t)
            for n in range(NT, NT + S_TR + 1):
                step(n // 4, n % 4, sc=False, den=n == NT, comb=n < NT + S_COMB, tr=n < NT + S_TR)
                if n == NT:
                    wo_lo(0)
                    wo_lo(1)
                    prompt_maps()
                if n == NT + 2:
                    wo_lo(2)
                    wo_lo(3)
                if n == NT + 3:
                    prompt_lo()
                    for o in range(4, DJ):
                        wo_lo(o)


            def norm(tg, h):
                n = GROUPS[tg][1]
                k = H * tg + h
                rs, y = crs[:, k % 2, 0:n], cy[:, k % 2, 0:n]
                if h == 0:
                    dve.wait_ge(c_at, 32 * (tg + 1))
                dve.wait_ge(c_std, k + 1)
                dve.reciprocal(rs, rs).then_inc(c_rs, 1)
                dve.wait_ge(c_rs, k + 1)
                dve.scalar_tensor_tensor(y, atr[:, h, 0:n], sublns[:], rs, ALU.mult, ALU.mult).then_inc(c_y1, 1)
                if h > 0:
                    mix_lo(tg, h - 1)
                dve.wait_ge(c_y1, k + 1)
                dve.tensor_tensor(y, y, gar[:, h, 0:n], ALU.mult).then_inc(c_y2, 1)

            def mix_lo(tg, h):
                n = GROUPS[tg][1]
                k = H * tg + h
                dve.wait_ge(c_hi, k + 1)
                dve.tensor_tensor(mix[:, tg % 2, 1, h, 0:n], cy[:, k % 2, 0:n], f32(mix[:, tg % 2, 0, h, 0:n]),
                                  ALU.subtract).then_inc(c_lo, 1)

            for h in range(H):
                norm(0, h)
            mix_lo(0, H - 1)
            for tg in range(NG):
                c0, n = GROUPS[tg]
                for o in range(DJ):
                    k = DJ * tg + o
                    dve.wait_ge(o_mm, k + 1)
                    if o == 0:
                        dve.wait_ge(c_x[tg % 2], 16 * (tg // 2 + 1))
                    wait(dve, o_st[o % 4], 16 * (2 * tg + o // 4))
                    for v, cols in ((0, slice(0, n)),) if tg < TG else ((0, slice(0, SPLIT)), (1, slice(SPLIT, n))):
                        ym = dve.scalar_tensor_tensor(yo[:, o % 4, cols], ps[:, k % 4, cols], mod[:, 16 + o, v:v + 1],
                                                      xr[:, tg % 2, o, cols], ALU.mult, ALU.add)
                    ym.then_inc(o_used, 1)
                    if tg + 1 < NG:
                        if o in NORM_AT:
                            norm(tg + 1, NORM_AT[o])
                        elif o == DJ - 1:
                            mix_lo(tg + 1, H - 1)


def _rope_tables():
    grid_w, freqs, base = 64, HD // 4, 10000.0
    t = np.arange(SAMPLE)
    inv = (np.float32(1.0) / (np.float32(base) ** (np.arange(freqs, dtype=np.float32) / np.float32(freqs))))
    inv = inv.astype(np.float32)
    ang = np.stack([(t // grid_w).astype(np.float32)[:, None] * inv, (t % grid_w).astype(np.float32)[:, None] * inv])
    cos, sin = np.cos(ang).astype(np.float32), np.sin(ang).astype(np.float32)
    table = np.zeros((P, 2, T), np.float32)
    table[:, 0, SAMPLE:] = 1.0
    for p in range(P):
        d = p % HD
        half, lower, i = d // 32, d % 32 < 16, d % 16
        table[p, 0, :SAMPLE] = cos[half, :, i]
        table[p, 1, :SAMPLE] = -sin[half, :, i] if lower else sin[half, :, i]
    return table.reshape(P, 2 * T)


def _constants():
    blk = np.zeros((P, P), np.float32)
    blk[:HD, :HD] = blk[HD:, HD:] = 1.0
    return np.stack([np.eye(P, dtype=np.float32), np.ones((P, P), np.float32), blk], axis=1)


def kernel(**inputs):
    import concourse.bacc as _bacc
    from concourse.bass_utils import run_bass_kernel_spmd as _run

    x = {k: np.asarray(v) for k, v in inputs.items()}

    def cols(v):
        return np.ascontiguousarray(v.reshape(-1, P).T)

    tokens = np.concatenate([x["x_sample"][0], x["x_prompt"][0]], axis=0)
    xT = tokens.T.reshape(DJ, P, T).transpose(1, 0, 2)
    w_in = x["w_in"][0].reshape(DJ, P, 32, P).transpose(2, 1, 0, 3)
    q0, k0, v0, ga0, cb0, cc0, ch0, gc0 = range(0, 32, 4)
    order = [v0 + i for i in range(4)]
    for i in range(H):
        order += [k0 + i, q0 + i]
    for i in range(H):
        order += [ga0 + i, gc0 + i, cb0 + i, cc0 + i, ch0 + i]
    small = np.concatenate([
        cols(x["norm_w"][0]), np.tile(x["q_norm_w"][0], 2)[:, None], np.tile(x["k_norm_w"][0], 2)[:, None],
        x["subln_w"][0][:, None],
        np.concatenate([np.concatenate([cols(x["conv_w"][0, i])[:, f:f + 1] for i in range(3)]
                                       + [cols(x["conv_b"][0])[:, f:f + 1]], axis=1) for f in range(4)], axis=1),
        cols(x["b_ada"][0]),
        np.stack([cols(x["c"][0]), cols(x["c_ctx"])], axis=2).reshape(P, 2 * DJ)], axis=1)
    arrays = {
        "xT": xT,
        "w_ada": x["w_ada"][0].reshape(DJ, P, 24, P).transpose(2, 1, 0, 3),
        "w_in": w_in[order],
        "w_out": x["w_out"][0].reshape(DJ, P, DJ, P).transpose(2, 1, 0, 3),
        "small": small,
        "lam": np.broadcast_to(np.stack([x["lambda_q1"][0], x["lambda_k1"][0], x["lambda_q2"][0], x["lambda_k2"][0]]),
                               (P, 4, HD)),
        "cache_k": x["cache_k"][0, 0].reshape(CACHE, H, P).transpose(1, 2, 0),
        "cache_v": x["cache_v"][0, 0].reshape(CACHE, H * P),
        "rope": _rope_tables(),
        "cst": _constants(),
    }
    nc = _bacc.Bacc("TRN2", target_bir_lowering=False, num_devices=1, dynamic_dma_scratch_size=1024)
    arrays = {f"in_{k}": np.ascontiguousarray(v) for k, v in arrays.items()}
    aps = {k[3:]: nc.dram_tensor(k, v.shape, mybir.dt.from_np(v.dtype), kind="ExternalInput").ap()
           for k, v in arrays.items()}
    for name, shape in (("y", [DJ, P, T]), ("new_k", [H, P, PROMPT]), ("new_v", [P, H * P])):
        aps[name] = nc.dram_tensor(f"out_{name}", shape, F32, kind="ExternalOutput").ap()
    hymba_layer(nc, aps)
    r = _run(nc, [arrays], core_ids=[0]).results[0]
    y = np.asarray(r["out_y"]).reshape(D, T).T
    new_k = np.asarray(r["out_new_k"]).transpose(2, 0, 1).reshape(1, 1, PROMPT, H, 2, HD)
    new_v = np.asarray(r["out_new_v"]).reshape(1, 1, PROMPT, H, P)
    return (np.ascontiguousarray(y[SAMPLE:])[None], np.ascontiguousarray(y[:SAMPLE])[None],
            np.ascontiguousarray(new_k), np.ascontiguousarray(new_v))
```
